# Optimizing a Trainium2 kernel written in Bass

```python
import jax, jax.numpy as jnp
from jax import lax
import numpy as np

D_MODEL = 1024
BATCH = 1
SEQ = 2048
DEPTH = 1

GRID_W = 64
GDN_HEADS = 4
GDN_DK = 128
GDN_DV = 128
CONV_W = 5
CHUNK = 64
ATT_HEADS = 8
ATT_KV_HEADS = 2
ATT_HEAD_DIM = 64
Q_BLOCK = 128
ROPE_THETA = 10000.0
D_MIX = GDN_HEADS * GDN_DV + ATT_HEADS * ATT_HEAD_DIM
N_GROUPS = 4
EXPERTS_PER_GROUP = 8
N_EXPERTS = N_GROUPS * EXPERTS_PER_GROUP
TOP_K = 2
EXPERT_FF = D_MODEL // 2
ROUTE_BLOCK = 128
EPS = 1e-6

GDN_QK = GDN_HEADS * GDN_DK
GDN_V = GDN_HEADS * GDN_DV
GDN_CONV_C = 2 * GDN_QK + GDN_V
ATT_Q = ATT_HEADS * ATT_HEAD_DIM
ATT_KV = ATT_KV_HEADS * ATT_HEAD_DIM
IN_SPLITS = (GDN_QK, GDN_QK, GDN_V, GDN_V, GDN_HEADS, GDN_HEADS, GDN_HEADS, GDN_HEADS, ATT_Q, ATT_KV, ATT_KV)
D_IN = 2 * GDN_QK + 2 * GDN_V + 4 * GDN_HEADS + ATT_Q + 2 * ATT_KV

kernel_name = 'hybrid_gdn_axial_gqa_hmoe_encoder'

def rms_norm(x, w):
    x32 = x.astype(jnp.float32)
    y = x32 * lax.rsqrt(jnp.mean(x32 * x32, axis=-1, keepdims=True) + EPS)
    return (y * w.astype(jnp.float32)).astype(x.dtype)

def l2_norm(x):
    return x * lax.rsqrt(jnp.sum(x * x, axis=-1, keepdims=True) + EPS)

def gated_delta_chunked(q, k, v, g, beta):
    B, S, H, DK = q.shape
    DV = v.shape[-1]
    N = S // CHUNK
    q = q * (DK ** -0.5)
    to_chunks = lambda t: t.reshape(B, N, CHUNK, H, t.shape[-1]).transpose(0, 3, 1, 2, 4)
    q, k, v = to_chunks(q), to_chunks(k), to_chunks(v)
    g = g.reshape(B, N, CHUNK, H).transpose(0, 3, 1, 2)
    beta = beta.reshape(B, N, CHUNK, H).transpose(0, 3, 1, 2)
    g_cum = jnp.cumsum(g, axis=-1)
    tril = jnp.tril(jnp.ones((CHUNK, CHUNK), dtype=bool))
    strict = jnp.tril(jnp.ones((CHUNK, CHUNK), dtype=bool), k=-1)
    diff = g_cum[..., :, None] - g_cum[..., None, :]
    decay = jnp.where(tril, jnp.exp(jnp.where(tril, diff, 0.0)), 0.0)
    k_beta = k * beta[..., None]
    v_beta = v * beta[..., None]
    lower = jnp.where(strict, jnp.einsum('bhncd,bhnsd->bhncs', k_beta, k) * decay, 0.0)
    eye = jnp.eye(CHUNK, dtype=jnp.float32)
    rhs = jnp.concatenate([v_beta, k_beta * jnp.exp(g_cum)[..., None]], axis=-1)
    sol = lax.linalg.triangular_solve(eye + lower, rhs, left_side=True, lower=True, unit_diagonal=True)
    u = sol[..., :DV]
    w = sol[..., DV:]
    attn_intra = jnp.where(tril, jnp.einsum('bhncd,bhnsd->bhncs', q, k) * decay, 0.0)
    q_decay = q * jnp.exp(g_cum)[..., None]
    k_tail = k * jnp.exp(g_cum[..., -1:] - g_cum)[..., None]
    chunk_decay = jnp.exp(g_cum[..., -1])

    def step(state, xs):
        u_i, w_i, qd_i, kt_i, a_i, d_i = xs
        v_new = u_i - jnp.einsum('bhcd,bhde->bhce', w_i, state)
        o_i = jnp.einsum('bhcd,bhde->bhce', qd_i, state) + jnp.einsum('bhcs,bhse->bhce', a_i, v_new)
        state = state * d_i[..., None, None] + jnp.einsum('bhcd,bhce->bhde', kt_i, v_new)
        return state, o_i

    xs = tuple(jnp.moveaxis(t, 2, 0) for t in (u, w, q_decay, k_tail, attn_intra, chunk_decay))
    state0 = jnp.zeros((B, H, DK, DV), jnp.float32)
    _, o = lax.scan(step, state0, xs)
    return o.transpose(1, 0, 3, 2, 4).reshape(B, S, H, DV)

def gdn_group(q, k, v, z, b_f, b_b, a_f, a_b, conv_w, a_log, dt_bias, norm_w):
    B, S, _ = q.shape
    dtype = q.dtype
    qkv = jnp.concatenate([q, k, v], axis=-1)
    qkv = lax.conv_general_dilated(
        qkv, conv_w.reshape(CONV_W, 1, GDN_CONV_C).astype(dtype), window_strides=(1,),
        padding=((CONV_W // 2, CONV_W // 2),), dimension_numbers=('NWC', 'WIO', 'NWC'),
        feature_group_count=GDN_CONV_C)
    qkv = jax.nn.silu(qkv).astype(jnp.float32)
    q = l2_norm(qkv[..., :GDN_QK].reshape(B, S, GDN_HEADS, GDN_DK))
    k = l2_norm(qkv[..., GDN_QK:2 * GDN_QK].reshape(B, S, GDN_HEADS, GDN_DK))
    v = qkv[..., 2 * GDN_QK:].reshape(B, S, GDN_HEADS, GDN_DV)
    a_log = a_log.astype(jnp.float32)
    dt_bias = dt_bias.astype(jnp.float32)
    beta_f = jax.nn.sigmoid(b_f.astype(jnp.float32))
    beta_b = jax.nn.sigmoid(b_b.astype(jnp.float32))
    g_f = -jnp.exp(a_log[0]) * jax.nn.softplus(a_f.astype(jnp.float32) + dt_bias[0])
    g_b = -jnp.exp(a_log[1]) * jax.nn.softplus(a_b.astype(jnp.float32) + dt_bias[1])
    flip = lambda t: jnp.flip(t, axis=1)
    o_fwd = gated_delta_chunked(q, k, v, g_f, beta_f)
    o_bwd = flip(gated_delta_chunked(flip(q), flip(k), flip(v), flip(g_b), flip(beta_b)))
    o = o_fwd + o_bwd
    o = o * lax.rsqrt(jnp.mean(o * o, axis=-1, keepdims=True) + EPS) * norm_w.astype(jnp.float32)
    o = o * jax.nn.silu(z.astype(jnp.float32).reshape(B, S, GDN_HEADS, GDN_DV))
    return o.reshape(B, S, GDN_HEADS * GDN_DV).astype(dtype)

def axial_rope_tables(seq_len):
    rows = seq_len // GRID_W
    row = jnp.repeat(jnp.arange(rows), GRID_W).astype(jnp.float32)
    col = jnp.tile(jnp.arange(GRID_W), rows).astype(jnp.float32)
    axis_dims = ATT_HEAD_DIM // 2
    inv_freq = ROPE_THETA ** (-jnp.arange(0, axis_dims, 2, dtype=jnp.float32) / axis_dims)
    ang = jnp.concatenate([row[:, None] * inv_freq, col[:, None] * inv_freq], axis=-1)
    return jnp.cos(ang), jnp.sin(ang)

def apply_rope(x, cos, sin):
    x32 = x.astype(jnp.float32).reshape(*x.shape[:-1], x.shape[-1] // 2, 2)
    x0, x1 = x32[..., 0], x32[..., 1]
    c, s = cos[None, :, None, :], sin[None, :, None, :]
    out = jnp.stack([x0 * c - x1 * s, x0 * s + x1 * c], axis=-1)
    return out.reshape(x.shape).astype(x.dtype)

def bidir_gqa_blocks(q, k, v):
    B, S, H, D = q.shape
    kvh = k.shape[2]
    grp = H // kvh
    nb = S // Q_BLOCK
    qb = jnp.moveaxis(q.reshape(B, nb, Q_BLOCK, kvh, grp, D), 1, 0)
    scale = D ** -0.5

    def one_block(q_blk):
        s = jnp.einsum('bqkgd,bskd->bkgqs', q_blk, k).astype(jnp.float32) * scale
        p = jax.nn.softmax(s, axis=-1).astype(v.dtype)
        return jnp.einsum('bkgqs,bskd->bqkgd', p, v)

    o = lax.map(one_block, qb)
    return jnp.moveaxis(o, 0, 1).reshape(B, S, H * D)

def hierarchical_moe(h, w_router_group, w_router_expert, w_gate, w_up, w_down):
    B, S, D = h.shape
    T = B * S
    xf = h.reshape(T, D)
    gp = jax.nn.softmax((xf @ w_router_group).astype(jnp.float32), axis=-1)
    gp_top, g_sel = lax.top_k(gp, 1)
    fine = (xf @ w_router_expert).astype(jnp.float32).reshape(T, N_GROUPS, EXPERTS_PER_GROUP)
    fine_sel = jnp.take_along_axis(fine, g_sel[:, :, None], axis=1)[:, 0]
    pf_top, e_loc = lax.top_k(jax.nn.softmax(fine_sel, axis=-1), TOP_K)
    gate = gp_top * pf_top / jnp.sum(pf_top, axis=-1, keepdims=True)
    expert = g_sel * EXPERTS_PER_GROUP + e_loc

    n_assign = T * TOP_K
    n_blocks = -(-(n_assign + N_EXPERTS * (ROUTE_BLOCK - 1)) // ROUTE_BLOCK)
    e_flat = expert.reshape(-1)
    tok_flat = jnp.repeat(jnp.arange(T), TOP_K)
    gate_flat = gate.reshape(-1)
    order = jnp.argsort(e_flat, stable=True)
    e_sorted, tok_sorted, gate_sorted = e_flat[order], tok_flat[order], gate_flat[order]
    counts = jnp.bincount(e_flat, length=N_EXPERTS)
    padded = (counts + ROUTE_BLOCK - 1) // ROUTE_BLOCK * ROUTE_BLOCK
    count_start = jnp.cumsum(counts) - counts
    pad_end = jnp.cumsum(padded)
    pad_start = pad_end - padded
    dest = pad_start[e_sorted] + (jnp.arange(n_assign) - count_start[e_sorted])
    x_buf = jnp.zeros((n_blocks * ROUTE_BLOCK, D), h.dtype).at[dest].set(xf[tok_sorted])
    block_start = jnp.arange(n_blocks) * ROUTE_BLOCK
    block_expert = jnp.minimum(jnp.searchsorted(pad_end, block_start, side='right'), N_EXPERTS - 1)

    def one_block(args):
        xb, e = args
        hid = jax.nn.silu(xb @ w_gate[e]) * (xb @ w_up[e])
        return hid @ w_down[e]

    y_buf = lax.map(one_block, (x_buf.reshape(n_blocks, ROUTE_BLOCK, D), block_expert)).reshape(-1, D)
    y = y_buf[dest] * gate_sorted[:, None].astype(h.dtype)
    out = jnp.zeros((T, D), h.dtype).at[tok_sorted].add(y)
    return out.reshape(B, S, D)

def setup_inputs(seed: int = 0) -> dict:
    key = jax.random.key(seed)
    ks = jax.random.split(key, 20)
    f32 = jnp.float32
    nrm = lambda k, shape, fan_in: jax.random.normal(k, shape, f32) * (fan_in ** -0.5)
    gain = lambda k, shape: 1.0 + 0.02 * jax.random.normal(k, shape, f32)
    dt = jnp.exp(jax.random.uniform(ks[5], (DEPTH, 2, GDN_HEADS), f32, np.log(1e-3), np.log(1e-1)))
    return {
        'x': jax.random.normal(ks[0], (BATCH, SEQ, D_MODEL), f32),
        'norm_mix_w': gain(ks[1], (DEPTH, D_MODEL)),
        'w_in': nrm(ks[2], (DEPTH, D_MODEL, D_IN), D_MODEL),
        'conv_w': nrm(ks[3], (DEPTH, CONV_W, GDN_CONV_C), CONV_W),
        'a_log': jnp.log(jax.random.uniform(ks[4], (DEPTH, 2, GDN_HEADS), f32, 1.0, 16.0)),
        'dt_bias': dt + jnp.log(-jnp.expm1(-dt)),
        'gdn_norm_w': gain(ks[6], (DEPTH, GDN_DV)),
        'q_norm_w': gain(ks[7], (DEPTH, ATT_HEAD_DIM)),
        'k_norm_w': gain(ks[8], (DEPTH, ATT_HEAD_DIM)),
        'w_out': nrm(ks[9], (DEPTH, D_MIX, D_MODEL), D_MIX),
        'norm_ffn_w': gain(ks[10], (DEPTH, D_MODEL)),
        'w_router_group': nrm(ks[11], (DEPTH, D_MODEL, N_GROUPS), D_MODEL),
        'w_router_expert': nrm(ks[12], (DEPTH, D_MODEL, N_EXPERTS), D_MODEL),
        'w_gate': nrm(ks[13], (DEPTH, N_EXPERTS, D_MODEL, EXPERT_FF), D_MODEL),
        'w_up': nrm(ks[14], (DEPTH, N_EXPERTS, D_MODEL, EXPERT_FF), D_MODEL),
        'w_down': nrm(ks[15], (DEPTH, N_EXPERTS, EXPERT_FF, D_MODEL), EXPERT_FF),
        'final_norm_w': gain(ks[16], (D_MODEL,)),
    }

def reference(x, norm_mix_w, w_in, conv_w, a_log, dt_bias, gdn_norm_w, q_norm_w, k_norm_w, w_out,
              norm_ffn_w, w_router_group, w_router_expert, w_gate, w_up, w_down, final_norm_w):
    B, S, _ = x.shape
    cos, sin = axial_rope_tables(S)
    split_idx = np.cumsum(IN_SPLITS)[:-1].tolist()
    for l in range(DEPTH):
        h = rms_norm(x, norm_mix_w[l])
        proj = h @ w_in[l]
        (q_a, k_a, v_a, z_a, b_f, b_b, a_f, a_b, q_b, k_b, v_b) = jnp.split(proj, split_idx, axis=-1)
        o_a = gdn_group(q_a, k_a, v_a, z_a, b_f, b_b, a_f, a_b, conv_w[l], a_log[l], dt_bias[l], gdn_norm_w[l])
        q_b = apply_rope(rms_norm(q_b.reshape(B, S, ATT_HEADS, ATT_HEAD_DIM), q_norm_w[l]), cos, sin)
        k_b = apply_rope(rms_norm(k_b.reshape(B, S, ATT_KV_HEADS, ATT_HEAD_DIM), k_norm_w[l]), cos, sin)
        v_b = v_b.reshape(B, S, ATT_KV_HEADS, ATT_HEAD_DIM)
        o_b = bidir_gqa_blocks(q_b, k_b, v_b)
        x = x + jnp.concatenate([o_a, o_b], axis=-1) @ w_out[l]
        x = x + hierarchical_moe(rms_norm(x, norm_ffn_w[l]), w_router_group[l], w_router_expert[l],
                                 w_gate[l], w_up[l], w_down[l])
    return rms_norm(x, final_norm_w)


_drawn_inputs = setup_inputs


def setup_inputs(seed=0):
    import zlib

    import numpy as np

    out = dict(_drawn_inputs(seed))
    spreads = {}
    factors = {'gdn_norm_w': 7.952,
     'q_norm_w': 8.0,
     'k_norm_w': 8.0,
     'final_norm_w': 8.158,
     'norm_ffn_w': 3.356}
    for name, (base, spread) in spreads.items():
        noise = np.random.default_rng([zlib.crc32(name.encode()), seed]).standard_normal(out[name].shape)
        drawn = base * np.exp(spread * noise) if base else spread * noise
        out[name] = __import__('jax').numpy.asarray(drawn.astype(out[name].dtype))
    for name, factor in factors.items():
        out[name] = (out[name] * factor).astype(out[name].dtype)
    return out
```

```python
import numpy as np
from contextlib import ExitStack
import concourse.bass as bass
from concourse import mybir
from concourse.alu_op_type import AluOpType as ALU

F32 = mybir.dt.float32
F32R = mybir.dt.float32r
I32 = mybir.dt.int32
ACT = mybir.ActivationFunctionType
AX = mybir.AxisListType

P = 128
SEQ, D_MODEL = 2048, 1024
TILES = SEQ // P
KD = D_MODEL // P
GDN_HEADS, GDN_D = 4, 128
CONV_W = 5
CONV_BLOCKS = 3 * GDN_HEADS
ATT_HEADS, KV_HEADS, ATT_D = 8, 2, 64
GROUP = ATT_HEADS // KV_HEADS
GRID_W = 64
N_GROUPS, PER_GROUP, TOP_K = 4, 8, 2
N_EXPERTS = N_GROUPS * PER_GROUP
FF = 512
KF = FF // P
EPS = 1e-6
GDN_W = GDN_HEADS * GDN_D
C_Z = 3 * GDN_W
C_GATES = C_Z + GDN_W
C_ATT = C_GATES + 4 * GDN_HEADS
ATT_QK = (ATT_HEADS + KV_HEADS) * ATT_D
ATT_KV = KV_HEADS * ATT_D
D_IN = C_ATT + ATT_QK + ATT_KV
N_BLOCKS = -(-(SEQ * TOP_K + N_EXPERTS * (P - 1)) // P)
SLOTS = N_BLOCKS * P


class Stage:

    def __init__(self, nc):
        self.nc, self.sems = nc, []

    def semaphore(self, name):
        self.sems.append(self.nc.alloc_semaphore(name=name))
        return self.sems[-1]

    def __enter__(self):
        return self

    def __exit__(self, *_):
        self.nc.clear_and_free_semaphores(self.sems)
        self.nc.all_engine_barrier()


class Event:

    def __init__(self, stage, name, per=1):
        self.sems = [stage.semaphore(f"{name}_{x}") for x in ("even", "odd")]
        self.per = per

    def __getitem__(self, j):
        return self.sems[j]

    def now(self, i, j, n=None):
        return self.sems[j], i * self.per + (self.per if n is None else n)

    def last(self, i, j):
        return self.sems[1 - j], (i + j) * self.per

    def before_last(self, i, j):
        return self.sems[j], i * self.per


class Count:

    def __init__(self, stage, name, per=1):
        self.sem, self.per = stage.semaphore(name), per

    def now(self, t, n=None):
        return self.sem, t * self.per + (self.per if n is None else n)

    def last(self, t):
        return self.sem, t * self.per


class Chain:

    def __init__(self, eng, sem, per_round=0):
        self.eng, self.sem, self.per, self.base, self.n, self.start = eng, sem, per_round, 0, 0, 0

    def round(self, i):
        self.base, self.n = i * self.per + self.start, 0

    def mark(self, ins):
        ins.then_inc(self.sem, 1)
        self.n += 1

    def wait(self):
        self.eng.wait_ge(self.sem, self.base + self.n)

    def link(self, ins):
        self.mark(ins)
        self.wait()

    def close(self):
        assert self.n == self.per, f"a round has {self.n} links"


def following(i, j):
    return (i, 1) if j == 0 else (i + 1, 0)


def rounds(eng, own, tile, n=TILES):
    def pair(i, end):
        if own:
            own.round(i)
        for j in range(2):
            tile(i, j, end and j == 1)

    if own:
        own.start = own.n
    with eng.Fori(0, n // 2 - 1) as i:
        pair(i, False)
        if own:
            own.close()
    pair(n // 2 - 1, True)


def tile_rows(dram, t, n=1):
    return dram.rearrange("(t p) w -> t p w", p=P)[bass.ds(t, 1), :, :].rearrange("a p w -> (a p) w")


def at(tensor, t):
    return tensor[:, bass.ds(t, 1), :].rearrange("p a w -> p (a w)")


def project_tokens(nc, top, dr, keep):
    NT = GDN_W + ATT_QK + ATT_KV + 16
    Z0, Q0, K0 = 0, GDN_W, 2 * GDN_W
    NK = NT - K0
    NH = ATT_HEADS + KV_HEADS
    half = ATT_D // 2
    with ExitStack() as ctx:
        sb = lambda n, s, d=F32: ctx.enter_context(nc.sbuf_tensor(n, s, d))
        ps = lambda n, s, d=F32: ctx.enter_context(nc.psum_tensor(n, s, d))
        sem = lambda n: top.semaphore(n)
        ev = lambda n, per=1: Event(top, n, per)
        w_tok = sb("w_tok", [P, KD, NT])
        ident = sb("ident_a", [P, P])
        nw = sb("norm_mix_cols", [P, KD])
        qkw = sb("qk_norm_rows", [P, NH, ATT_D])
        cos = sb("rope_cos", [P, TILES, half])
        sin = sb("rope_sin", [P, TILES, half])
        x_in = sb("x_in", [P, 2, D_MODEL])
        squares = sb("squares_a", [P, D_MODEL])
        stat = sb("stat_a", [P, 2, 4])
        eps = sb("eps_a", [P, 1])
        xn = sb("xn", [P, 2, D_MODEL])
        xT = sb("xT_tile", [P, 2, KD, P])
        zs = sb("z_silu", [P, 2, GDN_W])
        qk = sb("qk_raw", [P, 2, ATT_QK + ATT_KV])
        qsq = sb("qk_squares", [P, NH, ATT_D])
        qs = sb("qk_stats", [P, 2, 3, NH])
        qn = sb("qk_normed", [P, NH, ATT_D])
        rot = sb("rope_products", [P, 4, NH, half])
        qr = sb("qk_roped", [P, 2, ATT_QK])
        tp = ps("transposed", [P, KD, P])
        pz = ps("proj_z", [P, GDN_W])
        pq = ps("proj_q", [P, GDN_W])
        pk = ps("proj_kv", [P, NK])
        weights_in, consts_in = sem("a_weights_in"), sem("a_consts_in")
        eps_set = sem("a_eps_set")
        x_loaded, row_sum, row_rms, normed = ev("x_loaded", 16), ev("row_sum"), ev("row_rms"), ev("x_normed")
        transposed, xT_ready, copied = ev("x_transposed"), ev("xT_ready"), ev("xT_copied")
        projected, taken, z_ready = ev("projected", 3), ev("proj_taken"), ev("z_ready")
        qk_sums, qk_rms, roped = ev("qk_sums"), ev("qk_rms"), ev("qk_roped")
        stored_z, stored_qk, stored_v = ev("z_stored", 16), ev("qk_stored", 16), ev("v_stored", 16)
        dve_chain = sem("a_dve")
        xT_all, gates = keep["xT_all"], keep["gates"]

        with nc.Block() as block:
            @block.sync
            def _(sp):
                w = dr["w_in"].rearrange("(k p) n -> p k n", p=P)
                sp.dma_start(ident[:, :], dr["c_ident"]).then_inc(consts_in, 16)
                sp.dma_start(nw[:, :], dr["norm_mix_w"].rearrange("(k p) -> p k", p=P),
                             allow_slow_non_contiguous=True).then_inc(consts_in, 16)
                for h in range(NH):
                    src = dr["q_norm_w"] if h < ATT_HEADS else dr["k_norm_w"]
                    sp.dma_start(qkw[:, h, :], src.unsqueeze(0).broadcast_to([P, ATT_D])).then_inc(consts_in, 16)
                sp.dma_start(cos[:, :, :], dr["c_cos"].rearrange("(t p) f -> p t f", p=P)).then_inc(consts_in, 16)
                sp.dma_start(sin[:, :, :], dr["c_sin"].rearrange("(t p) f -> p t f", p=P)).then_inc(consts_in, 16)
                sp.dma_start(w_tok[:, :, 0:GDN_W], w[:, :, C_Z:C_GATES]).then_inc(weights_in, 16)
                sp.dma_start(w_tok[:, :, GDN_W:NT - 16], w[:, :, C_ATT:D_IN]).then_inc(weights_in, 16)
                sp.dma_start(w_tok[:, :, NT - 16:NT], w[:, :, C_GATES:C_ATT],
                             allow_slow_non_contiguous=True).then_inc(weights_in, 16)
                with sp.Fori(0, TILES // 2) as i:
                    for j in range(2):
                        sp.wait_ge(*row_sum.before_last(i, j))
                        sp.wait_ge(*normed.before_last(i, j))
                        sp.dma_start(x_in[:, j, :], tile_rows(dr["x"], i * 2 + j)).then_inc(x_loaded[j], 16)

            @block.gpsimd
            def _(pool):
                with pool.Fori(0, TILES // 2) as i:
                    for j in range(2):
                        t = i * 2 + j
                        pool.wait_ge(*z_ready.now(i, j))
                        pool.dma_start(tile_rows(dr["z"], t), zs[:, j, :]).then_inc(stored_z[j], 16)
                        pool.wait_ge(*roped.now(i, j))
                        pool.dma_start(tile_rows(dr["qk"], t), qr[:, j, :]).then_inc(stored_qk[j], 16)
                        pool.dma_start(tile_rows(dr["v"], t), qk[:, j, ATT_QK:]).then_inc(stored_v[j], 16)
                for j in range(2):
                    for s in (stored_z, stored_qk, stored_v):
                        pool.wait_ge(s[j], 16 * (TILES // 2))

            @block.scalar
            def _(act):
                act.wait_ge(eps_set, 1)

                def row_stats(i, j):
                    act.wait_ge(*x_loaded.now(i, j))
                    act.wait_ge(*normed.before_last(i, j))
                    act.activation(squares[:, :], x_in[:, j, :], ACT.Square, accum_out=stat[:, j, 0:1]).then_inc(row_sum[j], 1)
                    act.wait_ge(*row_sum.now(i, j))
                    act.activation(stat[:, j, 1:2], stat[:, j, 0:1], ACT.Sqrt, bias=eps[:, 0:1], scale=1.0 / D_MODEL).then_inc(row_rms[j], 1)

                def copy_xT(i, j):
                    act.wait_ge(*xT_ready.now(i, j))
                    act.activation(xT_all[:, :, bass.ds((i * 2 + j) * P, P)], xT[:, j, :, :], ACT.Copy).then_inc(copied[j], 1)

                def tile(i, j, last=False):
                    t = i * 2 + j
                    if not last:
                        row_stats(*following(i, j))
                    act.wait_ge(*projected.now(i, j, 1))
                    act.wait_ge(*stored_z.before_last(i, j))
                    act.activation(zs[:, j, :], pz[:, :], ACT.Silu).then_inc(z_ready[j], 1)
                    if not last:
                        copy_xT(*following(i, j))
                    act.wait_ge(*projected.now(i, j, 3))
                    act.wait_ge(*stored_v.before_last(i, j))
                    act.wait_ge(*roped.before_last(i, j))
                    act.activation(qk[:, j, 0:GDN_W], pq[:, :], ACT.Copy)
                    act.activation(qk[:, j, GDN_W:], pk[:, 0:NK - 16], ACT.Copy)
                    act.activation(at(gates, t), pk[:, NK - 16:NK], ACT.Copy).then_inc(taken[j], 1)
                    act.wait_ge(*qk_sums.now(i, j))
                    act.activation(qs[:, j, 1, :], qs[:, j, 0, :], ACT.Sqrt, bias=eps[:, 0:1], scale=1.0 / ATT_D).then_inc(qk_rms[j], 1)

                row_stats(0, 0)
                copy_xT(0, 0)
                rounds(act, None, tile)

            @block.vector
            def _(dve):
                own = Chain(dve, dve_chain, 2 * 10)
                dve.memset(eps[:, :], EPS).then_inc(eps_set, 1)
                dve.wait_ge(consts_in, 16 * (4 + NH))

                def normalize(i, j):
                    dve.wait_ge(*row_rms.now(i, j))
                    own.link(dve.reciprocal(stat[:, j, 2:3], stat[:, j, 1:2]))
                    dve.wait_ge(*transposed.before_last(i, j))
                    dve.tensor_scalar(xn[:, j, :], x_in[:, j, :], stat[:, j, 2:3], None, ALU.mult).then_inc(normed[j], 1)
                    dve.wait_ge(*transposed.now(i, j))
                    dve.wait_ge(*projected.before_last(i, j))
                    dve.wait_ge(*copied.before_last(i, j))
                    dve.tensor_tensor(xT[:, j, :, :], tp[:, :, :], nw[:, :].unsqueeze(2).broadcast_to([P, KD, P]),
                                      ALU.mult).then_inc(xT_ready[j], 1)

                def tile(i, j, last=False):
                    t = i * 2 + j
                    if not last:
                        normalize(*following(i, j))
                    dve.wait_ge(*taken.now(i, j))
                    raw = qk[:, j, 0:ATT_QK].rearrange("p (h d) -> p h d", d=ATT_D)
                    own.link(dve.tensor_tensor(qsq[:, :, :], raw, raw, ALU.mult))
                    dve.tensor_reduce(qs[:, j, 0, :], qsq[:, :, :], AX.X, ALU.add).then_inc(qk_sums[j], 1)
                    dve.wait_ge(*qk_rms.now(i, j))
                    own.link(dve.reciprocal(qs[:, j, 2, :], qs[:, j, 1, :]))
                    own.link(dve.tensor_tensor(qn[:, :, :], raw, qs[:, j, 2, :].unsqueeze(2).broadcast_to([P, NH, ATT_D]), ALU.mult))
                    own.link(dve.tensor_tensor(qn[:, :, :], qn[:, :, :], qkw[:, :, :], ALU.mult))
                    pair = qn[:, :, :].rearrange("p h (f two) -> p h f two", two=2)
                    c = at(cos, t).unsqueeze(1).broadcast_to([P, NH, half])
                    s = at(sin, t).unsqueeze(1).broadcast_to([P, NH, half])
                    own.mark(dve.tensor_tensor(rot[:, 0], pair[:, :, :, 0], c, ALU.mult))
                    own.mark(dve.tensor_tensor(rot[:, 1], pair[:, :, :, 1], s, ALU.mult))
                    own.mark(dve.tensor_tensor(rot[:, 2], pair[:, :, :, 0], s, ALU.mult))
                    own.link(dve.tensor_tensor(rot[:, 3], pair[:, :, :, 1], c, ALU.mult))
                    out = qr[:, j, :].rearrange("p (h f two) -> p h f two", h=NH, two=2)
                    dve.wait_ge(*stored_qk.before_last(i, j))
                    own.mark(dve.tensor_tensor(out[:, :, :, 0], rot[:, 0], rot[:, 1], ALU.subtract))
                    dve.tensor_tensor(out[:, :, :, 1], rot[:, 2], rot[:, 3], ALU.add).then_inc(roped[j], 1)

                normalize(0, 0)
                rounds(dve, own, tile)

            @block.tensor
            def _(pe):
                pe.wait_ge(consts_in, 16 * (4 + NH))

                def transposes(i, j):
                    pe.wait_ge(*normed.now(i, j))
                    pe.wait_ge(*xT_ready.last(i, j))
                    for k in range(KD):
                        ins = pe.transpose(tp[:, k, :], xn[:, j, k * P:(k + 1) * P], ident[:, :])
                    ins.then_inc(transposed[j], 1)

                def tile(i, j, last=False):
                    pe.wait_ge(*xT_ready.now(i, j))
                    for out, c0, c1 in ((pz, Z0, Q0), (pq, Q0, K0), (pk, K0, NT)):
                        if out is pk and not last:
                            transposes(*following(i, j))
                        pe.wait_ge(*(z_ready if out is pz else taken).last(i, j))
                        for k in range(KD):
                            ins = pe.matmul(out[:, :], xT[:, j, k, :], w_tok[:, k, c0:c1], start=k == 0, stop=k == KD - 1)
                        ins.then_inc(projected[j], 1)

                transposes(0, 0)
                pe.wait_ge(weights_in, 48)
                rounds(pe, None, tile)


def project_features(nc, top, dr, keep):
    N = CONV_BLOCKS
    C = SEQ // 512
    PAD = CONV_W // 2
    with ExitStack() as ctx:
        sb = lambda n, s, d=F32: ctx.enter_context(nc.sbuf_tensor(n, s, d))
        ps = lambda n, s, d=F32: ctx.enter_context(nc.psum_tensor(n, s, d))
        sem = lambda n: top.semaphore(n)
        ev = lambda n, per=1: Event(top, n, per)
        w_blk = sb("w_blk", [P, 2, KD, P])
        ident = sb("ident_b", [P, P])
        ones = sb("ones_b", [P, P])
        norm = sb("norm_scale_bias", [P, 2, N, 1])
        cw_rows = sb("conv_w_rows", [CONV_W, N * P])
        cw = sb("conv_w_cols", [P, N, CONV_W])
        raw = sb("conv_in", [P, 2, SEQ + 2 * PAD])
        acc = sb("conv_acc", [P, SEQ])
        act_out = sb("silu_out", [P, SEQ])
        sq = sb("squares_b", [P, SEQ])
        inv = sb("norms_b", [P, 3, TILES])
        feat = sb("features", [P, 2, SEQ])
        tok = sb("features_by_token", [P, 2, TILES, P])
        pp = ps("proj_b", [P, C, 512])
        pn = ps("norm_sums", [P, TILES])
        pt = ps("to_tokens", [P, 2, 4, P])
        pb = ps("to_channels", [P, 4, P])
        consts_in, cw_done, cw_ready, pads = sem("b_consts"), sem("b_conv_w_T"), sem("b_conv_w_ready"), sem("b_pads")
        w_loaded = ev("w_blk_loaded", 16)
        projected, raw_ready, conv_done = ev("b_projected", C), ev("b_raw", C), ev("b_conv")
        silu_done, squared, summed = ev("b_silu"), ev("b_squared"), ev("b_summed")
        norm2_ready, rms_ready = ev("b_norm2"), ev("b_rms")
        turned, tok_ready, returned, feat_ready = ev("b_turned", C), ev("b_tok", C), ev("b_returned", C), ev("b_feat", C)
        stored_f, stored_t = ev("b_feat_stored", 16), ev("b_tok_stored", 16)
        dve_chain = sem("b_dve")

        with nc.Block() as block:
            @block.sync
            def _(sp):
                sp.dma_start(ident[:, :], dr["c_ident"]).then_inc(consts_in, 16)
                sp.dma_start(ones[:, :], dr["c_ones"]).then_inc(consts_in, 16)
                sp.dma_start(cw_rows[:, :], dr["conv_w"]).then_inc(consts_in, 16)
                sp.dma_start(norm[:, :, :, :], dr["c_norm"].rearrange("p (a n) -> p a n", a=2).unsqueeze(3)).then_inc(consts_in, 16)

                def load(i, j):
                    w = dr["w_in"].rearrange("(k p) n -> p k n", p=P)
                    sp.wait_ge(*projected.before_last(i, j))
                    sp.dma_start(w_blk[:, j, :, :], w[:, :, bass.ds((i * 2 + j) * P, P)]).then_inc(w_loaded[j], 16)

                def tile(i, j, last=False):
                    m = i * 2 + j
                    if not last:
                        load(*following(i, j))
                    sp.wait_ge(*tok_ready.now(i, j))
                    sp.dma_start(dr["tok"].rearrange("(t p) c -> p t c", p=P)[:, :, bass.ds(m * P, P)], tok[:, j, :, :]).then_inc(stored_t[j], 16)
                    sp.wait_ge(*feat_ready.now(i, j))
                    sp.dma_start(dr["feat"][bass.ds(m, 1), :, :].rearrange("a p s -> (a p) s"), feat[:, j, :]).then_inc(stored_f[j], 16)

                load(0, 0)
                rounds(sp, None, tile, N)
                for j in range(2):
                    sp.wait_ge(stored_f[j], 16 * (N // 2))
                    sp.wait_ge(stored_t[j], 16 * (N // 2))

            @block.tensor
            def _(pe):
                pe.wait_ge(consts_in, 64)
                for m in range(N):
                    ins = pe.transpose(pt[:, 0, 0, m * CONV_W:(m + 1) * CONV_W], cw_rows[:, m * P:(m + 1) * P], ident[0:CONV_W, 0:CONV_W])
                ins.then_inc(cw_done, 1)
                pe.wait_ge(cw_ready, 1)

                def project(i, j, c, ks=range(KD)):
                    if c == 0:
                        pe.wait_ge(*w_loaded.now(i, j))
                    if ks[0] == 0:
                        pe.wait_ge(*raw_ready.last(i, j))
                    for k in ks:
                        ins = pe.matmul(pp[:, c, :], w_blk[:, j, k, :], keep["xT_all"][:, k, c * 512:(c + 1) * 512], start=k == 0, stop=k == KD - 1)
                    if ks[-1] == KD - 1:
                        ins.then_inc(projected[j], 1)

                def sums(i, j):
                    pe.wait_ge(*squared.now(i, j))
                    pe.wait_ge(*norm2_ready.last(i, j))
                    for t in range(TILES):
                        ins = pe.matmul(pn[:, t:t + 1], sq[:, t * P:(t + 1) * P], ones[:, 0:1], start=True, stop=True)
                    ins.then_inc(summed[j], 1)

                def turn(i, j, c):
                    pe.wait_ge(*(tok_ready.now(i, j, c - 1) if c >= 2 else tok_ready.last(i, j)))
                    for q in range(4):
                        ins = pe.transpose(pt[:, c % 2, q, :], act_out[:, (4 * c + q) * P:(4 * c + q + 1) * P], ident[:, :])
                    ins.then_inc(turned[j], 1)

                def turn_back(i, j, c):
                    pe.wait_ge(*tok_ready.now(i, j, c + 1))
                    pe.wait_ge(*(feat_ready.now(i, j, c) if c else feat_ready.last(i, j)))
                    for q in range(4):
                        ins = pe.transpose(pb[:, q, :], tok[:, j, 4 * c + q, :], ident[:, :])
                    ins.then_inc(returned[j], 1)

                def tile(i, j, last=False):
                    nxt = following(i, j)
                    if not last:
                        project(*nxt, 0)
                        project(*nxt, 1)
                        project(*nxt, 2, range(KD // 2))
                    sums(i, j)
                    turn(i, j, 0)
                    turn(i, j, 1)
                    if not last:
                        project(*nxt, 2, range(KD // 2, KD))
                    turn(i, j, 2)
                    turn(i, j, 3)
                    turn_back(i, j, 0)
                    if not last:
                        project(*nxt, 3, range(KD // 2))
                    turn_back(i, j, 1)
                    if not last:
                        project(*nxt, 3, range(KD // 2, KD))
                    turn_back(i, j, 2)
                    turn_back(i, j, 3)

                for c in range(C):
                    project(0, 0, c)
                rounds(pe, None, tile, N)

            @block.scalar
            def _(act):
                act.wait_ge(pads, 1)

                def copy_raw(i, j, c):
                    act.wait_ge(*projected.now(i, j, c + 1))
                    act.wait_ge(*conv_done.before_last(i, j))
                    act.activation(raw[:, j, PAD + c * 512:PAD + (c + 1) * 512], pp[:, c, :], ACT.Copy).then_inc(raw_ready[j], 1)

                def tile(i, j, last=False):
                    m = i * 2 + j
                    if not last:
                        copy_raw(*following(i, j), 0)
                        copy_raw(*following(i, j), 1)
                    act.wait_ge(*conv_done.now(i, j))
                    act.wait_ge(*turned.last(i, j))
                    act.activation(act_out[:, :], acc[:, :], ACT.Silu).then_inc(silu_done[j], 1)
                    act.wait_ge(*silu_done.now(i, j))
                    act.wait_ge(*summed.last(i, j))
                    act.activation(sq[:, :], act_out[:, :], ACT.Square).then_inc(squared[j], 1)
                    act.wait_ge(*norm2_ready.now(i, j))
                    act.activation(inv[:, 1, :], inv[:, 0, :], ACT.Sqrt).then_inc(rms_ready[j], 1)
                    if not last:
                        copy_raw(*following(i, j), 2)

                    def copy_feat(c):
                        act.wait_ge(*returned.now(i, j, c + 1))
                        act.wait_ge(*stored_f.before_last(i, j))
                        act.activation(feat[:, j, c * 512:(c + 1) * 512], pb[:, :, :].rearrange("p q c -> p (q c)"), ACT.Copy).then_inc(feat_ready[j], 1)

                    copy_feat(0)
                    copy_feat(1)
                    if not last:
                        copy_raw(*following(i, j), 3)
                    copy_feat(2)
                    copy_feat(3)

                for c in range(C):
                    copy_raw(0, 0, c)
                rounds(act, None, tile, N)

            @block.vector
            def _(dve):
                own = Chain(dve, dve_chain, 2 * CONV_W)
                dve.memset(raw[:, :, 0:PAD], 0.0)
                dve.memset(raw[:, :, SEQ + PAD:], 0.0).then_inc(pads, 1)
                dve.wait_ge(cw_done, 1)
                dve.tensor_copy(cw[:, :, :], pt[:, 0, 0, 0:N * CONV_W].rearrange("p (m w) -> p m w", w=CONV_W)).then_inc(cw_ready, 1)
                dve.wait_ge(cw_ready, 1)
                dve.wait_ge(consts_in, 64)

                def convolve(i, j):
                    m = i * 2 + j
                    dve.wait_ge(*raw_ready.now(i, j))
                    dve.wait_ge(*silu_done.last(i, j))
                    for w in range(CONV_W):
                        c = cw[:, bass.ds(m, 1), w:w + 1].rearrange("p a b -> p (a b)")
                        x = raw[:, j, w:w + SEQ]
                        if w == 0:
                            own.link(dve.tensor_scalar(acc[:, :], x, c, None, ALU.mult))
                        elif w < CONV_W - 1:
                            own.link(dve.scalar_tensor_tensor(out=acc[:, :], in0=x, scalar=c, in1=acc[:, :], op0=ALU.mult, op1=ALU.add))
                        else:
                            dve.scalar_tensor_tensor(out=acc[:, :], in0=x, scalar=c, in1=acc[:, :], op0=ALU.mult, op1=ALU.add).then_inc(conv_done[j], 1)

                def tile(i, j, last=False):
                    m = i * 2 + j
                    dve.wait_ge(*summed.now(i, j))
                    dve.tensor_scalar(inv[:, 0, :], pn[:, :], norm[:, 0, bass.ds(m, 1), :].rearrange("p a b -> p (a b)"),
                                      norm[:, 1, bass.ds(m, 1), :].rearrange("p a b -> p (a b)"), ALU.mult, ALU.add).then_inc(norm2_ready[j], 1)
                    dve.wait_ge(*rms_ready.now(i, j))
                    own.link(dve.reciprocal(inv[:, 2, :], inv[:, 1, :]))
                    dve.wait_ge(*stored_t.before_last(i, j))
                    dve.wait_ge(*returned.before_last(i, j))
                    for c in range(C):
                        dve.wait_ge(*turned.now(i, j, c + 1))
                        dve.tensor_tensor(tok[:, j, 4 * c:4 * c + 4, :], pt[:, c % 2, :, :],
                                          inv[:, 2, 4 * c:4 * c + 4].unsqueeze(2).broadcast_to([P, 4, P]), ALU.mult).then_inc(tok_ready[j], 1)
                    if not last:
                        convolve(*following(i, j))

                convolve(0, 0)
                rounds(dve, own, tile, N)


def gated_delta(nc, top, dr, gates):
    H, W = GDN_HEADS, GDN_W
    LEVELS = 7
    CUM, BETA, GROW, TAIL, END, LOG = range(6)
    with ExitStack() as ctx:
        sb = lambda n, s, d=F32: ctx.enter_context(nc.sbuf_tensor(n, s, d))
        ps = lambda n, s, d=F32: ctx.enter_context(nc.psum_tensor(n, s, d))
        sem = lambda n: top.semaphore(n)
        both = lambda make: [make(d) for d in ("fwd", "bwd")]
        ct = lambda n, per=1: both(lambda d: Count(top, f"c_{n}_{d}", per))
        ident, ones = sb("ident_c", [P, P]), sb("ones_c", [P, P])
        upto = sb("upto", [P, 2, P])
        level = sb("level_masks", [P, 2, LEVELS, P])
        dt_rows, a_rows = sb("dt_rows", [P, 8]), sb("a_log_rows", [P, 8])
        pre = sb("gate_work", [P, 4, TILES, 8])
        logs = sb("log_decays", [P, 2, TILES, H])
        cums = sb("cum_decays", [P, 2, 2, TILES, H])
        tab = sb("gate_table", [P, TILES, 2, 6 * H])
        banks = [[ps(f"bank_{d}{n}", [P, H, P]) for n in "abcd"] for d in ("f", "b")]
        consts_in, prep = sem("c_consts"), sem("c_prep")
        prep_act, prep_pe = sem("c_prep_act"), sem("c_prep_pe")

        def turned(eng, i, j):
            return i * (-2) + (TILES - 1 - j)

        with nc.Block() as block:
            @block.sync
            def _(sp):
                sp.dma_start(ident[:, :], dr["c_ident"]).then_inc(consts_in, 16)
                sp.dma_start(ones[:, :], dr["c_ones"]).then_inc(consts_in, 16)
                sp.dma_start(upto[:, :, :], dr["c_upto"]).then_inc(consts_in, 16)
                sp.dma_start(level[:, :, :, :], dr["c_level"]).then_inc(consts_in, 16)
                sp.dma_start(dt_rows[:, :], dr["dt_bias"].broadcast_to([P, 8])).then_inc(consts_in, 16)
                sp.dma_start(a_rows[:, :], dr["a_log"].broadcast_to([P, 8])).then_inc(consts_in, 16)

            @block.vector
            def _(dve):
                own = Chain(dve, prep)
                dve.wait_ge(consts_in, 96)
                rows = lambda x: x[:, :].unsqueeze(1).broadcast_to([P, TILES, 8])
                own.link(dve.tensor_tensor(pre[:, 0], gates[:, :, 8:16], rows(dt_rows), ALU.add))
                dve.wait_ge(prep_act, 4)
                own.link(dve.scalar_tensor_tensor(out=pre[:, 2], in0=pre[:, 0], scalar=0.0, in1=pre[:, 1], op0=ALU.max, op1=ALU.add))
                own.link(dve.tensor_scalar(a_rows[:, :], a_rows[:, :], -1.0, None, ALU.mult))
                for d in range(2):
                    own.link(dve.tensor_tensor(logs[:, d], pre[:, 2, :, 4 * d:4 * d + 4],
                                               a_rows[:, 4 * d:4 * d + 4].unsqueeze(1).broadcast_to([P, TILES, H]), ALU.mult))
                dve.wait_ge(prep_pe, 1)
                for d in range(2):
                    g = banks[d][0][:, 0, 0:TILES * H].rearrange("p (t h) -> p t h", h=H)
                    end = banks[d][1][:, 0, 0:TILES * H].rearrange("p (t h) -> p t h", h=H)
                    col = lambda n: tab[:, :, d, n * H:(n + 1) * H]
                    own.mark(dve.tensor_copy(col(CUM), g))
                    own.mark(dve.tensor_copy(col(LOG), logs[:, d]))
                    own.mark(dve.tensor_copy(cums[:, d, 0], end))
                    own.wait()
                    own.mark(dve.tensor_tensor(cums[:, d, 1], cums[:, d, 0], col(CUM), ALU.subtract))
                own.wait()

            @block.scalar
            def _(act):
                act.wait_ge(prep, 1)
                act.activation(pre[:, 1], pre[:, 0], ACT.Abs).then_inc(prep_act, 1)
                act.wait_ge(prep_act, 1)
                act.activation(pre[:, 1], pre[:, 1], ACT.Exp, scale=-1.0).then_inc(prep_act, 1)
                act.wait_ge(prep_act, 2)
                act.activation(pre[:, 1], pre[:, 1], ACT.Ln, bias=1.0).then_inc(prep_act, 1)
                act.activation(a_rows[:, :], a_rows[:, :], ACT.Exp).then_inc(prep_act, 1)
                for d in range(2):
                    act.activation(tab[:, :, d, BETA * H:(BETA + 1) * H], gates[:, :, 4 * d:4 * d + 4], ACT.Sigmoid)
                act.wait_ge(prep, 13)
                for d in range(2):
                    col = lambda n: tab[:, :, d, n * H:(n + 1) * H]
                    act.activation(col(GROW), col(CUM), ACT.Exp)
                    act.activation(col(TAIL), cums[:, d, 1], ACT.Exp)
                    act.activation(col(END), cums[:, d, 0], ACT.Exp)

            @block.tensor
            def _(pe):
                pe.wait_ge(prep, 5)
                for d in range(2):
                    x = logs[:, d].rearrange("p t h -> p (t h)")
                    pe.matmul(banks[d][0][:, 0, 0:TILES * H], upto[:, d, :], x, start=True, stop=True)
                    ins = pe.matmul(banks[d][1][:, 0, 0:TILES * H], ones[:, :], x, start=True, stop=True)
                ins.then_inc(prep_pe, 1)

        k_ch, q_ch = sb("k_channels", [P, 2, 2, H, P]), sb("q_channels", [P, 2, 2, H, P])
        k_tok, v_tok = sb("k_tokens", [P, 2, 2, H, P]), sb("v_tokens", [P, 2, 2, H, P])
        big = lambda n: [sb(f"{n}_{d}", [P, H, P]) for d in ("f", "b")]
        sc = [sb(f"scalars_{d}", [P, 6, H]) for d in ("f", "b")]
        g_wide, decay, grow, qd = big("g_wide"), big("decay"), big("grow"), big("q_grown")
        at_, lt, kg, kt = big("attn_T"), big("L_T"), big("k_grown"), big("k_tail")
        T, U, Y, nw, vn, S = big("T"), big("U"), big("Y"), big("minus_w_T"), big("v_new"), big("state")
        M = [sb(f"M_T_{d}", [P, LEVELS, H, P]) for d in ("f", "b")]
        o_sb = sb("o_chunk", [P, 2, 2, H, P])
        loaded = both(lambda d: Event(top, f"c_loaded_{d}", 64))
        stored = both(lambda d: Event(top, f"c_stored_{d}", 16))
        state_ready = both(lambda d: Event(top, f"c_state_{d}"))
        scalars, gram, diff, exps = ct("scalars"), ct("gram", 3), ct("diff"), ct("exps", 2)
        pool_out, masks = ct("pool_out", 3), ct("masks", LEVELS + 1)
        products = ct("products", 2)
        inv_pe = ct("inv_pe", 2 * LEVELS)
        y_copied, tu = ct("y_copied", LEVELS), ct("tu", LEVELS)
        w_pe, w_copied, vnew_pe, vnew, o_pe, o_copied, s_pe = (ct(x) for x in
            ("w_pe", "w_copied", "vnew_pe", "vnew", "o_pe", "o_copied", "s_pe"))
        states_set = sem("c_states_set")
        own_dve = sem("c_own_dve")
        wide = lambda x: x.unsqueeze(2).broadcast_to([P, H, P])
        heads = lambda m: m.unsqueeze(1).broadcast_to([P, H, P])

        with nc.Block() as block:
            @block.sync
            def _(sp):
                def load(i, j):
                    cs = (i * 2 + j, turned(sp, i, j))
                    for d in range(2):
                        c = cs[d]
                        sp.wait_ge(*state_ready[d].before_last(i, j))
                        for buf, h0 in ((q_ch, 0), (k_ch, H)):
                            sp.dma_start(buf[:, j, d], dr["feat"][h0:h0 + H, :, bass.ds(c * P, P)].rearrange("h p s -> p h s")).then_inc(loaded[d][j], 16)
                        for buf, c0 in ((k_tok, W), (v_tok, 2 * W)):
                            sp.dma_start(buf[:, j, d].rearrange("p h c -> p (h c)"), tile_rows(dr["tok"][:, c0:c0 + W], c)).then_inc(loaded[d][j], 16)

                def chunk(i, j, last=False):
                    if not last:
                        load(*following(i, j))
                    cs = (i * 2 + j, turned(sp, i, j))
                    for d in range(2):
                        c = cs[d]
                        sp.wait_ge(*o_copied[d].now(i * 2 + j))
                        sp.dma_start(tile_rows(dr["o_gdn"][d], c), o_sb[:, j, d].rearrange("p h c -> p (h c)")).then_inc(stored[d][j], 16)

                load(0, 0)
                rounds(sp, None, chunk)
                for d in range(2):
                    for j in range(2):
                        sp.wait_ge(stored[d][j], 16 * (TILES // 2))

            @block.gpsimd
            def _(pool):
                def chunk(i, j, last=False):
                    t = i * 2 + j
                    for d in range(2):
                        pool.wait_ge(*exps[d].now(t, 1))
                        pool.tensor_tensor(decay[d][:, :, :], decay[d][:, :, :], heads(upto[:, d, :]), ALU.mult).then_inc(masks[d].sem, 1)
                    for d in range(2):
                        pool.wait_ge(*products[d].now(t))
                        for n in range(LEVELS):
                            if n == 0:
                                pool.wait_ge(*tu[d].last(t))
                            pool.tensor_tensor(M[d][:, n], lt[d][:, :, :], heads(level[:, d, n, :]), ALU.mult).then_inc(masks[d].sem, 1)
                    for d in range(2):
                        pool.wait_ge(*loaded[d].now(i, j))
                        pool.wait_ge(*exps[d].now(t, 2))
                        pool.wait_ge(*s_pe[d].last(t))
                        pool.tensor_tensor(kg[d][:, :, :], k_tok[:, j, d], wide(sc[d][:, GROW, :]), ALU.mult).then_inc(pool_out[d].sem, 1)
                        pool.tensor_tensor(qd[d][:, :, :], q_ch[:, j, d], grow[d][:, :, :], ALU.mult).then_inc(pool_out[d].sem, 1)
                        pool.tensor_tensor(kt[d][:, :, :], k_tok[:, j, d], wide(sc[d][:, TAIL, :]), ALU.mult).then_inc(pool_out[d].sem, 1)

                rounds(pool, None, chunk)

            @block.scalar
            def _(act):
                def chunk(i, j, last=False):
                    t = i * 2 + j
                    for d in range(2):
                        act.wait_ge(*diff[d].now(t))
                        act.activation(decay[d][:, :, :], decay[d][:, :, :], ACT.Exp).then_inc(exps[d].sem, 1)
                        act.wait_ge(*pool_out[d].last(t))
                        act.activation(grow[d][:, :, :], banks[d][0][:, :, :], ACT.Exp).then_inc(exps[d].sem, 1)
                    for n in range(LEVELS):
                        for d in range(2):
                            act.wait_ge(*inv_pe[d].now(t, 2 * n + 1))
                            if n == 0:
                                act.wait_ge(*tu[d].last(t))
                            act.activation(Y[d][:, :, :], banks[d][1 if n == 0 else 0][:, :, :], ACT.Copy).then_inc(y_copied[d].sem, 1)
                    for d in range(2):
                        act.wait_ge(*w_pe[d].now(t))
                        act.wait_ge(*vnew[d].last(t))
                        act.activation(nw[d][:, :, :], banks[d][0][:, :, :], ACT.Copy, scale=-1.0).then_inc(w_copied[d].sem, 1)
                    for d in range(2):
                        act.wait_ge(*o_pe[d].now(t))
                        act.wait_ge(*stored[d].before_last(i, j))
                        act.activation(o_sb[:, j, d], banks[d][3][:, :, :], ACT.Copy).then_inc(o_copied[d].sem, 1)

                rounds(act, None, chunk)

            @block.vector
            def _(dve):
                own = Chain(dve, own_dve, 2 * 2 * 3 + 2 * 2 * 3 + 2 * 2 * 2 + 2 * 2 * (LEVELS - 1) + 2 * 2 * 3)
                for d in range(2):
                    ins = dve.memset(S[d][:, :, :], 0.0)
                ins.then_inc(states_set, 1)

                def chunk(i, j, last=False):
                    t = i * 2 + j
                    cs = (t, turned(dve, i, j))
                    for d in range(2):
                        c = cs[d]
                        row = tab[:, bass.ds(c, 1), d, :].rearrange("p a w -> p (a w)")
                        dve.wait_ge(*state_ready[d].last(i, j))
                        own.mark(dve.tensor_copy(sc[d][:, :, :].rearrange("p n h -> p (n h)"), row))
                        own.wait()
                        dve.tensor_copy(g_wide[d][:, :, :], wide(sc[d][:, LOG, :])).then_inc(scalars[d].sem, 1)
                    for d in range(2):
                        dve.wait_ge(*gram[d].now(t, 1))
                        for h in range(H):
                            ins = dve.tensor_scalar(decay[d][:, h, :], banks[d][0][:, h, :], sc[d][:, CUM, h:h + 1], 0.0, ALU.subtract, ALU.min)
                            if h < H - 1:
                                own.mark(ins)
                        ins.then_inc(diff[d].sem, 1)
                    for d in range(2):
                        dve.wait_ge(*masks[d].now(t, 1))
                        dve.wait_ge(*gram[d].now(t, 3))
                        dve.tensor_tensor(at_[d][:, :, :], banks[d][3][:, :, :], decay[d][:, :, :], ALU.mult).then_inc(products[d].sem, 1)
                        for h in range(H):
                            ins = dve.scalar_tensor_tensor(out=lt[d][:, h, :], in0=banks[d][2][:, h, :], scalar=sc[d][:, BETA, h:h + 1],
                                                           in1=decay[d][:, h, :], op0=ALU.mult, op1=ALU.mult)
                            if h < H - 1:
                                own.mark(ins)
                        ins.then_inc(products[d].sem, 1)
                    for n in range(LEVELS):
                        for d in range(2):
                            if n == 0:
                                dve.wait_ge(*y_copied[d].now(t, 1))
                                own.mark(dve.tensor_tensor(T[d][:, :, :], heads(ident[:, :]), banks[d][1][:, :, :], ALU.subtract))
                                dve.wait_ge(*inv_pe[d].now(t, 2))
                                dve.tensor_tensor(U[d][:, :, :], heads(ident[:, :]), banks[d][2][:, :, :], ALU.subtract).then_inc(tu[d].sem, 1)
                                continue
                            dve.wait_ge(*tu[d].now(t, n))
                            dve.wait_ge(*inv_pe[d].now(t, 2 * n + 2))
                            if n < LEVELS - 1:
                                own.mark(dve.tensor_tensor(T[d][:, :, :], T[d][:, :, :], banks[d][1][:, :, :], ALU.subtract))
                            dve.tensor_tensor(U[d][:, :, :], U[d][:, :, :], banks[d][2][:, :, :], ALU.subtract).then_inc(tu[d].sem, 1)
                    for d in range(2):
                        dve.wait_ge(*vnew_pe[d].now(t))
                        dve.tensor_tensor(vn[d][:, :, :], banks[d][1][:, :, :], wide(sc[d][:, BETA, :]), ALU.mult).then_inc(vnew[d].sem, 1)
                    for d in range(2):
                        dve.wait_ge(*s_pe[d].now(t))
                        for h in range(H):
                            ins = dve.scalar_tensor_tensor(out=S[d][:, h, :], in0=S[d][:, h, :], scalar=sc[d][:, END, h:h + 1],
                                                           in1=banks[d][2][:, h, :], op0=ALU.mult, op1=ALU.add)
                            if h < H - 1:
                                own.mark(ins)
                        ins.then_inc(state_ready[d][j], 1)

                own.per = 2 * (2 * 1 + 2 * 3 + 2 * 3 + 2 * (LEVELS - 1) + 2 * 3)
                rounds(dve, own, chunk)

            @block.tensor
            def _(pe):
                pe.wait_ge(states_set, 1)

                def each_head(f):
                    for h in range(H):
                        ins = f(h)
                    return ins

                def chunk(i, j, last=False):
                    t = i * 2 + j
                    mm = pe.matmul
                    for d in range(2):
                        A, B, C, D = banks[d]
                        pe.wait_ge(*scalars[d].now(t))
                        each_head(lambda h: mm(A[:, h, :], g_wide[d][:, h, :], upto[:, d, :], start=True, stop=True)).then_inc(gram[d].sem, 1)
                        pe.wait_ge(*loaded[d].now(i, j))
                        pe.wait_ge(*state_ready[d].last(i, j))
                        each_head(lambda h: mm(C[:, h, :], k_ch[:, j, d, h, :], k_ch[:, j, d, h, :], start=True, stop=True)).then_inc(gram[d].sem, 1)
                        pe.wait_ge(*o_copied[d].last(t))
                        each_head(lambda h: mm(D[:, h, :], k_ch[:, j, d, h, :], q_ch[:, j, d, h, :], start=True, stop=True)).then_inc(gram[d].sem, 1)
                    for n in range(LEVELS):
                        for d in range(2):
                            A, B, C, D = banks[d]
                            pe.wait_ge(*masks[d].now(t, n + 2))
                            if n == 0:
                                pe.wait_ge(*vnew[d].last(t))
                                each_head(lambda h: pe.transpose(B[:, h, :], M[d][:, 0, h, :], ident[:, :])).then_inc(inv_pe[d].sem, 1)
                            else:
                                pe.wait_ge(*tu[d].now(t, n))
                                each_head(lambda h: mm(A[:, h, :], M[d][:, n, h, :], T[d][:, h, :], start=True, stop=True)).then_inc(inv_pe[d].sem, 1)
                        for d in range(2):
                            A, B, C, D = banks[d]
                            pe.wait_ge(*y_copied[d].now(t, n + 1))
                            if n == 0:
                                pe.wait_ge(*products[d].now(t))
                                each_head(lambda h: pe.transpose(C[:, h, :], Y[d][:, h, :], ident[:, :])).then_inc(inv_pe[d].sem, 1)
                            else:
                                if n < LEVELS - 1:
                                    each_head(lambda h: mm(B[:, h, :], U[d][:, h, :], Y[d][:, h, :], start=True, stop=True))
                                each_head(lambda h: mm(C[:, h, :], Y[d][:, h, :], U[d][:, h, :], start=True, stop=True)).then_inc(inv_pe[d].sem, 1)
                    for d in range(2):
                        A, B, C, D = banks[d]
                        pe.wait_ge(*tu[d].now(t))
                        pe.wait_ge(*pool_out[d].now(t))
                        each_head(lambda h: mm(A[:, h, :], kg[d][:, h, :], U[d][:, h, :], start=True, stop=True)).then_inc(w_pe[d].sem, 1)
                    for d in range(2):
                        A, B, C, D = banks[d]
                        pe.wait_ge(*w_copied[d].now(t))
                        for h in range(H):
                            mm(B[:, h, :], U[d][:, h, :], v_tok[:, j, d, h, :], start=True, stop=False)
                            ins = mm(B[:, h, :], nw[d][:, h, :], S[d][:, h, :], start=False, stop=True)
                        ins.then_inc(vnew_pe[d].sem, 1)
                    for d in range(2):
                        A, B, C, D = banks[d]
                        pe.wait_ge(*vnew[d].now(t))
                        for h in range(H):
                            mm(D[:, h, :], qd[d][:, h, :], S[d][:, h, :], start=True, stop=False)
                            ins = mm(D[:, h, :], at_[d][:, h, :], vn[d][:, h, :], start=False, stop=True)
                        ins.then_inc(o_pe[d].sem, 1)
                        each_head(lambda h: mm(C[:, h, :], kt[d][:, h, :], vn[d][:, h, :], start=True, stop=True)).then_inc(s_pe[d].sem, 1)

                rounds(pe, None, chunk)


def attention(nc, top, dr):
    H, K = ATT_HEADS, KV_HEADS
    C = SEQ // 512
    SCALE = ATT_D ** -0.5
    VW = ATT_D + 1
    HALF = ATT_D
    with ExitStack() as ctx:
        sb = lambda n, s, d=F32: ctx.enter_context(nc.sbuf_tensor(n, s, d))
        ps = lambda n, s, d=F32: ctx.enter_context(nc.psum_tensor(n, s, d))
        sem = lambda n: top.semaphore(n)
        ident = sb("ident_d", [P, P])
        v_in = sb("v_in", [P, TILES, K, VW])
        kT = sb("kT", [P, K, 2, SEQ], F32R)
        sc = ps("scores", [P, C, 512])
        consts_in, ones_set = sem("d_consts"), sem("d_ones")
        with ExitStack() as pre:
            k_in = pre.enter_context(nc.sbuf_tensor("k_in", [P, TILES, K, 2, ATT_D], F32))
            q_in = pre.enter_context(nc.sbuf_tensor("q_in", [P, 2, TILES, 2, ATT_D], F32))
            first = pre.enter_context(nc.sbuf_tensor("q_first", [P, 2, SEQ], F32R))
            q_parts = pre.enter_context(nc.sbuf_tensor("q_parts", [P, 2, SEQ], F32R))
            sc2 = pre.enter_context(nc.psum_tensor("turned_q", [P, C, 512], F32))
            k_turned, k_first, k_ready, q_turned = (sem(n) for n in ("d_k_turned", "d_k_first", "d_k_ready", "d_q_turned"))
            q_first, q_ready = sem("d_q_first"), sem("d_q_ready")
            q_in_done, q_stored = [sem(f"d_q_in{j}") for j in range(2)], [sem(f"d_q_stored{j}") for j in range(2)]
            banks = lambda x: x.rearrange("p (c n) -> p c n", c=C)

            with nc.Block() as block:
                @block.sync
                def _(sp):
                    sp.dma_start(ident[:, :], dr["c_ident"]).then_inc(consts_in, 16)
                    k = dr["qk"][:, H * ATT_D:].rearrange("(t p) (g d) -> p t g d", p=P, g=K)
                    for half in range(2):
                        for g in range(K):
                            sp.dma_start(k_in[:, :, g, half, :], k[:, :, g, :]).then_inc(consts_in, 16)
                    for g in range(K):
                        sp.dma_start(v_in[:, :, g, 0:ATT_D], dr["v"].rearrange("(t p) (g d) -> p t g d", p=P, g=K)[:, :, g, :]).then_inc(consts_in, 16)

                    def load(h):
                        if h >= 2:
                            sp.wait_ge(q_turned, h - 1)
                        for half in range(2):
                            sp.dma_start(q_in[:, h % 2, :, half, :], dr["qk"][:, h * ATT_D:(h + 1) * ATT_D].rearrange("(t p) c -> p t c", p=P)).then_inc(q_in_done[h % 2], 16)

                    load(0)
                    for h in range(H):
                        if h + 1 < H:
                            load(h + 1)
                        sp.wait_ge(q_ready, h + 1)
                        sp.dma_start(dr["qT"].rearrange("t p x c -> p x t c")[:, h], q_parts[:, h % 2, :].bitcast(F32).rearrange("p (t c) -> p t c", c=P)).then_inc(q_stored[h % 2], 16)
                    for j in range(2):
                        sp.wait_ge(q_stored[j], 16 * (H // 2))

                @block.gpsimd
                def _(pool):
                    pool.memset(v_in[:, :, :, ATT_D:], 1.0).then_inc(ones_set, 1)

                @block.tensor
                def _(pe):
                    pe.wait_ge(consts_in, 16 * 7)
                    for g in range(K):
                        if g:
                            pe.wait_ge(k_ready, g)
                        for t in range(TILES):
                            ins = pe.transpose(sc[:, t // 4, (t % 4) * P:(t % 4 + 1) * P], k_in[:, t, g].rearrange("p a d -> p (a d)"), ident[:, :])
                        ins.then_inc(k_turned, 1)
                    for h in range(H):
                        pe.wait_ge(q_in_done[h % 2], 32 * (h // 2 + 1))
                        if h:
                            pe.wait_ge(q_ready, h)
                        for t in range(TILES):
                            ins = pe.transpose(sc2[:, t // 4, (t % 4) * P:(t % 4 + 1) * P], q_in[:, h % 2, t].rearrange("p a d -> p (a d)"), ident[:, :])
                        ins.then_inc(q_turned, 1)

                @block.scalar
                def _(act):
                    for g in range(K):
                        act.wait_ge(k_turned, g + 1)
                        act.activation(banks(kT[:, g, 0, :]), sc[:, :, :], ACT.Copy).then_inc(k_first, 1)
                    for h in range(H):
                        act.wait_ge(q_turned, h + 1)
                        if h >= 2:
                            act.wait_ge(q_stored[h % 2], 16 * (h // 2))
                        act.activation(banks(first[:, h % 2, :]), sc2[:, :, :], ACT.Copy).then_inc(q_first, 1)

                @block.vector
                def _(dve):
                    for g in range(K):
                        dve.wait_ge(k_first, g + 1)
                        dve.tensor_tensor(banks(kT[:, g, 1, :]), sc[:, :, :], banks(kT[:, g, 0, :].bitcast(F32)), ALU.subtract).then_inc(k_ready, 1)
                    for h in range(H):
                        dve.wait_ge(q_first, h + 1)
                        if h >= 2:
                            dve.wait_ge(q_stored[h % 2], 16 * (h // 2))
                        f = first[:, h % 2, :].bitcast(F32)
                        dve.tensor_copy(q_parts[0:HALF, h % 2, :], f[0:HALF, :])
                        dve.tensor_tensor(banks(q_parts[HALF:P, h % 2, :]), sc2[HALF:P, :, :], banks(f[HALF:P, :]), ALU.subtract).then_inc(q_ready, 1)

        qT = sb("qT_tile", [P, 2, H, P], F32R)
        TB = 2
        BY_ACT = (0, 1)
        peak = sb("row_max", [P, 2, C])
        bias = sb("minus_max", [P, 2, 2])
        prob = sb("probs", [P, 2, SEQ])
        pT = sb("probs_T", [P, C, 4, P])
        over = sb("one_over_sum", [P, 2, 1])
        o_out = sb("o_tile", [P, 2, H * ATT_D])
        tr = ps("probs_turned", [P, TB, 4, P])
        po = ps("pv", [P, 2, 512])
        q_loaded, stored = Event(top, "d_q_loaded", 16), Event(top, "d_stored", 16)
        ct = lambda n, per=1: Count(top, f"d_{n}", per)
        scored, peak_ready, exped, turned = ct("scored", C), ct("peak_ready"), ct("exped", C), ct("turned", C)
        by_act, by_dve = ct("copied_act", len(BY_ACT)), ct("copied_dve", C - len(BY_ACT))
        weighed = ct("weighed", C)
        finished = (sem("d_finished_even"), sem("d_finished_odd"))
        own_dve, blank_set = sem("d_own_dve"), sem("d_blank_set")

        def copied(n, c):
            return by_act.now(n, c + 1) if c in BY_ACT else by_dve.now(n, c - len(BY_ACT) + 1)

        def before(i, j, h):
            return (i * 2 + j) * (H // 2) + h // 2

        def steps(i, j, last):
            for h in range(H):
                nxt = (h + 1, j) if h < H - 1 else (0, 1 - j)
                yield (i * 2 + j) * H + h, h, None if last and h == H - 1 else nxt

        with nc.Block() as block:
            @block.sync
            def _(sp):
                def load(i, j):
                    sp.dma_start(qT[:, j, :, :].bitcast(F32), dr["qT"][bass.ds(i * 2 + j, 1), :, :, :].rearrange("a p x c -> (a p) x c")).then_inc(q_loaded[j], 16)

                def tile(i, j, last=False):
                    if not last:
                        load(*following(i, j))
                    sp.wait_ge(finished[1], (i * 2 + j + 1) * (H // 2) + 1)
                    sp.dma_start(tile_rows(dr["o_att"], i * 2 + j), o_out[:, j, :]).then_inc(stored[j], 16)

                load(0, 0)
                rounds(sp, None, tile)
                for j in range(2):
                    sp.wait_ge(stored[j], 16 * (TILES // 2))

            @block.tensor
            def _(pe):
                def score(n, h, j, c, free):
                    if free is not None:
                        pe.wait_ge(exped.sem, free)
                    for part in range(2):
                        ins = pe.matmul(sc[:, c, :], qT[:, j, h, :], kT[:, h // GROUP, part, c * 512:(c + 1) * 512], start=part == 0, stop=part == 1)
                    ins.then_inc(scored.sem, 1)

                def turn(n, h, c):
                    pe.wait_ge(*(copied(n, c - TB) if c >= TB else by_dve.last(n)))
                    pe.wait_ge(*exped.now(n, c + 1))
                    for q in range(4):
                        ins = pe.transpose(tr[:, c % TB, q, :], prob[:, h % 2, (4 * c + q) * P:(4 * c + q + 1) * P], ident[:, :])
                    ins.then_inc(turned.sem, 1)

                def weigh(i, j, n, h, c):
                    pe.wait_ge(*copied(n, c))
                    if c == 0:
                        pe.wait_ge(finished[h % 2], before(i, j, h) + h % 2)
                    for q in range(4):
                        t = 4 * c + q
                        ins = pe.matmul(po[:, h % 2, 0:VW], pT[:, c, q, :], v_in[:, t, h // GROUP, :], start=t == 0, stop=t == TILES - 1)
                    ins.then_inc(weighed.sem, 1)

                def tile(i, j, last=False):
                    for n, h, nxt in steps(i, j, last):
                        if nxt and nxt[0] == 0:
                            pe.wait_ge(*q_loaded.now(*following(i, j)))
                        for c in range(C):
                            if nxt:
                                score(n + 1, *nxt, c, n * C + c + 1)
                            if c < TB:
                                turn(n, h, c)
                        turn(n, h, 2)
                        weigh(i, j, n, h, 0)
                        turn(n, h, 3)
                        for c in range(1, C):
                            weigh(i, j, n, h, c)

                pe.wait_ge(q_loaded[0], 16)
                for c in range(C):
                    score(0, 0, 0, c, None)
                rounds(pe, None, tile)

            @block.vector
            def _(dve):
                own = Chain(dve, own_dve, 2 * H * (C + 2))

                def peaks(n, h):
                    p = h % 2
                    for c in range(C):
                        dve.wait_ge(*scored.now(n, c + 1))
                        own.mark(dve.tensor_reduce(peak[:, p, c:c + 1], sc[:, c, :], AX.X, ALU.max))
                    own.wait()
                    own.link(dve.tensor_reduce(bias[:, p, 0:1], peak[:, p, :], AX.X, ALU.max))
                    dve.tensor_scalar(bias[:, p, 1:2], bias[:, p, 0:1], -SCALE, None, ALU.mult).then_inc(peak_ready.sem, 1)

                def finish(n1, h, j, i):
                    dve.wait_ge(*weighed.last(n1))
                    own.link(dve.reciprocal(over[:, h % 2], po[:, h % 2, ATT_D:VW]))
                    if h == 0:
                        dve.wait_ge(*stored.before_last(i, j))
                    dve.tensor_scalar(o_out[:, j, h * ATT_D:(h + 1) * ATT_D], po[:, h % 2, 0:ATT_D], over[:, h % 2], None, ALU.mult).then_inc(finished[h % 2], 1)

                def tile(i, j, last=False):
                    for n, h, nxt in steps(i, j, last):
                        if nxt:
                            peaks(n + 1, nxt[0])
                        finish(n, (h - 1) % H, j if h else 1 - j, i)
                        for c in range(len(BY_ACT), C):
                            dve.wait_ge(*turned.now(n, c + 1))
                            dve.wait_ge(*weighed.last(n))
                            dve.tensor_copy(pT[:, c, :, :], tr[:, c % TB, :, :]).then_inc(by_dve.sem, 1)

                dve.memset(po[:, 1, 0:VW], 1.0).then_inc(blank_set, 1)
                dve.wait_ge(blank_set, 1)
                peaks(0, 0)
                rounds(dve, own, tile)
                finish(TILES * H, H - 1, 1, TILES // 2 - 1)

            @block.scalar
            def _(act):
                def exps(n, h, quarters, free):
                    act.wait_ge(*peak_ready.now(n))
                    if free is not None:
                        act.wait_ge(turned.sem, free)
                    for c in quarters:
                        act.activation(prob[:, h % 2, c * 512:(c + 1) * 512], sc[:, c, :], ACT.Exp, bias=bias[:, h % 2, 1:2],
                                       scale=SCALE).then_inc(exped.sem, 1)

                def tile(i, j, last=False):
                    for n, h, nxt in steps(i, j, last):
                        for c in BY_ACT:
                            act.wait_ge(*turned.now(n, c + 1))
                            act.wait_ge(*weighed.last(n))
                            act.activation(pT[:, c, :, :], tr[:, c % TB, :, :], ACT.Copy).then_inc(by_act.sem, 1)
                        if nxt:
                            exps(n + 1, nxt[0], range(C), n * C)

                exps(0, 0, range(C), None)
                rounds(act, None, tile)


def mix_out(nc, top, dr, logits):
    H, W = GDN_HEADS, GDN_W
    NL = N_GROUPS + N_EXPERTS
    with ExitStack() as ctx:
        sb = lambda n, s, d=F32: ctx.enter_context(nc.sbuf_tensor(n, s, d))
        ps = lambda n, s, d=F32: ctx.enter_context(nc.psum_tensor(n, s, d))
        sem = lambda n: top.semaphore(n)
        ev = lambda n, per=1: Event(top, f"e_{n}", per)
        ident, eps = sb("ident_e", [P, P]), sb("eps_e", [P, 1])
        w_out = sb("w_out_sb", [P, KD, D_MODEL])
        w_rt = sb("w_router", [P, KD, NL])
        nw = sb("norm_ffn_rows", [P, D_MODEL])
        gw = sb("gdn_norm_rows", [P, GDN_D])
        o_in = sb("o_both", [P, 2, 2, W])
        z_in = sb("z_in", [P, 2, W])
        a_in = sb("att_in", [P, 2, W])
        x_in = sb("x_in_e", [P, 2, D_MODEL])
        gn = sb("gdn_out", [P, 2, W])
        gsq = sb("gdn_squares", [P, W])
        gst = sb("gdn_stats", [P, 3, H])
        catT = sb("mixed_T", [P, 2, KD, P])
        x1 = sb("x1_tile", [P, 2, D_MODEL])
        sq = sb("squares_e", [P, D_MODEL])
        st = sb("stats_e", [P, 2, 3])
        h2 = sb("h2_tile", [P, 2, D_MODEL])
        hT = sb("h2_T", [P, KD, P])
        pc, po, ph, pl = ps("cat_turned", [P, KD, P]), ps("out_proj", [P, 2, 512]), ps("h2_turned", [P, KD, P]), ps("router", [P, NL])
        consts_in, eps_set, own_dve = sem("e_consts"), sem("e_eps"), sem("e_own_dve")
        o_loaded, x_loaded = ev("o_loaded", 64), ev("x_loaded", 16)
        g_sums, g_rms, g_ready, cat_turned, cat_ready = (ev(n) for n in ("g_sums", "g_rms", "g_ready", "cat_turned", "cat_ready"))
        mixed, x1_ready, x1_sum, x1_rms, h2_ready = (ev(n) for n in ("mixed", "x1_ready", "x1_sum", "x1_rms", "h2_ready"))
        h_turned, hT_ready, routed, kept = (ev(n) for n in ("h_turned", "hT_ready", "routed", "kept"))
        x1_stored, h2_stored = ev("x1_stored", 16), ev("h2_stored", 16)

        with nc.Block() as block:
            @block.sync
            def _(sp):
                def consts(dst, src, **kw):
                    sp.dma_start(dst, src, **kw).then_inc(consts_in, 16)

                def load(i, j):
                    t = i * 2 + j
                    sp.wait_ge(*g_ready.before_last(i, j))
                    sp.wait_ge(*cat_turned.before_last(i, j))
                    for d in range(2):
                        sp.dma_start(o_in[:, j, d, :], tile_rows(dr["o_gdn"][d], t)).then_inc(o_loaded[j], 16)
                    sp.dma_start(z_in[:, j, :], tile_rows(dr["z"], t)).then_inc(o_loaded[j], 16)
                    sp.dma_start(a_in[:, j, :], tile_rows(dr["o_att"], t)).then_inc(o_loaded[j], 16)
                    sp.wait_ge(*x1_ready.before_last(i, j))
                    sp.dma_start(x_in[:, j, :], tile_rows(dr["x"], t)).then_inc(x_loaded[j], 16)

                consts(ident[:, :], dr["c_ident"])
                consts(gw[:, :], dr["gdn_norm_w"].unsqueeze(0).broadcast_to([P, GDN_D]))
                load(0, 0)
                load(0, 1)
                consts(nw[:, :], dr["norm_ffn_w"].unsqueeze(0).broadcast_to([P, D_MODEL]))
                consts(w_out[:, :, :], dr["w_out"].rearrange("(k p) n -> p k n", p=P))
                consts(w_rt[:, :, 0:N_GROUPS], dr["w_router_group"].rearrange("(k p) n -> p k n", p=P), allow_slow_non_contiguous=True)
                consts(w_rt[:, :, N_GROUPS:], dr["w_router_expert"].rearrange("(k p) n -> p k n", p=P), allow_slow_non_contiguous=True)

                def tile(i, j, last=False):
                    t = i * 2 + j
                    sp.wait_ge(*x1_ready.now(i, j))
                    sp.dma_start(tile_rows(dr["x1"], t), x1[:, j, :]).then_inc(x1_stored[j], 16)
                    if not isinstance(i, int):
                        load(i + 1, j)
                    sp.wait_ge(*h2_ready.now(i, j))
                    sp.dma_start(tile_rows(dr["h2"], t), h2[:, j, :]).then_inc(h2_stored[j], 16)

                rounds(sp, None, tile)
                for j in range(2):
                    sp.wait_ge(x1_stored[j], 16 * (TILES // 2))
                    sp.wait_ge(h2_stored[j], 16 * (TILES // 2))

            @block.scalar
            def _(act):
                act.wait_ge(eps_set, 1)

                def head_rms(i, j):
                    act.wait_ge(*g_sums.now(i, j))
                    act.activation(gst[:, 1, :], gst[:, 0, :], ACT.Sqrt, bias=eps[:, :], scale=1.0 / GDN_D).then_inc(g_rms[j], 1)

                def copy_cat(i, j):
                    act.wait_ge(*cat_turned.now(i, j))
                    act.wait_ge(*mixed.before_last(i, j))
                    act.activation(catT[:, j, :, :], pc[:, :, :], ACT.Copy).then_inc(cat_ready[j], 1)

                def tile(i, j, last=False):
                    t = i * 2 + j
                    if not last:
                        copy_cat(*following(i, j))
                    act.wait_ge(*x1_ready.now(i, j))
                    act.wait_ge(*h2_ready.before_last(i, j))
                    act.activation(sq[:, :], x1[:, j, :], ACT.Square, accum_out=st[:, j, 0:1]).then_inc(x1_sum[j], 1)
                    act.wait_ge(*x1_sum.now(i, j))
                    act.activation(st[:, j, 1:2], st[:, j, 0:1], ACT.Sqrt, bias=eps[:, :], scale=1.0 / D_MODEL).then_inc(x1_rms[j], 1)
                    if not isinstance(i, int):
                        head_rms(i + 1, j)
                    act.wait_ge(*h_turned.now(i, j))
                    act.wait_ge(*routed.last(i, j))
                    act.activation(hT[:, :, :], ph[:, :, :], ACT.Copy).then_inc(hT_ready[j], 1)
                    act.wait_ge(*routed.now(i, j))
                    act.activation(at(logits, t), pl[:, :], ACT.Copy).then_inc(kept[j], 1)

                head_rms(0, 0)
                head_rms(0, 1)
                copy_cat(0, 0)
                rounds(act, None, tile)

            @block.vector
            def _(dve):
                own = Chain(dve, own_dve, 2 * 6)
                dve.memset(eps[:, :], EPS).then_inc(eps_set, 1)

                def gdn_out(i, j):
                    heads = lambda x: x.rearrange("p (h d) -> p h d", h=H)
                    o = o_in[:, j, 0, :]
                    dve.wait_ge(*o_loaded.now(i, j))
                    own.link(dve.tensor_tensor(o, o, o_in[:, j, 1, :], ALU.add))
                    own.link(dve.tensor_tensor(gsq[:, :], o, o, ALU.mult))
                    dve.tensor_reduce(gst[:, 0, :], heads(gsq[:, :]), AX.X, ALU.add).then_inc(g_sums[j], 1)
                    own.mark(dve.tensor_tensor(heads(z_in[:, j, :]), heads(z_in[:, j, :]), gw[:, :].unsqueeze(1).broadcast_to([P, H, GDN_D]), ALU.mult))
                    dve.wait_ge(*g_rms.now(i, j))
                    own.link(dve.reciprocal(gst[:, 2, :], gst[:, 1, :]))
                    own.link(dve.tensor_tensor(heads(o), heads(o), gst[:, 2, :].unsqueeze(2).broadcast_to([P, H, GDN_D]), ALU.mult))
                    dve.wait_ge(*cat_turned.before_last(i, j))
                    dve.tensor_tensor(gn[:, j, :], o, z_in[:, j, :], ALU.mult).then_inc(g_ready[j], 1)

                def tile(i, j, last=False):
                    dve.wait_ge(*mixed.now(i, j))
                    dve.wait_ge(*x_loaded.now(i, j))
                    dve.wait_ge(*x1_stored.before_last(i, j))
                    dve.tensor_tensor(x1[:, j, :], x_in[:, j, :], po[:, :, :].rearrange("p a n -> p (a n)"), ALU.add).then_inc(x1_ready[j], 1)
                    dve.wait_ge(*x1_rms.now(i, j))
                    own.link(dve.reciprocal(st[:, j, 2:3], st[:, j, 1:2]))
                    dve.wait_ge(*h2_stored.before_last(i, j))
                    dve.wait_ge(*h_turned.before_last(i, j))
                    dve.scalar_tensor_tensor(out=h2[:, j, :], in0=x1[:, j, :], scalar=st[:, j, 2:3], in1=nw[:, :], op0=ALU.mult, op1=ALU.mult).then_inc(h2_ready[j], 1)
                    if not isinstance(i, int):
                        gdn_out(i + 1, j)

                dve.wait_ge(consts_in, 16 * 6)
                gdn_out(0, 0)
                gdn_out(0, 1)
                rounds(dve, own, tile)

            @block.tensor
            def _(pe):
                pe.wait_ge(consts_in, 16 * 6)

                def turn_cat(i, j):
                    pe.wait_ge(*g_ready.now(i, j))
                    pe.wait_ge(*o_loaded.now(i, j))
                    pe.wait_ge(*cat_ready.last(i, j))
                    for k in range(KD):
                        src = gn[:, j, k * P:(k + 1) * P] if k < H else a_in[:, j, (k - H) * P:(k - H + 1) * P]
                        ins = pe.transpose(pc[:, k, :], src, ident[:, :])
                    ins.then_inc(cat_turned[j], 1)

                def mix(i, j, half):
                    if half == 0:
                        pe.wait_ge(*cat_ready.now(i, j))
                        pe.wait_ge(*x1_ready.last(i, j))
                    for k in range(KD):
                        ins = pe.matmul(po[:, half, :], catT[:, j, k, :], w_out[:, k, half * 512:(half + 1) * 512], start=k == 0, stop=k == KD - 1)
                    if half:
                        ins.then_inc(mixed[j], 1)

                def tile(i, j, last=False):
                    nxt = following(i, j)
                    if not last:
                        turn_cat(*nxt)
                        mix(*nxt, 0)
                    pe.wait_ge(*h2_ready.now(i, j))
                    pe.wait_ge(*hT_ready.last(i, j))
                    for k in range(KD):
                        ins = pe.transpose(ph[:, k, :], h2[:, j, k * P:(k + 1) * P], ident[:, :])
                    ins.then_inc(h_turned[j], 1)
                    if not last:
                        mix(*nxt, 1)
                    pe.wait_ge(*hT_ready.now(i, j))
                    pe.wait_ge(*kept.last(i, j))
                    for k in range(KD):
                        ins = pe.matmul(pl[:, :], hT[:, k, :], w_rt[:, k, :], start=k == 0, stop=k == KD - 1)
                    ins.then_inc(routed[j], 1)

                turn_cat(0, 0)
                mix(0, 0, 0)
                mix(0, 0, 1)
                rounds(pe, None, tile)


BT_SLOT, BT_EVEN, BT_ODD, BT_UPTO = range(4)
BT_ROWS = 4
W_DMAS = 3 * 16


def route(nc, top, dr, logits, dest, gate, table):
    G, E, N = N_GROUPS, PER_GROUP, N_EXPERTS
    BIG = 1e30
    with ExitStack() as ctx:
        sb = lambda n, s, d=F32: ctx.enter_context(nc.sbuf_tensor(n, s, d))
        ps = lambda n, s, d=F32: ctx.enter_context(nc.psum_tensor(n, s, d))
        sem = lambda n: top.semaphore(n)
        iota, before, ones = sb("iota", [P, 64]), sb("before", [P, P]), sb("ones_f", [P, P])
        tokens = sb("token_ids", [P, TILES], I32)
        wide = [P, TILES, E]
        group_d, group_e, group_1 = sb("group_diff", [P, TILES, G]), sb("group_exp", [P, TILES, G]), sb("group_onehot", [P, TILES, G])
        group_p = sb("group_prob", [P, TILES])
        picked = sb("picked_products", [P, TILES, G, E])
        fine, fine_d, fine_e = sb("fine", wide), sb("fine_diff", wide), sb("fine_exp", wide)
        hot = [sb(f"expert_onehot{k}", wide) for k in range(TOP_K)]
        top_v = sb("top_values", [P, 4, TILES])
        col = sb("columns_f", [P, 4, TILES])
        work = sb("index_work", wide)
        OH = [sb(f"assigned{k}", [P, TILES, N]) for k in range(TOP_K)]
        cnt, pos = sb("assigned_both", [P, TILES, N]), sb("positions", [P, TILES, N])
        base = sb("tile_base", [P, TILES + 1, N])
        nb, nbi, incl = sb("expert_blocks", [P, N]), sb("expert_blocks_int", [P, N], I32), sb("blocks_upto", [P, N])
        start = sb("first_slot", [P, N])
        cmp = sb("block_compare", [1, N_BLOCKS, N])
        eb, ebi = sb("block_expert", [1, N_BLOCKS]), sb("block_expert_int", [1, 2, N_BLOCKS], I32)
        rank, tot = ps("rank_in_tile", [P, TILES, N]), ps("tile_totals", [P, TILES, N])
        consts_in, cleared, chain, act_done, counted = sem("f_consts"), sem("f_cleared"), sem("f_dve"), sem("f_act"), sem("f_counted")
        marks = {n: sem(f"f_{n}") for n in ("group_diff", "fine_diff", "counts", "dest")}
        scattered = [sem(f"f_scattered{k}") for k in range(2)]

        with nc.Block() as block:
            @block.sync
            def _(sp):
                for dst, src in ((iota[:, :], "c_iota"), (before[:, :], "c_before"), (ones[:, :], "c_ones"), (tokens[:, :], "c_tokens")):
                    sp.dma_start(dst, dr[src]).then_inc(consts_in, 16)
                sp.dma_start(dr["slot_token"], dr["c_slot0"]).then_inc(cleared, 16)

            @block.vector
            def _(dve):
                own = Chain(dve, chain)
                link = own.link
                tt, ts = dve.tensor_tensor, dve.tensor_scalar
                along = lambda x, n: x.unsqueeze(2).broadcast_to([P, TILES, n])
                numbers = lambda n: iota[:, 0:n].unsqueeze(1).broadcast_to([P, TILES, n])

                def first_hot(out, hits, n, c):
                    w = work[:, :, 0:n]
                    link(ts(w, numbers(n), -64.0, None, ALU.add))
                    link(tt(w, w, hits, ALU.mult))
                    link(dve.tensor_reduce(col[:, c, :], w, AX.X, ALU.min))
                    link(ts(w, numbers(n), -64.0, None, ALU.add))
                    link(tt(out, w, along(col[:, c, :], n), ALU.is_equal))

                dve.wait_ge(consts_in, 64)
                gl = logits[:, :, 0:G]
                link(dve.tensor_reduce(top_v[:, 0, :], gl, AX.X, ALU.max))
                tt(group_d[:, :, :], gl, along(top_v[:, 0, :], G), ALU.subtract).then_inc(marks["group_diff"], 1)
                dve.wait_ge(marks["group_diff"], 1)
                link(ts(group_1[:, :, :], group_d[:, :, :], 0.0, None, ALU.is_ge))
                first_hot(group_1[:, :, :], group_1[:, :, :], G, 0)
                link(tt(picked[:, :, :, :], logits[:, :, G:].rearrange("p t (g e) -> p t g e", g=G),
                        group_1[:, :, :].unsqueeze(3).broadcast_to([P, TILES, G, E]), ALU.mult))
                link(dve.tensor_reduce(fine[:, :, :], picked[:, :, :, :].rearrange("p t g e -> p t e g"), AX.X, ALU.add))
                link(dve.tensor_reduce(top_v[:, 1, :], fine[:, :, :], AX.X, ALU.max))
                tt(fine_d[:, :, :], fine[:, :, :], along(top_v[:, 1, :], E), ALU.subtract).then_inc(marks["fine_diff"], 1)
                dve.wait_ge(marks["fine_diff"], 1)
                link(ts(hot[0][:, :, :], fine_d[:, :, :], 0.0, None, ALU.is_ge))
                first_hot(hot[0][:, :, :], hot[0][:, :, :], E, 1)
                link(dve.scalar_tensor_tensor(out=fine[:, :, :], in0=hot[0][:, :, :], scalar=-BIG, in1=fine_d[:, :, :], op0=ALU.mult, op1=ALU.add))
                dve.tensor_reduce(top_v[:, 2, :], fine[:, :, :], AX.X, ALU.max).then_inc(marks["fine_diff"], 1)
                dve.wait_ge(marks["fine_diff"], 2)
                link(tt(hot[1][:, :, :], fine[:, :, :], along(top_v[:, 2, :], E), ALU.is_equal))
                first_hot(hot[1][:, :, :], hot[1][:, :, :], E, 2)
                for k in range(TOP_K):
                    own.mark(tt(OH[k][:, :, :].rearrange("p t (g e) -> p t g e", g=G), group_1[:, :, :].unsqueeze(3).broadcast_to([P, TILES, G, E]),
                                hot[k][:, :, :].unsqueeze(2).broadcast_to([P, TILES, G, E]), ALU.mult))
                own.wait()
                tt(cnt[:, :, :], OH[0][:, :, :], OH[1][:, :, :], ALU.add).then_inc(marks["counts"], 1)
                dve.wait_ge(act_done, 3)
                own.mark(dve.tensor_reduce(col[:, 0, :], group_e[:, :, :], AX.X, ALU.add))
                link(dve.tensor_reduce(col[:, 1, :], fine_e[:, :, :], AX.X, ALU.add))
                link(dve.reciprocal(col[:, 0:2, :], col[:, 0:2, :]))
                link(tt(col[:, 2, :], top_v[:, 3, :], col[:, 1, :], ALU.mult))
                link(tt(col[:, 3, :], col[:, 1, :], col[:, 2, :], ALU.add))
                link(dve.reciprocal(col[:, 3, :], col[:, 3, :]))
                link(tt(col[:, 3, :], col[:, 3, :], col[:, 0, :], ALU.mult))
                own.mark(tt(gate[:, 0, :], col[:, 1, :], col[:, 3, :], ALU.mult))
                own.mark(tt(gate[:, 1, :], col[:, 2, :], col[:, 3, :], ALU.mult))
                dve.wait_ge(counted, 1)
                link(dve.memset(base[:, 0, :], 0.0))
                for t in range(TILES):
                    link(tt(base[:, t + 1, :], base[:, t, :], tot[:, t, :], ALU.add))
                link(ts(nb[:, :], base[:, TILES, :], float(P - 1), None, ALU.add))
                link(dve.tensor_copy(nbi[:, :], nb[:, :]))
                link(ts(nbi[:, :], nbi[:, :], 7, None, ALU.logical_shift_right))
                link(dve.tensor_copy(nb[:, :], nbi[:, :]))
                link(dve.tensor_tensor_scan(incl[:, :], ones[:, 0:N], nb[:, :], 0.0, ALU.mult, ALU.add))
                link(tt(start[:, :], incl[:, :], nb[:, :], ALU.subtract))
                link(ts(start[:, :], start[:, :], float(P), None, ALU.mult))
                link(tt(pos[:, :, :], rank[:, :, :], base[:, 0:TILES, :], ALU.add))
                link(tt(pos[:, :, :], pos[:, :, :], start[:, :].unsqueeze(1).broadcast_to([P, TILES, N]), ALU.add))
                for k in range(TOP_K):
                    link(tt(OH[k][:, :, :], OH[k][:, :, :], pos[:, :, :], ALU.mult))
                    link(dve.tensor_reduce(col[:, k, :], OH[k][:, :, :], AX.X, ALU.add))
                dve.tensor_copy(dest[:, :, :], col[:, 0:TOP_K, :]).then_inc(marks["dest"], 1)
                link(tt(cmp[:, :, :], incl[0:1, :].unsqueeze(1).broadcast_to([1, N_BLOCKS, N]),
                        iota[0:1, 0:N_BLOCKS].unsqueeze(2).broadcast_to([1, N_BLOCKS, N]), ALU.is_le))
                link(dve.tensor_reduce(eb[:, :], cmp[:, :, :], AX.X, ALU.add))
                link(ts(eb[:, :], eb[:, :], float(N - 1), None, ALU.min))
                link(dve.tensor_copy(ebi[:, 0, :], eb[:, :]))
                own.mark(ts(table[:, BT_SLOT, :], ebi[:, 0, :], 1, None, ALU.bitwise_and))
                link(ts(ebi[:, 1, :], ebi[:, 0, :], 1, None, ALU.logical_shift_right))
                link(dve.tensor_copy(eb[:, :], ebi[:, 1, :]))
                link(ts(eb[:, :], eb[:, :], float(W_DMAS), float(W_DMAS), ALU.mult, ALU.add))
                link(dve.tensor_copy(table[:, BT_EVEN, :], eb[:, :]))
                own.mark(dve.tensor_copy(cmp[:, 0, :], ebi[:, 0, 0:N]))
                link(dve.tensor_copy(cmp[:, 1, :], ebi[:, 0, N:2 * N]))
                odd = cmp[:, 0:2, :].rearrange("o a b -> o (a b)")
                link(ts(odd, odd, 1.0, None, ALU.add))
                link(dve.tensor_copy(ebi[:, 1, :], odd))
                link(ts(ebi[:, 1, :], ebi[:, 1, :], 1, None, ALU.logical_shift_right))
                link(dve.tensor_copy(odd, ebi[:, 1, :]))
                link(ts(odd, odd, float(W_DMAS), None, ALU.mult))
                link(dve.tensor_copy(table[:, BT_ODD, :], odd))
                link(dve.tensor_copy(table[:, BT_UPTO, 0:N], incl[0:1, :]))

            @block.scalar
            def _(act):
                act.wait_ge(marks["group_diff"], 1)
                act.activation(group_e[:, :, :], group_d[:, :, :], ACT.Exp).then_inc(act_done, 1)
                act.wait_ge(marks["fine_diff"], 1)
                act.activation(fine_e[:, :, :], fine_d[:, :, :], ACT.Exp).then_inc(act_done, 1)
                act.wait_ge(marks["fine_diff"], 2)
                act.activation(top_v[:, 3, :], top_v[:, 2, :], ACT.Exp).then_inc(act_done, 1)

            @block.tensor
            def _(pe):
                pe.wait_ge(marks["counts"], 1)
                rows = cnt[:, :, :].rearrange("p t e -> p (t e)")
                pe.matmul(rank[:, :, :].rearrange("p t e -> p (t e)"), before[:, :], rows, start=True, stop=True)
                pe.matmul(tot[:, :, :].rearrange("p t e -> p (t e)"), ones[:, :], rows, start=True, stop=True).then_inc(counted, 1)

            @block.gpsimd
            def _(pool):
                pool.wait_ge(cleared, 16)
                pool.wait_ge(marks["dest"], 1)
                n = 0
                for t in range(TILES):
                    for k in range(TOP_K):
                        if n >= 2:
                            pool.wait_ge(scattered[n % 2], 16 * (n // 2))
                        pool.indirect_dma_start(dr["slot_token"], bass.IndirectOffsetOnAxis(ap=dest[:, k, t:t + 1], axis=0),
                                                tokens[:, t:t + 1], None).then_inc(scattered[n % 2], 16)
                        n += 1
                for x in range(2):
                    pool.wait_ge(scattered[x], 16 * (n // 2))


def experts(nc, top, dr, table):
    with ExitStack() as ctx:
        sb = lambda n, s, d=F32: ctx.enter_context(nc.sbuf_tensor(n, s, d))
        ps = lambda n, s, d=F32: ctx.enter_context(nc.psum_tensor(n, s, d))
        sem = lambda n: top.semaphore(n)
        ev = lambda n, per=1: Event(top, f"g_{n}", per)
        wg, wu = sb("w_gate_slots", [P, 2, KD * FF]), sb("w_up_slots", [P, 2, KD * FF])
        wd = sb("w_down_slots", [P, 2, KF * D_MODEL])
        ident = sb("ident_g", [P, P])
        ids = sb("row_tokens", [P, 2, 1], I32)
        rows = sb("rows", [P, 2, D_MODEL])
        rowsT = sb("rows_T", [P, 2, KD, P])
        sg, hid, hidT = sb("silu_gate", [P, FF]), sb("hidden", [P, FF]), sb("hidden_T", [P, KF, P])
        y = sb("y_block", [P, 2, D_MODEL])
        zeros = sb("zeros_g", [P, D_MODEL])
        pt = ps("rows_turned", [P, KD, P])
        pg, pu, ph = ps("gate_psum", [P, FF]), ps("up_psum", [P, FF]), ps("hidden_turned", [P, KF, P])
        py = ps("down", [P, 2, 512])
        consts_in, zeros_set, passed = sem("g_consts"), sem("g_zeros"), sem("g_passed")
        loaded = Event(top, "g_weights", W_DMAS)
        ids_in, gathered, turned, rowsT_ready = ev("ids", 16), ev("gathered", 16), ev("turned"), ev("rowsT")
        gated, upped, silued, hid_ready, hid_turned, hidT_ready = (ev(n) for n in ("gate", "up", "silu", "hid", "hid_turned", "hidT"))
        downed, y_ready, stored = ev("down", 1), ev("y_ready"), ev("stored", 16)
        done = sem("g_blocks_done")

        def block_loop(eng, body, without=None):
            count = eng.value_load(table[0:1, BT_UPTO, N_EXPERTS - 1:N_EXPERTS], min_val=1, max_val=N_BLOCKS)
            with eng.Fori(0, N_BLOCKS // 2) as i:
                for j in range(2):
                    with eng.If(i * 2 + j < count):
                        body(i, j)
                    if without:
                        with eng.Else():
                            without(i, j)

        with nc.Block() as block:
            @block.sync
            def _(sp):
                sp.dma_start(ident[:, :], dr["c_ident"]).then_inc(consts_in, 16)

                def load(e, j):
                    for buf, name, k in ((wg, "w_gate", KD), (wu, "w_up", KD), (wd, "w_down", KF)):
                        src = dr[name][bass.ds(e, 1) if not isinstance(e, int) else slice(e, e + 1), :, :].rearrange("a (k p) n -> p (a k) n", p=P)
                        sp.dma_start(buf[:, j, :].rearrange("p (k n) -> p k n", k=k), src).then_inc(loaded[j], 16)

                for e in range(2):
                    load(e, e)
                with sp.Fori(1, N_EXPERTS // 2) as i:
                    for j in range(2):
                        upto = sp.value_load(table[0:1, BT_UPTO, bass.ds(i * 2 + (j - 2), 1)], min_val=0, max_val=N_BLOCKS)
                        sp.wait_ge(done, upto)
                        load(i * 2 + j, j)
                for j in range(2):
                    sp.wait_ge(loaded[j], W_DMAS * (N_EXPERTS // 2))

            @block.gpsimd
            def _(pool):
                def gather(i, j):
                    b = i * 2 + j
                    pool.wait_ge(*turned.before_last(i, j))
                    pool.dma_start(ids[:, j, :], tile_rows(dr["slot_token"], b)).then_inc(ids_in[j], 16)
                    pool.wait_ge(*ids_in.now(i, j))
                    pool.sem_inc(passed, 1)
                    pool.indirect_dma_start(rows[:, j, :], None, dr["h2"], bass.IndirectOffsetOnAxis(ap=ids[:, j, :], axis=0)).then_inc(gathered[j], 16)

                gather(0, 0)
                block_loop(pool, lambda i, j: gather(*following(i, j)))

            @block.scalar
            def _(act):
                def copy_rows(i, j):
                    act.wait_ge(*turned.now(i, j))
                    act.wait_ge(*upped.before_last(i, j))
                    act.activation(rowsT[:, j, :, :], pt[:, :, :], ACT.Copy).then_inc(rowsT_ready[j], 1)

                def body(i, j):
                    act.wait_ge(*gated.now(i, j))
                    act.wait_ge(*hid_ready.last(i, j))
                    act.activation(sg[:, :], pg[:, :], ACT.Silu).then_inc(silued[j], 1)
                    copy_rows(*following(i, j))
                    act.wait_ge(*hid_turned.now(i, j))
                    act.wait_ge(*downed.last(i, j))
                    act.activation(hidT[:, :, :], ph[:, :, :], ACT.Copy).then_inc(hidT_ready[j], 1)
                    act.wait_ge(*y_ready.now(i, j))
                    act.dma_start(tile_rows(dr["y"], i * 2 + j), y[:, j, :]).then_inc(stored[j], 16)

                def zero(i, j):
                    act.dma_start(tile_rows(dr["y"], i * 2 + j), zeros[:, :]).then_inc(stored[j], 16)

                copy_rows(0, 0)
                act.wait_ge(zeros_set, 1)
                block_loop(act, body, zero)
                for j in range(2):
                    act.wait_ge(stored[j], 16 * (N_BLOCKS // 2))

            @block.vector
            def _(dve):
                def body(i, j):
                    dve.wait_ge(*silued.now(i, j))
                    dve.wait_ge(*upped.now(i, j))
                    dve.wait_ge(*hid_turned.last(i, j))
                    dve.tensor_tensor(hid[:, :], sg[:, :], pu[:, :], ALU.mult).then_inc(hid_ready[j], 1)
                    dve.wait_ge(*downed.now(i, j))
                    dve.wait_ge(*stored.before_last(i, j))
                    dve.tensor_copy(y[:, j, :], py[:, :, :].rearrange("p a n -> p (a n)")).then_inc(y_ready[j], 1)

                dve.memset(zeros[:, :], 0.0).then_inc(zeros_set, 1)
                block_loop(dve, body)

            @block.tensor
            def _(pe):
                pe.wait_ge(consts_in, 16)

                def turn_rows(i, j):
                    pe.wait_ge(*gathered.now(i, j))
                    pe.wait_ge(*rowsT_ready.last(i, j))
                    for k in range(KD):
                        ins = pe.transpose(pt[:, k, :], rows[:, j, k * P:(k + 1) * P], ident[:, :])
                    ins.then_inc(turned[j], 1)

                def body(i, j):
                    b = i * 2 + j
                    entry = lambda r, top: pe.value_load(table[0:1, r, bass.ds(b, 1)], min_val=0, max_val=top)
                    even, odd = entry(BT_EVEN, 65535), entry(BT_ODD, 65535)
                    slot = entry(BT_SLOT, 1)
                    pe.wait_ge(loaded[0], even)
                    pe.wait_ge(loaded[1], odd)
                    part = lambda w, c0, c1: w[:, bass.ds(slot, 1), c0:c1].rearrange("p a n -> p (a n)")
                    pe.wait_ge(*rowsT_ready.now(i, j))
                    pe.wait_ge(*silued.last(i, j))
                    for k in range(KD):
                        ins = pe.matmul(pg[:, :], rowsT[:, j, k, :], part(wg, k * FF, (k + 1) * FF), start=k == 0, stop=k == KD - 1)
                    ins.then_inc(gated[j], 1)
                    turn_rows(*following(i, j))
                    pe.wait_ge(*hid_ready.last(i, j))
                    for k in range(KD):
                        ins = pe.matmul(pu[:, :], rowsT[:, j, k, :], part(wu, k * FF, (k + 1) * FF), start=k == 0, stop=k == KD - 1)
                    ins.then_inc(upped[j], 1)
                    pe.wait_ge(*hid_ready.now(i, j))
                    pe.wait_ge(*hidT_ready.last(i, j))
                    for k in range(KF):
                        ins = pe.transpose(ph[:, k, :], hid[:, k * P:(k + 1) * P], ident[:, :])
                    ins.then_inc(hid_turned[j], 1)
                    pe.wait_ge(*hidT_ready.now(i, j))
                    pe.wait_ge(*y_ready.last(i, j))
                    for half in range(2):
                        for k in range(KF):
                            c = k * D_MODEL + half * 512
                            ins = pe.matmul(py[:, half, :], hidT[:, k, :], part(wd, c, c + 512), start=k == 0, stop=k == KF - 1)
                    ins.then_inc(downed[j], 1)
                    pe.wait_ge(*downed.now(i, j))
                    pe.sem_inc(done, 1)

                turn_rows(0, 0)
                block_loop(pe, body)


def combine(nc, top, dr, dest, gate):
    with ExitStack() as ctx:
        sb = lambda n, s, d=F32: ctx.enter_context(nc.sbuf_tensor(n, s, d))
        sem = lambda n: top.semaphore(n)
        ev = lambda n, per=1: Event(top, f"h_{n}", per)
        eps, nw = sb("eps_h", [P, 1]), sb("final_norm_rows", [P, D_MODEL])
        x1 = sb("x1_h", [P, 2, D_MODEL])
        idx = sb("slots_h", [P, 2, TOP_K], I32)
        g = sb("gates_h", [P, 2, TOP_K])
        ys = sb("y_rows", [P, 2, TOP_K, D_MODEL])
        acc, sq = sb("sum_h", [P, 2, D_MODEL]), sb("squares_h", [P, D_MODEL])
        st = sb("stats_h", [P, 2, 3])
        out = sb("out_tile", [P, 2, D_MODEL])
        consts_in, eps_set, own_dve = sem("h_consts"), sem("h_eps"), sem("h_own_dve")
        passed = sem("h_passed")
        x_loaded, indexed, gathered, summed = ev("x_loaded", 16), ev("indexed"), ev("gathered", 32), ev("summed")
        sum_sq, rms, ready, stored = ev("sum_sq"), ev("rms"), ev("ready"), ev("stored", 16)

        with nc.Block() as block:
            @block.sync
            def _(sp):
                sp.dma_start(nw[:, :], dr["final_norm_w"].unsqueeze(0).broadcast_to([P, D_MODEL])).then_inc(consts_in, 16)

                def load(i, j):
                    sp.wait_ge(*summed.before_last(i, j))
                    sp.dma_start(x1[:, j, :], tile_rows(dr["x1"], i * 2 + j)).then_inc(x_loaded[j], 16)

                def tile(i, j, last=False):
                    if not last:
                        load(*following(i, j))
                    sp.wait_ge(*ready.now(i, j))
                    sp.dma_start(tile_rows(dr["out"], i * 2 + j), out[:, j, :]).then_inc(stored[j], 16)

                load(0, 0)
                rounds(sp, None, tile)
                for j in range(2):
                    sp.wait_ge(stored[j], 16 * (TILES // 2))

            @block.gpsimd
            def _(pool):
                with pool.Fori(0, TILES // 2) as i:
                    for j in range(2):
                        pool.wait_ge(*indexed.now(i, j))
                        pool.wait_ge(*summed.before_last(i, j))
                        pool.sem_inc(passed, 1)
                        for k in range(TOP_K):
                            pool.indirect_dma_start(ys[:, j, k, :], None, dr["y"],
                                                    bass.IndirectOffsetOnAxis(ap=idx[:, j, k:k + 1], axis=0)).then_inc(gathered[j], 16)

            @block.scalar
            def _(act):
                act.wait_ge(eps_set, 1)
                with act.Fori(0, TILES // 2) as i:
                    for j in range(2):
                        act.wait_ge(*summed.now(i, j))
                        act.activation(sq[:, :], acc[:, j, :], ACT.Square, accum_out=st[:, j, 0:1]).then_inc(sum_sq[j], 1)
                        act.wait_ge(*sum_sq.now(i, j))
                        act.activation(st[:, j, 1:2], st[:, j, 0:1], ACT.Sqrt, bias=eps[:, :], scale=1.0 / D_MODEL).then_inc(rms[j], 1)

            @block.vector
            def _(dve):
                own = Chain(dve, own_dve, 2 * 4)

                def index(i, j):
                    t = i * 2 + j
                    dve.wait_ge(*gathered.before_last(i, j))
                    own.mark(dve.tensor_copy(g[:, j, :].unsqueeze(2), gate[:, :, bass.ds(t, 1)]))
                    dve.tensor_copy(idx[:, j, :].unsqueeze(2), dest[:, :, bass.ds(t, 1)]).then_inc(indexed[j], 1)

                def tile(i, j, last=False):
                    if not last:
                        index(*following(i, j))
                    own.wait()
                    dve.wait_ge(*gathered.now(i, j))
                    own.link(dve.tensor_scalar(acc[:, j, :], ys[:, j, 0, :], g[:, j, 0:1], None, ALU.mult))
                    own.link(dve.scalar_tensor_tensor(out=acc[:, j, :], in0=ys[:, j, 1, :], scalar=g[:, j, 1:2], in1=acc[:, j, :], op0=ALU.mult, op1=ALU.add))
                    dve.wait_ge(*x_loaded.now(i, j))
                    dve.tensor_tensor(acc[:, j, :], acc[:, j, :], x1[:, j, :], ALU.add).then_inc(summed[j], 1)
                    dve.wait_ge(*rms.now(i, j))
                    own.link(dve.reciprocal(st[:, j, 2:3], st[:, j, 1:2]))
                    dve.wait_ge(*stored.before_last(i, j))
                    dve.scalar_tensor_tensor(out=out[:, j, :], in0=acc[:, j, :], scalar=st[:, j, 2:3], in1=nw[:, :], op0=ALU.mult, op1=ALU.mult).then_inc(ready[j], 1)

                dve.memset(eps[:, :], EPS).then_inc(eps_set, 1)
                dve.wait_ge(consts_in, 16)
                index(0, 0)
                rounds(dve, own, tile)


def build(nc, dr, until=99):
    for name, shape in SCRATCH.items():
        dr[name] = nc.dram_tensor(f"scratch_{name}", shape, F32, kind="Internal").ap()
    dr["qT"] = nc.dram_tensor("scratch_qT", (TILES, P, ATT_HEADS, P), F32, kind="Internal").ap()
    dr["slot_token"] = nc.dram_tensor("scratch_slot_token", (SLOTS + P, 1), I32, kind="Internal").ap()
    with ExitStack() as top:
        sb = lambda n, s, d=F32: top.enter_context(nc.sbuf_tensor(n, s, d))
        gates = sb("gates", [P, TILES, 16])
        with nc.sbuf_tensor("xT_all", [P, KD, SEQ], F32) as xT_all:
            keep = {"xT_all": xT_all, "gates": gates}
            with Stage(nc) as stage:
                project_tokens(nc, stage, dr, keep)
            if until > 1:
                with Stage(nc) as stage:
                    project_features(nc, stage, dr, keep)
        if until > 2:
            with Stage(nc) as stage:
                gated_delta(nc, stage, dr, gates)
        if until > 3:
            with Stage(nc) as stage:
                attention(nc, stage, dr)
        if until > 4:
            logits = sb("logits", [P, TILES, N_GROUPS + N_EXPERTS])
            dest = sb("dest", [P, TOP_K, TILES], I32)
            gate = sb("gate", [P, TOP_K, TILES])
            table = sb("block_table", [1, BT_ROWS, N_BLOCKS], I32)
            with Stage(nc) as stage:
                mix_out(nc, stage, dr, logits)
            if until > 5:
                with Stage(nc) as stage:
                    route(nc, stage, dr, logits, dest, gate, table)
            if until > 6:
                with Stage(nc) as stage:
                    experts(nc, stage, dr, table)
            if until > 7:
                with Stage(nc) as stage:
                    combine(nc, stage, dr, dest, gate)
def constants():
    f = np.float32
    p = np.arange(P)
    rows = SEQ // GRID_W
    row = np.repeat(np.arange(rows), GRID_W).astype(f)
    col = np.tile(np.arange(GRID_W), rows).astype(f)
    axis = ATT_D // 2
    inv = (f(10000.0) ** (-np.arange(0, axis, 2).astype(f) / f(axis))).astype(f)
    ang = np.concatenate([row[:, None] * inv, col[:, None] * inv], axis=-1).astype(f)
    out = {"c_ident": np.eye(P, dtype=f), "c_cos": np.cos(ang).astype(f), "c_sin": np.sin(ang).astype(f),
           "c_ones": np.ones((P, P), f)}
    upto = (p[:, None] <= p[None, :]).astype(f)
    out["c_upto"] = np.stack([upto, upto.T], 0).transpose(1, 0, 2).copy()
    out["c_before"] = (p[:, None] < p[None, :]).astype(f)
    level = []
    for n in range(7):
        b = 1 << n
        same = (p[:, None] // (2 * b)) == (p[None, :] // (2 * b))
        m = (same & (p[:, None] % (2 * b) < b) & (p[None, :] % (2 * b) >= b)).astype(f)
        level.append([m, m.T])
    out["c_level"] = np.array(level, f).transpose(2, 1, 0, 3).copy()
    n = np.zeros((2, CONV_BLOCKS), f)
    n[0, :GDN_HEADS], n[1, :GDN_HEADS] = GDN_D, GDN_D * EPS
    n[0, GDN_HEADS:2 * GDN_HEADS], n[1, GDN_HEADS:2 * GDN_HEADS] = 1, EPS
    n[1, 2 * GDN_HEADS:] = 1
    out["c_norm"] = np.broadcast_to(n.reshape(1, -1), (P, 2 * CONV_BLOCKS)).copy()
    out["c_iota"] = np.broadcast_to(np.arange(64, dtype=f), (P, 64)).copy()
    out["c_slot0"] = np.zeros((SLOTS + P, 1), np.int32)
    out["c_tokens"] = (np.arange(TILES)[None, :] * P + p[:, None]).astype(np.int32)
    return out


SHAPES = {"x": (SEQ, D_MODEL), "norm_mix_w": (D_MODEL,), "w_in": (D_MODEL, D_IN), "conv_w": (CONV_W, 3 * GDN_W),
          "a_log": (1, 8), "dt_bias": (1, 8), "gdn_norm_w": (GDN_D,), "q_norm_w": (ATT_D,),
          "k_norm_w": (ATT_D,), "w_out": (D_MODEL, D_MODEL), "norm_ffn_w": (D_MODEL,),
          "w_router_group": (D_MODEL, N_GROUPS), "w_router_expert": (D_MODEL, N_EXPERTS),
          "w_gate": (N_EXPERTS, D_MODEL, FF), "w_up": (N_EXPERTS, D_MODEL, FF), "w_down": (N_EXPERTS, FF, D_MODEL),
          "final_norm_w": (D_MODEL,)}
SCRATCH = {"z": (SEQ, GDN_W), "qk": (SEQ, ATT_QK), "v": (SEQ, ATT_KV),
           "feat": (CONV_BLOCKS, P, SEQ), "tok": (SEQ, 3 * GDN_W), "o_gdn": (2, SEQ, GDN_W), "o_att": (SEQ, GDN_W), 
           "x1": (SEQ, D_MODEL), "h2": (SEQ, D_MODEL), "y": (SLOTS, D_MODEL)}


def kernel(**inputs):
    import numpy as _np
    import concourse.bacc as _bacc
    from concourse import mybir as _mybir
    from concourse.bass_utils import run_bass_kernel_spmd as _run

    nc = _bacc.Bacc("TRN2", target_bir_lowering=False, num_devices=1)
    arrays, dr = {}, {}
    for name, shape in SHAPES.items():
        a = _np.ascontiguousarray(inputs[name]).reshape(shape)
        arrays[f"in_{name}"] = a
        dr[name] = nc.dram_tensor(f"in_{name}", a.shape, _mybir.dt.from_np(a.dtype), kind="ExternalInput").ap()
    for name, a in constants().items():
        arrays[name] = a
        dr[name] = nc.dram_tensor(name, a.shape, _mybir.dt.from_np(a.dtype), kind="ExternalInput").ap()
    dr["out"] = nc.dram_tensor("out", (SEQ, D_MODEL), F32, kind="ExternalOutput").ap()
    build(nc, dr)
    r = _run(nc, [arrays], core_ids=[0])
    return r.results[0]["out"].reshape(1, SEQ, D_MODEL)
```

```python
import numpy as np
from contextlib import ExitStack
import concourse.bass as bass
from concourse import mybir
from concourse.alu_op_type import AluOpType as ALU

F32 = mybir.dt.float32
F32R = mybir.dt.float32r
I32 = mybir.dt.int32
ACT = mybir.ActivationFunctionType
AX = mybir.AxisListType

P = 128
SEQ, D_MODEL = 2048, 1024
TILES = SEQ // P
KD = D_MODEL // P
GDN_HEADS, GDN_D = 4, 128
CONV_W = 5
CONV_BLOCKS = 3 * GDN_HEADS
ATT_HEADS, KV_HEADS, ATT_D = 8, 2, 64
GROUP = ATT_HEADS // KV_HEADS
GRID_W = 64
N_GROUPS, PER_GROUP, TOP_K = 4, 8, 2
N_EXPERTS = N_GROUPS * PER_GROUP
FF = 512
KF = FF // P
EPS = 1e-6
GDN_W = GDN_HEADS * GDN_D
C_Z = 3 * GDN_W
C_GATES = C_Z + GDN_W
C_ATT = C_GATES + 4 * GDN_HEADS
ATT_QK = (ATT_HEADS + KV_HEADS) * ATT_D
ATT_KV = KV_HEADS * ATT_D
D_IN = C_ATT + ATT_QK + ATT_KV
N_BLOCKS = -(-(SEQ * TOP_K + N_EXPERTS * (P - 1)) // P)
SLOTS = N_BLOCKS * P


class Stage:

    def __init__(self, nc):
        self.nc, self.sems = nc, []

    def semaphore(self, name):
        self.sems.append(self.nc.alloc_semaphore(name=name))
        return self.sems[-1]

    def __enter__(self):
        return self

    def __exit__(self, *_):
        self.nc.clear_and_free_semaphores(self.sems)
        self.nc.all_engine_barrier()


class Event:

    def __init__(self, stage, name, per=1):
        self.sems = [stage.semaphore(f"{name}_{x}") for x in ("even", "odd")]
        self.per = per

    def __getitem__(self, j):
        return self.sems[j]

    def now(self, i, j, n=None):
        return self.sems[j], i * self.per + (self.per if n is None else n)

    def last(self, i, j):
        return self.sems[1 - j], (i + j) * self.per

    def before_last(self, i, j):
        return self.sems[j], i * self.per


class Count:

    def __init__(self, stage, name, per=1):
        self.sem, self.per = stage.semaphore(name), per

    def now(self, t, n=None):
        return self.sem, t * self.per + (self.per if n is None else n)

    def last(self, t):
        return self.sem, t * self.per


class Chain:

    def __init__(self, eng, sem, per_round=0):
        self.eng, self.sem, self.per, self.base, self.n, self.start = eng, sem, per_round, 0, 0, 0

    def round(self, i):
        self.base, self.n = i * self.per + self.start, 0

    def mark(self, ins):
        ins.then_inc(self.sem, 1)
        self.n += 1

    def wait(self):
        self.eng.wait_ge(self.sem, self.base + self.n)

    def link(self, ins):
        self.mark(ins)
        self.wait()

    def close(self):
        assert self.n == self.per, f"a round has {self.n} links"


def following(i, j):
    return (i, 1) if j == 0 else (i + 1, 0)


def rounds(eng, own, tile, n=TILES):
    def pair(i, end):
        if own:
            own.round(i)
        for j in range(2):
            tile(i, j, end and j == 1)

    if own:
        own.start = own.n
    with eng.Fori(0, n // 2 - 1) as i:
        pair(i, False)
        if own:
            own.close()
    pair(n // 2 - 1, True)


def tile_rows(dram, t, n=1):
    return dram.rearrange("(t p) w -> t p w", p=P)[bass.ds(t, 1), :, :].rearrange("a p w -> (a p) w")


def at(tensor, t):
    return tensor[:, bass.ds(t, 1), :].rearrange("p a w -> p (a w)")


def project_tokens(nc, top, dr, keep):
    NT = GDN_W + ATT_QK + ATT_KV + 16
    Z0, Q0, K0 = 0, GDN_W, 2 * GDN_W
    NK = NT - K0
    NH = ATT_HEADS + KV_HEADS
    half = ATT_D // 2
    with ExitStack() as ctx:
        sb = lambda n, s, d=F32: ctx.enter_context(nc.sbuf_tensor(n, s, d))
        ps = lambda n, s, d=F32: ctx.enter_context(nc.psum_tensor(n, s, d))
        sem = lambda n: top.semaphore(n)
        ev = lambda n, per=1: Event(top, n, per)
        w_tok = sb("w_tok", [P, KD, NT])
        ident = sb("ident_a", [P, P])
        nw = sb("norm_mix_cols", [P, KD])
        qkw = sb("qk_norm_rows", [P, NH, ATT_D])
        cos = sb("rope_cos", [P, TILES, half])
        sin = sb("rope_sin", [P, TILES, half])
        x_in = sb("x_in", [P, 2, D_MODEL])
        squares = sb("squares_a", [P, D_MODEL])
        stat = sb("stat_a", [P, 2, 4])
        eps = sb("eps_a", [P, 1])
        xn = sb("xn", [P, 2, D_MODEL])
        xT = sb("xT_tile", [P, 2, KD, P])
        zs = sb("z_silu", [P, 2, GDN_W])
        qk = sb("qk_raw", [P, 2, ATT_QK + ATT_KV])
        qsq = sb("qk_squares", [P, NH, ATT_D])
        qs = sb("qk_stats", [P, 2, 3, NH])
        qn = sb("qk_normed", [P, NH, ATT_D])
        rot = sb("rope_products", [P, 4, NH, half])
        qr = sb("qk_roped", [P, 2, ATT_QK])
        tp = ps("transposed", [P, KD, P])
        pz = ps("proj_z", [P, GDN_W])
        pq = ps("proj_q", [P, GDN_W])
        pk = ps("proj_kv", [P, NK])
        z_weights_in, weights_in = sem("a_z_weights_in"), sem("a_weights_in")
        consts_in, rope_in = sem("a_consts_in"), sem("a_rope_in")
        eps_set = sem("a_eps_set")
        x_loaded, row_sum, row_rms, normed = ev("x_loaded", 16), ev("row_sum"), ev("row_rms"), ev("x_normed")
        transposed, xT_ready, copied = ev("x_transposed"), ev("xT_ready"), ev("xT_copied")
        projected, taken, z_ready = ev("projected", 3), ev("proj_taken"), ev("z_ready")
        qk_sums, qk_rms, roped = ev("qk_sums"), ev("qk_rms"), ev("qk_roped")
        stored_z, stored_qk, stored_v = ev("z_stored", 16), ev("qk_stored", 16), ev("v_stored", 16)
        dve_chain = sem("a_dve")
        xT_all, gates = keep["xT_all"], keep["gates"]

        with nc.Block() as block:
            @block.sync
            def _(sp):
                def load(i, j):
                    sp.wait_ge(*row_sum.before_last(i, j))
                    sp.wait_ge(*normed.before_last(i, j))
                    sp.dma_start(x_in[:, j, :], tile_rows(dr["x"], i * 2 + j)).then_inc(x_loaded[j], 16)

                w = dr["w_in"].rearrange("(k p) n -> p k n", p=P)
                load(0, 0)
                sp.dma_start(ident[:, :], dr["c_ident"]).then_inc(consts_in, 16)
                sp.dma_start(nw[:, :], dr["norm_mix_w"].rearrange("(k p) -> p k", p=P),
                             allow_slow_non_contiguous=True).then_inc(consts_in, 16)
                sp.dma_start(w_tok[:, :, 0:GDN_W], w[:, :, C_Z:C_GATES]).then_inc(z_weights_in, 16)
                load(0, 1)
                sp.dma_start(w_tok[:, :, GDN_W:NT - 16], w[:, :, C_ATT:D_IN]).then_inc(weights_in, 16)
                sp.dma_start(w_tok[:, :, NT - 16:NT], w[:, :, C_GATES:C_ATT],
                             allow_slow_non_contiguous=True).then_inc(weights_in, 16)
                for h in range(NH):
                    src = dr["q_norm_w"] if h < ATT_HEADS else dr["k_norm_w"]
                    sp.dma_start(qkw[:, h, :], src.unsqueeze(0).broadcast_to([P, ATT_D])).then_inc(rope_in, 16)
                sp.dma_start(cos[:, :, :], dr["c_cos"].rearrange("(t p) f -> p t f", p=P)).then_inc(rope_in, 16)
                sp.dma_start(sin[:, :, :], dr["c_sin"].rearrange("(t p) f -> p t f", p=P)).then_inc(rope_in, 16)
                with sp.Fori(1, TILES // 2) as i:
                    for j in range(2):
                        load(i, j)

            @block.gpsimd
            def _(pool):
                with pool.Fori(0, TILES // 2) as i:
                    for j in range(2):
                        t = i * 2 + j
                        pool.wait_ge(*z_ready.now(i, j))
                        pool.dma_start(tile_rows(dr["z"], t), zs[:, j, :]).then_inc(stored_z[j], 16)
                        pool.wait_ge(*roped.now(i, j))
                        pool.dma_start(tile_rows(dr["qk"], t), qr[:, j, :]).then_inc(stored_qk[j], 16)
                        pool.dma_start(tile_rows(dr["v"], t), qk[:, j, ATT_QK:]).then_inc(stored_v[j], 16)
                for j in range(2):
                    for s in (stored_z, stored_qk, stored_v):
                        pool.wait_ge(s[j], 16 * (TILES // 2))

            @block.scalar
            def _(act):
                act.wait_ge(eps_set, 1)

                def row_stats(i, j):
                    act.wait_ge(*x_loaded.now(i, j))
                    act.wait_ge(*normed.before_last(i, j))
                    act.activation(squares[:, :], x_in[:, j, :], ACT.Square, accum_out=stat[:, j, 0:1]).then_inc(row_sum[j], 1)
                    act.wait_ge(*row_sum.now(i, j))
                    act.activation(stat[:, j, 1:2], stat[:, j, 0:1], ACT.Sqrt, bias=eps[:, 0:1], scale=1.0 / D_MODEL).then_inc(row_rms[j], 1)

                def copy_xT(i, j):
                    act.wait_ge(*xT_ready.now(i, j))
                    act.activation(xT_all[:, :, bass.ds((i * 2 + j) * P, P)], xT[:, j, :, :], ACT.Copy).then_inc(copied[j], 1)

                def tile(i, j, last=False):
                    t = i * 2 + j
                    if not last:
                        row_stats(*following(i, j))
                    act.wait_ge(*projected.now(i, j, 1))
                    act.wait_ge(*stored_z.before_last(i, j))
                    act.activation(zs[:, j, :], pz[:, :], ACT.Silu).then_inc(z_ready[j], 1)
                    if not last:
                        copy_xT(*following(i, j))
                    act.wait_ge(*projected.now(i, j, 3))
                    act.wait_ge(*stored_v.before_last(i, j))
                    act.wait_ge(*roped.before_last(i, j))
                    act.activation(qk[:, j, 0:GDN_W], pq[:, :], ACT.Copy)
                    act.activation(qk[:, j, GDN_W:], pk[:, 0:NK - 16], ACT.Copy)
                    act.activation(at(gates, t), pk[:, NK - 16:NK], ACT.Copy).then_inc(taken[j], 1)
                    act.wait_ge(*qk_sums.now(i, j))
                    act.activation(qs[:, j, 1, :], qs[:, j, 0, :], ACT.Sqrt, bias=eps[:, 0:1], scale=1.0 / ATT_D).then_inc(qk_rms[j], 1)

                row_stats(0, 0)
                copy_xT(0, 0)
                rounds(act, None, tile)

            @block.vector
            def _(dve):
                own = Chain(dve, dve_chain, 2 * 10)
                dve.memset(eps[:, :], EPS).then_inc(eps_set, 1)
                dve.wait_ge(consts_in, 32)

                def normalize(i, j):
                    dve.wait_ge(*row_rms.now(i, j))
                    own.link(dve.reciprocal(stat[:, j, 2:3], stat[:, j, 1:2]))
                    dve.wait_ge(*transposed.before_last(i, j))
                    dve.tensor_scalar(xn[:, j, :], x_in[:, j, :], stat[:, j, 2:3], None, ALU.mult).then_inc(normed[j], 1)
                    dve.wait_ge(*transposed.now(i, j))
                    dve.wait_ge(*projected.before_last(i, j))
                    dve.wait_ge(*copied.before_last(i, j))
                    dve.tensor_tensor(xT[:, j, :, :], tp[:, :, :], nw[:, :].unsqueeze(2).broadcast_to([P, KD, P]),
                                      ALU.mult).then_inc(xT_ready[j], 1)

                def tile(i, j, last=False):
                    t = i * 2 + j
                    if not last:
                        normalize(*following(i, j))
                    dve.wait_ge(*taken.now(i, j))
                    raw = qk[:, j, 0:ATT_QK].rearrange("p (h d) -> p h d", d=ATT_D)
                    own.link(dve.tensor_tensor(qsq[:, :, :], raw, raw, ALU.mult))
                    dve.tensor_reduce(qs[:, j, 0, :], qsq[:, :, :], AX.X, ALU.add).then_inc(qk_sums[j], 1)
                    dve.wait_ge(*qk_rms.now(i, j))
                    own.link(dve.reciprocal(qs[:, j, 2, :], qs[:, j, 1, :]))
                    own.link(dve.tensor_tensor(qn[:, :, :], raw, qs[:, j, 2, :].unsqueeze(2).broadcast_to([P, NH, ATT_D]), ALU.mult))
                    own.link(dve.tensor_tensor(qn[:, :, :], qn[:, :, :], qkw[:, :, :], ALU.mult))
                    pair = qn[:, :, :].rearrange("p h (f two) -> p h f two", two=2)
                    c = at(cos, t).unsqueeze(1).broadcast_to([P, NH, half])
                    s = at(sin, t).unsqueeze(1).broadcast_to([P, NH, half])
                    own.mark(dve.tensor_tensor(rot[:, 0], pair[:, :, :, 0], c, ALU.mult))
                    own.mark(dve.tensor_tensor(rot[:, 1], pair[:, :, :, 1], s, ALU.mult))
                    own.mark(dve.tensor_tensor(rot[:, 2], pair[:, :, :, 0], s, ALU.mult))
                    own.link(dve.tensor_tensor(rot[:, 3], pair[:, :, :, 1], c, ALU.mult))
                    out = qr[:, j, :].rearrange("p (h f two) -> p h f two", h=NH, two=2)
                    dve.wait_ge(*stored_qk.before_last(i, j))
                    own.mark(dve.tensor_tensor(out[:, :, :, 0], rot[:, 0], rot[:, 1], ALU.subtract))
                    dve.tensor_tensor(out[:, :, :, 1], rot[:, 2], rot[:, 3], ALU.add).then_inc(roped[j], 1)

                normalize(0, 0)
                dve.wait_ge(rope_in, 16 * (2 + NH))
                rounds(dve, own, tile)

            @block.tensor
            def _(pe):
                pe.wait_ge(consts_in, 32)

                def transposes(i, j):
                    pe.wait_ge(*normed.now(i, j))
                    pe.wait_ge(*xT_ready.last(i, j))
                    for k in range(KD):
                        ins = pe.transpose(tp[:, k, :], xn[:, j, k * P:(k + 1) * P], ident[:, :])
                    ins.then_inc(transposed[j], 1)

                def tile(i, j, last=False):
                    pe.wait_ge(*xT_ready.now(i, j))
                    for out, c0, c1 in ((pz, Z0, Q0), (pq, Q0, K0), (pk, K0, NT)):
                        if out is pq:
                            pe.wait_ge(weights_in, 32)
                        if out is pk and not last:
                            transposes(*following(i, j))
                        pe.wait_ge(*(z_ready if out is pz else taken).last(i, j))
                        for k in range(KD):
                            ins = pe.matmul(out[:, :], xT[:, j, k, :], w_tok[:, k, c0:c1], start=k == 0, stop=k == KD - 1)
                        ins.then_inc(projected[j], 1)

                transposes(0, 0)
                pe.wait_ge(z_weights_in, 16)
                rounds(pe, None, tile)


def project_features(nc, top, dr, keep):
    N = CONV_BLOCKS
    C = SEQ // 512
    PAD = CONV_W // 2
    TB = 3
    with ExitStack() as ctx:
        sb = lambda n, s, d=F32: ctx.enter_context(nc.sbuf_tensor(n, s, d))
        ps = lambda n, s, d=F32: ctx.enter_context(nc.psum_tensor(n, s, d))
        sem = lambda n: top.semaphore(n)
        ev = lambda n, per=1: Event(top, n, per)
        w_blk = sb("w_blk", [P, 2, KD, P])
        ident = sb("ident_b", [P, P])
        norm = sb("norm_scale_bias", [P, 2, N, 1])
        cw_rows = sb("conv_w_rows", [CONV_W, N * P])
        cw = sb("conv_w_cols", [P, N, CONV_W])
        raw = sb("conv_in", [P, 2, SEQ + 2 * PAD])
        acc = sb("conv_acc", [P, SEQ])
        act_out = sb("silu_out", [P, SEQ])
        sq = sb("squares_b", [P, 4, P])
        inv = sb("norms_b", [P, 3, TILES])
        feat = sb("features", [P, 2, SEQ])
        tok = sb("features_by_token", [P, 2, TILES, P])
        pp = ps("proj_b", [P, C, 512])
        pt = ps("to_tokens", [P, TB, 4, P])
        pb = ps("to_channels", [P, 4, P])
        consts_in, cw_done, cw_ready, pads = sem("b_consts"), sem("b_conv_w_T"), sem("b_conv_w_ready"), sem("b_pads")
        w_loaded = ev("w_blk_loaded", 16)
        projected, raw_ready, conv_done = ev("b_projected", C), ev("b_raw", C), ev("b_conv")
        silu_done = ev("b_silu")
        summed, norm2_ready, rms_ready = ev("b_summed", C), ev("b_norm2", C), ev("b_rms", C)
        turned, tok_ready, returned, feat_ready = ev("b_turned", C), ev("b_tok", C), ev("b_returned", C), ev("b_feat", C)
        stored_f, stored_t = ev("b_feat_stored", 16), ev("b_tok_stored", 16)
        dve_chain = sem("b_dve")

        with nc.Block() as block:
            @block.sync
            def _(sp):
                sp.dma_start(ident[:, :], dr["c_ident"]).then_inc(consts_in, 16)
                sp.dma_start(cw_rows[:, :], dr["conv_w"]).then_inc(consts_in, 16)
                sp.dma_start(norm[:, :, :, :], dr["c_norm"].rearrange("p (a n) -> p a n", a=2).unsqueeze(3)).then_inc(consts_in, 16)

                def load(i, j):
                    w = dr["w_in"].rearrange("(k p) n -> p k n", p=P)
                    sp.wait_ge(*projected.before_last(i, j))
                    sp.dma_start(w_blk[:, j, :, :], w[:, :, bass.ds((i * 2 + j) * P, P)]).then_inc(w_loaded[j], 16)

                def tile(i, j, ahead):
                    m = i * 2 + j
                    if ahead:
                        load(i + 1, j)
                    sp.wait_ge(*tok_ready.now(i, j))
                    sp.dma_start(dr["tok"].rearrange("(t p) c -> p t c", p=P)[:, :, bass.ds(m * P, P)], tok[:, j, :, :]).then_inc(stored_t[j], 16)
                    sp.wait_ge(*feat_ready.now(i, j))
                    sp.dma_start(dr["feat"][bass.ds(m, 1), :, :].rearrange("a p s -> (a p) s"), feat[:, j, :]).then_inc(stored_f[j], 16)

                load(0, 0)
                load(0, 1)
                with sp.Fori(0, N // 2 - 1) as i:
                    for j in range(2):
                        tile(i, j, True)
                for j in range(2):
                    tile(N // 2 - 1, j, False)
                for j in range(2):
                    sp.wait_ge(stored_f[j], 16 * (N // 2))
                    sp.wait_ge(stored_t[j], 16 * (N // 2))

            @block.tensor
            def _(pe):
                pe.wait_ge(consts_in, 48)
                for m in range(N):
                    ins = pe.transpose(pt[:, 0, 0, m * CONV_W:(m + 1) * CONV_W], cw_rows[:, m * P:(m + 1) * P], ident[0:CONV_W, 0:CONV_W])
                ins.then_inc(cw_done, 1)
                pe.wait_ge(cw_ready, 1)

                def project(i, j, c, ks=range(KD)):
                    if c == 0:
                        pe.wait_ge(*w_loaded.now(i, j))
                    if ks[0] == 0:
                        pe.wait_ge(*raw_ready.last(i, j))
                    for k in ks:
                        ins = pe.matmul(pp[:, c, :], w_blk[:, j, k, :], keep["xT_all"][:, k, c * 512:(c + 1) * 512], start=k == 0, stop=k == KD - 1)
                    if ks[-1] == KD - 1:
                        ins.then_inc(projected[j], 1)

                def turn(i, j, c):
                    pe.wait_ge(*(tok_ready.now(i, j, c - TB + 1) if c >= TB else tok_ready.last(i, j)))
                    if c == 0:
                        pe.wait_ge(*silu_done.now(i, j))
                    for q in range(4):
                        ins = pe.transpose(pt[:, c % TB, q, :], act_out[:, (4 * c + q) * P:(4 * c + q + 1) * P], ident[:, :])
                    ins.then_inc(turned[j], 1)

                def turn_back(i, j, c):
                    pe.wait_ge(*tok_ready.now(i, j, c + 1))
                    pe.wait_ge(*(feat_ready.now(i, j, c) if c else feat_ready.last(i, j)))
                    for q in range(4):
                        ins = pe.transpose(pb[:, q, :], tok[:, j, 4 * c + q, :], ident[:, :])
                    ins.then_inc(returned[j], 1)

                def tile(i, j, last=False):
                    nxt = following(i, j)
                    if not last:
                        project(*nxt, 0)
                        project(*nxt, 1)
                        project(*nxt, 2, range(KD // 2))
                    for c in range(TB):
                        turn(i, j, c)
                    if not last:
                        project(*nxt, 2, range(KD // 2, KD))
                    turn(i, j, 3)
                    turn_back(i, j, 0)
                    if not last:
                        project(*nxt, 3, range(KD // 4))
                    turn_back(i, j, 1)
                    if not last:
                        project(*nxt, 3, range(KD // 4, KD // 2))
                    turn_back(i, j, 2)
                    if not last:
                        project(*nxt, 3, range(KD // 2, KD))
                    turn_back(i, j, 3)

                for c in range(C):
                    project(0, 0, c)
                rounds(pe, None, tile, N)

            @block.scalar
            def _(act):
                act.wait_ge(pads, 1)

                def copy_raw(i, j, c):
                    act.wait_ge(*projected.now(i, j, c + 1))
                    act.wait_ge(*conv_done.before_last(i, j))
                    act.activation(raw[:, j, PAD + c * 512:PAD + (c + 1) * 512], pp[:, c, :], ACT.Copy).then_inc(raw_ready[j], 1)

                def tile(i, j, last=False):
                    m = i * 2 + j
                    if not last:
                        copy_raw(*following(i, j), 0)
                        copy_raw(*following(i, j), 1)
                    act.wait_ge(*conv_done.now(i, j))
                    act.wait_ge(*turned.last(i, j))
                    act.activation(act_out[:, :], acc[:, :], ACT.Silu).then_inc(silu_done[j], 1)
                    act.wait_ge(*tok_ready.last(i, j))

                    def norms(c):
                        act.wait_ge(*turned.now(i, j, c + 1))
                        for q in range(4):
                            n = 4 * c + q
                            ins = act.activation(sq[:, q, :], pt[:, c % TB, q, :], ACT.Square, accum_out=inv[:, 0, n:n + 1])
                        ins.then_inc(summed[j], 1)
                        act.wait_ge(*norm2_ready.now(i, j, c + 1))
                        act.activation(inv[:, 1, 4 * c:4 * c + 4], inv[:, 0, 4 * c:4 * c + 4], ACT.Sqrt).then_inc(rms_ready[j], 1)

                    for c in range(TB):
                        norms(c)
                    if not last:
                        copy_raw(*following(i, j), 2)

                    def copy_feat(c):
                        act.wait_ge(*returned.now(i, j, c + 1))
                        act.wait_ge(*stored_f.before_last(i, j))
                        act.activation(feat[:, j, c * 512:(c + 1) * 512], pb[:, :, :].rearrange("p q c -> p (q c)"), ACT.Copy).then_inc(feat_ready[j], 1)

                    norms(3)
                    copy_feat(0)
                    copy_feat(1)
                    copy_feat(2)
                    if not last:
                        copy_raw(*following(i, j), 3)
                    copy_feat(3)

                for c in range(C):
                    copy_raw(0, 0, c)
                rounds(act, None, tile, N)

            @block.vector
            def _(dve):
                own = Chain(dve, dve_chain, 2 * (CONV_W - 1 + C))
                dve.memset(raw[:, :, 0:PAD], 0.0)
                dve.memset(raw[:, :, SEQ + PAD:], 0.0).then_inc(pads, 1)
                dve.wait_ge(cw_done, 1)
                dve.tensor_copy(cw[:, :, :], pt[:, 0, 0, 0:N * CONV_W].rearrange("p (m w) -> p m w", w=CONV_W)).then_inc(cw_ready, 1)
                dve.wait_ge(cw_ready, 1)
                dve.wait_ge(consts_in, 48)

                def convolve(i, j):
                    m = i * 2 + j
                    dve.wait_ge(*raw_ready.now(i, j))
                    dve.wait_ge(*silu_done.last(i, j))
                    for w in range(CONV_W):
                        c = cw[:, bass.ds(m, 1), w:w + 1].rearrange("p a b -> p (a b)")
                        x = raw[:, j, w:w + SEQ]
                        if w == 0:
                            own.link(dve.tensor_scalar(acc[:, :], x, c, None, ALU.mult))
                        elif w < CONV_W - 1:
                            own.link(dve.scalar_tensor_tensor(out=acc[:, :], in0=x, scalar=c, in1=acc[:, :], op0=ALU.mult, op1=ALU.add))
                        else:
                            dve.scalar_tensor_tensor(out=acc[:, :], in0=x, scalar=c, in1=acc[:, :], op0=ALU.mult, op1=ALU.add).then_inc(conv_done[j], 1)

                def tile(i, j, last=False):
                    m = i * 2 + j
                    dve.wait_ge(*stored_t.before_last(i, j))
                    dve.wait_ge(*returned.before_last(i, j))
                    for c in range(C):
                        part = slice(4 * c, 4 * c + 4)
                        col = lambda r: norm[:, r, bass.ds(m, 1), :].rearrange("p a b -> p (a b)")
                        dve.wait_ge(*summed.now(i, j, c + 1))
                        dve.tensor_scalar(inv[:, 0, part], inv[:, 0, part], col(0), col(1), ALU.mult, ALU.add).then_inc(norm2_ready[j], 1)
                        dve.wait_ge(*rms_ready.now(i, j, c + 1))
                        own.link(dve.reciprocal(inv[:, 2, part], inv[:, 1, part]))
                        dve.tensor_tensor(tok[:, j, part, :], pt[:, c % TB, :, :],
                                          inv[:, 2, part].unsqueeze(2).broadcast_to([P, 4, P]), ALU.mult).then_inc(tok_ready[j], 1)
                    if not last:
                        convolve(*following(i, j))

                convolve(0, 0)
                rounds(dve, own, tile, N)


def gated_delta(nc, top, dr, gates):
    H, W = GDN_HEADS, GDN_W
    LEVELS = 7
    CUM, BETA, GROW, TAIL, END, LOG = range(6)
    with ExitStack() as ctx:
        sb = lambda n, s, d=F32: ctx.enter_context(nc.sbuf_tensor(n, s, d))
        ps = lambda n, s, d=F32: ctx.enter_context(nc.psum_tensor(n, s, d))
        sem = lambda n: top.semaphore(n)
        both = lambda make: [make(d) for d in ("fwd", "bwd")]
        ct = lambda n, per=1: both(lambda d: Count(top, f"c_{n}_{d}", per))
        ident, ones = sb("ident_c", [P, P]), sb("ones_c", [P, P])
        upto = sb("upto", [P, 2, P])
        level = sb("level_masks", [P, 2, LEVELS, P])
        dt_rows, a_rows = sb("dt_rows", [P, 8]), sb("a_log_rows", [P, 8])
        pre = sb("gate_work", [P, 4, TILES, 8])
        logs = sb("log_decays", [P, 2, TILES, H])
        cums = sb("cum_decays", [P, 2, 2, TILES, H])
        tab = sb("gate_table", [P, TILES, 2, 6 * H])
        banks = [[ps(f"bank_{d}{n}", [P, H, P]) for n in "abcd"] for d in ("f", "b")]
        consts_in, prep = sem("c_consts"), sem("c_prep")
        prep_act, prep_pe = sem("c_prep_act"), sem("c_prep_pe")

        def turned(eng, i, j):
            return i * (-2) + (TILES - 1 - j)

        with nc.Block() as block:
            @block.sync
            def _(sp):
                sp.dma_start(ident[:, :], dr["c_ident"]).then_inc(consts_in, 16)
                sp.dma_start(ones[:, :], dr["c_ones"]).then_inc(consts_in, 16)
                sp.dma_start(upto[:, :, :], dr["c_upto"]).then_inc(consts_in, 16)
                sp.dma_start(level[:, :, :, :], dr["c_level"]).then_inc(consts_in, 16)
                sp.dma_start(dt_rows[:, :], dr["dt_bias"].broadcast_to([P, 8])).then_inc(consts_in, 16)
                sp.dma_start(a_rows[:, :], dr["a_log"].broadcast_to([P, 8])).then_inc(consts_in, 16)

            @block.vector
            def _(dve):
                own = Chain(dve, prep)
                dve.wait_ge(consts_in, 96)
                rows = lambda x: x[:, :].unsqueeze(1).broadcast_to([P, TILES, 8])
                own.link(dve.tensor_tensor(pre[:, 0], gates[:, :, 8:16], rows(dt_rows), ALU.add))
                dve.wait_ge(prep_act, 4)
                own.link(dve.scalar_tensor_tensor(out=pre[:, 2], in0=pre[:, 0], scalar=0.0, in1=pre[:, 1], op0=ALU.max, op1=ALU.add))
                own.link(dve.tensor_scalar(a_rows[:, :], a_rows[:, :], -1.0, None, ALU.mult))
                for d in range(2):
                    own.link(dve.tensor_tensor(logs[:, d], pre[:, 2, :, 4 * d:4 * d + 4],
                                               a_rows[:, 4 * d:4 * d + 4].unsqueeze(1).broadcast_to([P, TILES, H]), ALU.mult))
                dve.wait_ge(prep_pe, 1)
                for d in range(2):
                    g = banks[d][0][:, 0, 0:TILES * H].rearrange("p (t h) -> p t h", h=H)
                    end = banks[d][1][:, 0, 0:TILES * H].rearrange("p (t h) -> p t h", h=H)
                    col = lambda n: tab[:, :, d, n * H:(n + 1) * H]
                    own.mark(dve.tensor_copy(col(CUM), g))
                    own.mark(dve.tensor_copy(col(LOG), logs[:, d]))
                    own.mark(dve.tensor_copy(cums[:, d, 0], end))
                    own.wait()
                    own.mark(dve.tensor_tensor(cums[:, d, 1], cums[:, d, 0], col(CUM), ALU.subtract))
                own.wait()

            @block.scalar
            def _(act):
                act.wait_ge(prep, 1)
                act.activation(pre[:, 1], pre[:, 0], ACT.Abs).then_inc(prep_act, 1)
                act.wait_ge(prep_act, 1)
                act.activation(pre[:, 1], pre[:, 1], ACT.Exp, scale=-1.0).then_inc(prep_act, 1)
                act.wait_ge(prep_act, 2)
                act.activation(pre[:, 1], pre[:, 1], ACT.Ln, bias=1.0).then_inc(prep_act, 1)
                act.activation(a_rows[:, :], a_rows[:, :], ACT.Exp).then_inc(prep_act, 1)
                for d in range(2):
                    act.activation(tab[:, :, d, BETA * H:(BETA + 1) * H], gates[:, :, 4 * d:4 * d + 4], ACT.Sigmoid)
                act.wait_ge(prep, 13)
                for d in range(2):
                    col = lambda n: tab[:, :, d, n * H:(n + 1) * H]
                    act.activation(col(GROW), col(CUM), ACT.Exp)
                    act.activation(col(TAIL), cums[:, d, 1], ACT.Exp)
                    act.activation(col(END), cums[:, d, 0], ACT.Exp)

            @block.tensor
            def _(pe):
                pe.wait_ge(prep, 5)
                for d in range(2):
                    x = logs[:, d].rearrange("p t h -> p (t h)")
                    pe.matmul(banks[d][0][:, 0, 0:TILES * H], upto[:, d, :], x, start=True, stop=True)
                    ins = pe.matmul(banks[d][1][:, 0, 0:TILES * H], ones[:, :], x, start=True, stop=True)
                ins.then_inc(prep_pe, 1)

        k_ch, q_ch = sb("k_channels", [P, 2, 2, H, P]), sb("q_channels", [P, 2, 2, H, P])
        k_tok, v_tok = sb("k_tokens", [P, 2, 2, H, P]), sb("v_tokens", [P, 2, 2, H, P])
        big = lambda n: [sb(f"{n}_{d}", [P, H, P]) for d in ("f", "b")]
        pair = lambda n: [[sb(f"{n}_{d}{j}", [P, H, P]) for j in range(2)] for d in ("f", "b")]
        sc = sb("scalars", [P, 2, 2, 6, H])
        g_wide, decay, grow, lt = big("g_wide"), big("decay"), big("grow"), big("L_T")
        qd, kg, kt, at_ = pair("q_grown"), pair("k_grown"), pair("k_tail"), pair("attn_T")
        T, U, rest, vn, S = big("T"), big("U"), big("v_less_known"), big("v_new"), big("state")
        M = [sb(f"M_T_{d}", [P, LEVELS, H, P]) for d in ("f", "b")]
        Y, Y_last = big("Y"), big("Y_last")
        o_sb = sb("o_chunk", [P, 2, 2, H, P])
        loaded = both(lambda d: Event(top, f"c_loaded_{d}", 64))
        stored = both(lambda d: Event(top, f"c_stored_{d}", 16))
        state_ready = both(lambda d: Event(top, f"c_state_{d}"))
        scalars, gram, diff, exps = ct("scalars"), ct("gram", 3), ct("diff"), ct("exps", 2)
        k_tail, grown = ct("k_tail"), ct("grown", 2)
        masks = ct("masks", LEVELS + 1)
        products = ct("products", 2)
        y_pe, y_copied = ct("y_pe", LEVELS - 1), ct("y_copied", LEVELS - 1)
        tmt_pe, t_ready = ct("tmt_pe", LEVELS - 1), ct("t_ready", LEVELS - 1)
        u_first, u_last, umu_pe = ct("u_first"), ct("u_last"), ct("umu_pe")
        u_pe, u_copied = ct("u_pe", LEVELS - 2), ct("u_copied", LEVELS - 2)
        known_pe, rest_ready, vnew_pe, vnew, o_pe, o_copied, s_pe = (ct(x) for x in
            ("known_pe", "rest", "vnew_pe", "vnew", "o_pe", "o_copied", "s_pe"))
        cleared = sem("c_cleared")
        own_dve = sem("c_own_dve")
        wide = lambda x: x.unsqueeze(2).broadcast_to([P, H, P])
        heads = lambda m: m.unsqueeze(1).broadcast_to([P, H, P])

        def blocks(x, n, parity):
            return x.rearrange("p h (m two b) -> p (h m) two b", two=2, b=1 << n)[:, :, parity, :]

        WIDE = 2
        some_blocks = lambda x, n, parity: x if n <= WIDE else blocks(x, n, parity)

        def head_blocks(x, n, parity):
            return x if n <= WIDE else mask_blocks(x, n, parity)

        def mask_blocks(x, n, parity):
            return x.rearrange("p (m two b) -> p m two b", two=2, b=1 << n)[:, :, parity, :]

        with nc.Block() as block:
            @block.sync
            def _(sp):
                def load(i, j):
                    cs = (i * 2 + j, turned(sp, i, j))
                    for d in range(2):
                        c = cs[d]
                        sp.wait_ge(*state_ready[d].before_last(i, j))
                        for buf, h0 in ((q_ch, 0), (k_ch, H)):
                            sp.dma_start(buf[:, j, d], dr["feat"][h0:h0 + H, :, bass.ds(c * P, P)].rearrange("h p s -> p h s")).then_inc(loaded[d][j], 16)
                        for buf, c0 in ((k_tok, W), (v_tok, 2 * W)):
                            sp.dma_start(buf[:, j, d].rearrange("p h c -> p (h c)"), tile_rows(dr["tok"][:, c0:c0 + W], c)).then_inc(loaded[d][j], 16)

                def chunk(i, j, last=False):
                    if not last:
                        load(*following(i, j))
                    cs = (i * 2 + j, turned(sp, i, j))
                    for d in range(2):
                        c = cs[d]
                        sp.wait_ge(*o_copied[d].now(i * 2 + j))
                        sp.dma_start(tile_rows(dr["o_gdn"][d], c), o_sb[:, j, d].rearrange("p h c -> p (h c)")).then_inc(stored[d][j], 16)

                load(0, 0)
                rounds(sp, None, chunk)
                for d in range(2):
                    for j in range(2):
                        sp.wait_ge(stored[d][j], 16 * (TILES // 2))

            @block.gpsimd
            def _(pool):
                def prepare(i, j, last_t):
                    t = i * 2 + j
                    for d in range(2):
                        pool.wait_ge(*loaded[d].now(i, j))
                        pool.wait_ge(*scalars[d].now(t))
                        pool.wait_ge(*state_ready[d].before_last(i, j))
                        pool.tensor_tensor(kt[d][j][:, :, :], k_tok[:, j, d], wide(sc[:, d, j, TAIL, :]), ALU.mult).then_inc(k_tail[d].sem, 1)
                    for d in range(2):
                        pool.wait_ge(*exps[d].now(t, 1))
                        pool.tensor_tensor(decay[d][:, :, :], decay[d][:, :, :], heads(upto[:, d, :]), ALU.mult).then_inc(masks[d].sem, 1)
                        pool.wait_ge(*exps[d].now(t, 2))
                        pool.tensor_tensor(kg[d][j][:, :, :], k_ch[:, j, d], grow[d][:, :, :], ALU.mult).then_inc(grown[d].sem, 1)
                        pool.tensor_tensor(qd[d][j][:, :, :], q_ch[:, j, d], grow[d][:, :, :], ALU.mult).then_inc(grown[d].sem, 1)
                    for n in range(LEVELS):
                        for d in range(2):
                            pool.wait_ge(*products[d].now(t, 1))
                            if last_t is not None:
                                if n == 0:
                                    pool.wait_ge(*u_first[d].now(last_t))
                                    pool.wait_ge(*tmt_pe[d].now(last_t, 1))
                                else:
                                    pool.wait_ge(*y_pe[d].now(last_t, n))
                            b = 1 << n
                            cols = lambda x: x.rearrange("p h (m two b) -> p h m two b", two=2, b=b)[:, :, :, 1 - d, :]
                            mask = mask_blocks(level[:, d, n, :], n, 1 - d).unsqueeze(1).broadcast_to([P, H, P // (2 * b), b])
                            pool.tensor_tensor(cols(M[d][:, n]), cols(lt[d][:, :, :]), mask, ALU.mult).then_inc(masks[d].sem, 1)

                pool.wait_ge(cleared, 1)
                prepare(0, 0, None)
                rounds(pool, None, lambda i, j, last=False: None if last else prepare(*following(i, j), i * 2 + j))

            @block.scalar
            def _(act):
                def exponents(i, j, d):
                    t = i * 2 + j
                    act.wait_ge(*diff[d].now(t))
                    act.activation(decay[d][:, :, :], decay[d][:, :, :], ACT.Exp).then_inc(exps[d].sem, 1)
                    act.wait_ge(*grown[d].last(t))
                    act.activation(grow[d][:, :, :], banks[d][3][:, :, :], ACT.Exp).then_inc(exps[d].sem, 1)

                def chunk(i, j, last=False):
                    t = i * 2 + j
                    for n in range(1, LEVELS):
                        for d in range(2):
                            act.wait_ge(*y_pe[d].now(t, n))
                            if n == LEVELS - 1:
                                act.wait_ge(*umu_pe[d].last(t))
                            out = Y if n < LEVELS - 1 else Y_last
                            act.activation(some_blocks(out[d][:, :, :], n, d), some_blocks(banks[d][0][:, :, :], n, d), ACT.Copy).then_inc(y_copied[d].sem, 1)
                            if n > 1:
                                act.wait_ge(*u_pe[d].now(t, n - 1))
                                act.activation(U[d][:, :, :], banks[d][2][:, :, :], ACT.Copy).then_inc(u_copied[d].sem, 1)
                        if n in (2, 3) and not last:
                            exponents(*following(i, j), n - 2)
                    for d in range(2):
                        act.wait_ge(*o_pe[d].now(t))
                        act.wait_ge(*stored[d].before_last(i, j))
                        act.activation(o_sb[:, j, d], banks[d][3][:, :, :], ACT.Copy).then_inc(o_copied[d].sem, 1)

                act.wait_ge(cleared, 1)
                for d in range(2):
                    exponents(0, 0, d)
                rounds(act, None, chunk)

            @block.vector
            def _(dve):
                own = Chain(dve, own_dve, 2 * 2 * (1 + 3 * (H - 1)))
                for d in range(2):
                    dve.memset(S[d][:, :, :], 0.0)
                    dve.memset(Y_last[d][:, :, :], 0.0)
                    ins = dve.memset(M[d][:, :, :, :], 0.0)
                ins.then_inc(cleared, 1)

                def take_scalars(i, j):
                    cs = (i * 2 + j, turned(dve, i, j))
                    for d in range(2):
                        row = tab[:, bass.ds(cs[d], 1), d, :].rearrange("p a w -> p (a w)")
                        dve.wait_ge(*state_ready[d].before_last(i, j))
                        own.link(dve.tensor_copy(sc[:, d, j, :, :].rearrange("p n h -> p (n h)"), row))
                        dve.tensor_copy(g_wide[d][:, :, :], wide(sc[:, d, j, LOG, :])).then_inc(scalars[d].sem, 1)

                def differences(i, j, d):
                    dve.wait_ge(*gram[d].now(i * 2 + j, 1))
                    for h in range(H):
                        ins = dve.tensor_scalar(decay[d][:, h, :], banks[d][3][:, h, :], sc[:, d, j, CUM, h:h + 1], 0.0, ALU.subtract, ALU.min)
                        if h < H - 1:
                            own.mark(ins)
                    ins.then_inc(diff[d].sem, 1)

                def lower(i, j, d):
                    t = i * 2 + j
                    dve.wait_ge(*masks[d].last(t))
                    dve.wait_ge(*masks[d].now(t, 1))
                    dve.wait_ge(*gram[d].now(t, 2))
                    for h in range(H):
                        ins = dve.scalar_tensor_tensor(out=lt[d][:, h, :], in0=banks[d][3][:, h, :], scalar=sc[:, d, j, BETA, h:h + 1],
                                                       in1=decay[d][:, h, :], op0=ALU.mult, op1=ALU.mult)
                        if h < H - 1:
                            own.mark(ins)
                    ins.then_inc(products[d].sem, 1)

                def attend(i, j, d):
                    dve.wait_ge(*gram[d].now(i * 2 + j, 3))
                    dve.tensor_tensor(at_[d][j][:, :, :], banks[d][3][:, :, :], decay[d][:, :, :], ALU.mult).then_inc(products[d].sem, 1)

                def first_level(t, d):
                    dve.wait_ge(*masks[d].now(t, 2))
                    dve.tensor_tensor(U[d][:, :, :], heads(ident[:, :]), M[d][:, 0], ALU.subtract).then_inc(u_first[d].sem, 1)
                    dve.wait_ge(*tmt_pe[d].now(t, 1))
                    dve.tensor_tensor(T[d][:, :, :], heads(ident[:, :]), banks[d][1][:, :, :], ALU.subtract).then_inc(t_ready[d].sem, 1)

                def chunk(i, j, last=False):
                    t = i * 2 + j
                    nxt = following(i, j)
                    if not last:
                        take_scalars(*nxt)
                    for n in range(1, LEVELS):
                        for d in range(2):
                            if n < LEVELS - 1:
                                dve.wait_ge(*t_ready[d].now(t, n))
                                dve.wait_ge(*tmt_pe[d].now(t, n + 1))
                                x = blocks(T[d][:, :, :], n, d)
                                dve.tensor_tensor(x, x, blocks(banks[d][1][:, :, :], n, d), ALU.subtract).then_inc(t_ready[d].sem, 1)
                            else:
                                dve.wait_ge(*umu_pe[d].now(t))
                                x = blocks(U[d][:, :, :], n, 1 - d)
                                dve.tensor_tensor(x, x, blocks(banks[d][2][:, :, :], n, 1 - d), ALU.subtract).then_inc(u_last[d].sem, 1)
                        if not last:
                            if n in (1, 2):
                                differences(*nxt, n - 1)
                            if n in (4, 5):
                                lower(*nxt, n - 4)
                            if n == 5:
                                attend(*nxt, 0)
                    for d in range(2):
                        dve.wait_ge(*known_pe[d].now(t))
                        dve.tensor_tensor(rest[d][:, :, :], v_tok[:, j, d], banks[d][0][:, :, :], ALU.subtract).then_inc(rest_ready[d].sem, 1)
                    if not last:
                        attend(*nxt, 1)
                    for d in range(2):
                        dve.wait_ge(*vnew_pe[d].now(t))
                        dve.tensor_tensor(vn[d][:, :, :], banks[d][1][:, :, :], wide(sc[:, d, j, BETA, :]), ALU.mult).then_inc(vnew[d].sem, 1)
                    if not last:
                        for d in range(2):
                            first_level(nxt[0] * 2 + nxt[1], d)
                    for d in range(2):
                        dve.wait_ge(*s_pe[d].now(t))
                        for h in range(H):
                            ins = dve.scalar_tensor_tensor(out=S[d][:, h, :], in0=S[d][:, h, :], scalar=sc[:, d, j, END, h:h + 1],
                                                           in1=banks[d][2][:, h, :], op0=ALU.mult, op1=ALU.add)
                            if h < H - 1:
                                own.mark(ins)
                        ins.then_inc(state_ready[d][j], 1)

                take_scalars(0, 0)
                for step in (differences, lower, attend):
                    for d in range(2):
                        step(0, 0, d)
                for d in range(2):
                    first_level(0, d)
                rounds(dve, own, chunk)

            @block.tensor
            def _(pe):
                mm = pe.matmul
                A, B, C, D = zip(*banks)

                def each_head(f):
                    for h in range(H):
                        ins = f(h)
                    return ins

                def sums(i, j, d, last_t):
                    pe.wait_ge(*scalars[d].now(i * 2 + j))
                    if last_t is not None:
                        pe.wait_ge(*o_copied[d].last(last_t))
                    each_head(lambda h: mm(D[d][:, h, :], g_wide[d][:, h, :], upto[:, d, :], start=True, stop=True)).then_inc(gram[d].sem, 1)

                def keys_keys(i, j, d):
                    pe.wait_ge(*loaded[d].now(i, j))
                    pe.wait_ge(*exps[d].now(i * 2 + j, 2))
                    each_head(lambda h: mm(D[d][:, h, :], k_ch[:, j, d, h, :], k_ch[:, j, d, h, :], start=True, stop=True)).then_inc(gram[d].sem, 1)

                def keys_queries(i, j, d):
                    pe.wait_ge(*products[d].now(i * 2 + j, 1))
                    each_head(lambda h: mm(D[d][:, h, :], k_ch[:, j, d, h, :], q_ch[:, j, d, h, :], start=True, stop=True)).then_inc(gram[d].sem, 1)

                def first_level(t, d):
                    pe.wait_ge(*masks[d].now(t, 2))
                    each_head(lambda h: pe.transpose(B[d][:, h, :], M[d][:, 0, h, :], ident[:, :])).then_inc(tmt_pe[d].sem, 1)

                def m_t(t, n, d):
                    pe.wait_ge(*masks[d].now(t, n + 2))
                    pe.wait_ge(*t_ready[d].now(t, n))
                    each_head(lambda h: mm(head_blocks(A[d][:, h, :], n, d), M[d][:, n, h, :], head_blocks(T[d][:, h, :], n, d),
                                           start=True, stop=True)).then_inc(y_pe[d].sem, 1)

                def t_turned(t, n, d):
                    pe.wait_ge(*t_ready[d].now(t, n))
                    if n > 2:
                        pe.wait_ge(*u_copied[d].now(t, n - 2))
                    each_head(lambda h: pe.transpose(C[d][:, h, :], T[d][:, h, :], ident[:, :])).then_inc(u_pe[d].sem, 1)

                def t_m_t(t, n, d):
                    pe.wait_ge(*y_copied[d].now(t, n))
                    pe.wait_ge(*(u_first[d].now(t) if n == 1 else u_copied[d].now(t, n - 1)))
                    each_head(lambda h: mm(head_blocks(B[d][:, h, :], n, d), U[d][:, h, :], head_blocks(Y[d][:, h, :], n, d),
                                           start=True, stop=True)).then_inc(tmt_pe[d].sem, 1)

                def t_m_t_turned(t, d):
                    pe.wait_ge(*y_copied[d].now(t))
                    pe.wait_ge(*u_copied[d].now(t))
                    each_head(lambda h: mm(head_blocks(C[d][:, h, :], LEVELS - 1, 1 - d), Y_last[d][:, h, :],
                                           head_blocks(U[d][:, h, :], LEVELS - 1, 1 - d), start=True, stop=True)).then_inc(umu_pe[d].sem, 1)

                def chunk(i, j, last=False):
                    t = i * 2 + j
                    nxt = following(i, j)
                    for n in range(1, LEVELS):
                        for d in range(2):
                            m_t(t, n, d)
                            if n == 2:
                                pe.wait_ge(*state_ready[d].last(i, j))
                            if n > 1:
                                t_turned(t, n, d)
                        if n < LEVELS - 1:
                            for d in range(2):
                                t_m_t(t, n, d)
                        if not last:
                            if n in (1, 2):
                                sums(*nxt, n - 1, t)
                            if n in (3, 4):
                                keys_keys(*nxt, n - 3)
                            if n in (5, 6):
                                keys_queries(*nxt, n - 5)
                    for d in range(2):
                        t_m_t_turned(t, d)
                        pe.wait_ge(*grown[d].now(t))
                        each_head(lambda h: mm(A[d][:, h, :], kg[d][j][:, h, :], S[d][:, h, :], start=True, stop=True)).then_inc(known_pe[d].sem, 1)
                    for d in range(2):
                        pe.wait_ge(*u_last[d].now(t))
                        pe.wait_ge(*rest_ready[d].now(t))
                        each_head(lambda h: mm(B[d][:, h, :], U[d][:, h, :], rest[d][:, h, :], start=True, stop=True)).then_inc(vnew_pe[d].sem, 1)
                    for d in range(2):
                        pe.wait_ge(*vnew[d].now(t))
                        if not last:
                            first_level(nxt[0] * 2 + nxt[1], d)
                        pe.wait_ge(*k_tail[d].now(t))
                        pe.wait_ge(*(products[d].now(t) if last else products[d].now(nxt[0] * 2 + nxt[1])))
                        for h in range(H):
                            mm(D[d][:, h, :], qd[d][j][:, h, :], S[d][:, h, :], start=True, stop=False)
                            ins = mm(D[d][:, h, :], at_[d][j][:, h, :], vn[d][:, h, :], start=False, stop=True)
                        ins.then_inc(o_pe[d].sem, 1)
                        each_head(lambda h: mm(C[d][:, h, :], kt[d][j][:, h, :], vn[d][:, h, :], start=True, stop=True)).then_inc(s_pe[d].sem, 1)

                pe.wait_ge(cleared, 1)
                for d in range(2):
                    sums(0, 0, d, None)
                for d in range(2):
                    keys_keys(0, 0, d)
                for d in range(2):
                    keys_queries(0, 0, d)
                for d in range(2):
                    first_level(0, d)
                rounds(pe, None, chunk)


def attention(nc, top, dr, w_out):
    H, K = ATT_HEADS, KV_HEADS
    C = SEQ // 512
    SCALE = ATT_D ** -0.5
    VW = ATT_D + 1
    HALF = ATT_D
    with ExitStack() as ctx:
        sb = lambda n, s, d=F32: ctx.enter_context(nc.sbuf_tensor(n, s, d))
        ps = lambda n, s, d=F32: ctx.enter_context(nc.psum_tensor(n, s, d))
        sem = lambda n: top.semaphore(n)
        ident = sb("ident_d", [P, P])
        v_in = sb("v_in", [P, TILES, K, VW])
        kT = sb("kT", [P, K, 2, SEQ], F32R)
        sc = ps("scores", [P, C, 512])
        consts_in, ones_set = sem("d_consts"), sem("d_ones")
        with ExitStack() as pre:
            k_in = pre.enter_context(nc.sbuf_tensor("k_in", [P, TILES, K, 2, ATT_D], F32))
            q_in = pre.enter_context(nc.sbuf_tensor("q_in", [P, 2, TILES, 2, ATT_D], F32))
            first = pre.enter_context(nc.sbuf_tensor("q_first", [P, 2, SEQ], F32R))
            q_parts = pre.enter_context(nc.sbuf_tensor("q_parts", [P, 2, SEQ], F32R))
            sc2 = pre.enter_context(nc.psum_tensor("turned_q", [P, C, 512], F32))
            k_turned, k_first, k_ready, q_turned = (sem(n) for n in ("d_k_turned", "d_k_first", "d_k_ready", "d_q_turned"))
            q_first, q_ready = sem("d_q_first"), sem("d_q_ready")
            q_in_done, q_stored = [sem(f"d_q_in{j}") for j in range(2)], [sem(f"d_q_stored{j}") for j in range(2)]
            banks = lambda x: x.rearrange("p (c n) -> p c n", c=C)

            with nc.Block() as block:
                @block.sync
                def _(sp):
                    sp.dma_start(ident[:, :], dr["c_ident"]).then_inc(consts_in, 16)
                    k = dr["qk"][:, H * ATT_D:].rearrange("(t p) (g d) -> p t g d", p=P, g=K)
                    for half in range(2):
                        for g in range(K):
                            sp.dma_start(k_in[:, :, g, half, :], k[:, :, g, :]).then_inc(consts_in, 16)
                    for g in range(K):
                        sp.dma_start(v_in[:, :, g, 0:ATT_D], dr["v"].rearrange("(t p) (g d) -> p t g d", p=P, g=K)[:, :, g, :]).then_inc(consts_in, 16)

                    def load(h):
                        if h >= 2:
                            sp.wait_ge(q_turned, h - 1)
                        for half in range(2):
                            sp.dma_start(q_in[:, h % 2, :, half, :], dr["qk"][:, h * ATT_D:(h + 1) * ATT_D].rearrange("(t p) c -> p t c", p=P)).then_inc(q_in_done[h % 2], 16)

                    load(0)
                    for h in range(H):
                        if h + 1 < H:
                            load(h + 1)
                        sp.wait_ge(q_ready, h + 1)
                        sp.dma_start(dr["qT"].rearrange("t p x c -> p x t c")[:, h], q_parts[:, h % 2, :].bitcast(F32).rearrange("p (t c) -> p t c", c=P)).then_inc(q_stored[h % 2], 16)
                    for j in range(2):
                        sp.wait_ge(q_stored[j], 16 * (H // 2))

                @block.gpsimd
                def _(pool):
                    pool.memset(v_in[:, :, :, ATT_D:], 1.0).then_inc(ones_set, 1)

                @block.tensor
                def _(pe):
                    pe.wait_ge(consts_in, 16 * 7)
                    for g in range(K):
                        if g:
                            pe.wait_ge(k_ready, g)
                        for t in range(TILES):
                            ins = pe.transpose(sc[:, t // 4, (t % 4) * P:(t % 4 + 1) * P], k_in[:, t, g].rearrange("p a d -> p (a d)"), ident[:, :])
                        ins.then_inc(k_turned, 1)
                    for h in range(H):
                        pe.wait_ge(q_in_done[h % 2], 32 * (h // 2 + 1))
                        if h:
                            pe.wait_ge(q_ready, h)
                        for t in range(TILES):
                            ins = pe.transpose(sc2[:, t // 4, (t % 4) * P:(t % 4 + 1) * P], q_in[:, h % 2, t].rearrange("p a d -> p (a d)"), ident[:, :])
                        ins.then_inc(q_turned, 1)

                @block.scalar
                def _(act):
                    for g in range(K):
                        act.wait_ge(k_turned, g + 1)
                        act.activation(banks(kT[:, g, 0, :]), sc[:, :, :], ACT.Copy).then_inc(k_first, 1)
                    for h in range(H):
                        act.wait_ge(q_turned, h + 1)
                        if h >= 2:
                            act.wait_ge(q_stored[h % 2], 16 * (h // 2))
                        act.activation(banks(first[:, h % 2, :]), sc2[:, :, :], ACT.Copy).then_inc(q_first, 1)

                @block.vector
                def _(dve):
                    for g in range(K):
                        dve.wait_ge(k_first, g + 1)
                        dve.tensor_tensor(banks(kT[:, g, 1, :]), sc[:, :, :], banks(kT[:, g, 0, :].bitcast(F32)), ALU.subtract).then_inc(k_ready, 1)
                    for h in range(H):
                        dve.wait_ge(q_first, h + 1)
                        if h >= 2:
                            dve.wait_ge(q_stored[h % 2], 16 * (h // 2))
                        f = first[:, h % 2, :].bitcast(F32)
                        dve.tensor_copy(q_parts[0:HALF, h % 2, :], f[0:HALF, :])
                        dve.tensor_tensor(banks(q_parts[HALF:P, h % 2, :]), sc2[HALF:P, :, :], banks(f[HALF:P, :]), ALU.subtract).then_inc(q_ready, 1)

        qT = sb("qT_tile", [P, 2, H, P], F32R)
        TB = 2
        BY_ACT = (0, 1)
        peak = sb("row_max", [P, 2, C])
        bias = sb("minus_max", [P, 2, 2])
        prob = sb("probs", [P, 2, SEQ])
        pT = sb("probs_T", [P, C, 4, P])
        over = sb("one_over_sum", [P, 2, 1])
        o_out = sb("o_tile", [P, 2, H * ATT_D])
        tr = ps("probs_turned", [P, TB, 4, P])
        po = ps("pv", [P, 2, 512])
        q_loaded, stored = Event(top, "d_q_loaded", 16), Event(top, "d_stored", 16)
        ct = lambda n, per=1: Count(top, f"d_{n}", per)
        scored, peak_ready, exped, turned = ct("scored", C), ct("peak_ready"), ct("exped", C), ct("turned", C)
        by_act, by_dve = ct("copied_act", len(BY_ACT)), ct("copied_dve", C - len(BY_ACT))
        weighed = ct("weighed", C)
        finished = (sem("d_finished_even"), sem("d_finished_odd"))
        w_out_in = sem("d_w_out_in")
        own_dve, blank_set = sem("d_own_dve"), sem("d_blank_set")

        def copied(n, c):
            return by_act.now(n, c + 1) if c in BY_ACT else by_dve.now(n, c - len(BY_ACT) + 1)

        def before(i, j, h):
            return (i * 2 + j) * (H // 2) + h // 2

        def steps(i, j, last):
            for h in range(H):
                nxt = (h + 1, j) if h < H - 1 else (0, 1 - j)
                yield (i * 2 + j) * H + h, h, None if last and h == H - 1 else nxt

        with nc.Block() as block:
            @block.sync
            def _(sp):
                def load(i, j):
                    sp.dma_start(qT[:, j, :, :].bitcast(F32), dr["qT"][bass.ds(i * 2 + j, 1), :, :, :].rearrange("a p x c -> (a p) x c")).then_inc(q_loaded[j], 16)

                def tile(i, j, last=False):
                    if not last:
                        load(*following(i, j))
                    sp.wait_ge(finished[1], (i * 2 + j + 1) * (H // 2) + 1)
                    sp.dma_start(tile_rows(dr["o_att"], i * 2 + j), o_out[:, j, :]).then_inc(stored[j], 16)

                load(0, 0)
                sp.dma_start(w_out[:, :, :], dr["w_out"].rearrange("(k p) n -> p k n", p=P)).then_inc(w_out_in, 16)
                rounds(sp, None, tile)
                sp.wait_ge(w_out_in, 16)
                for j in range(2):
                    sp.wait_ge(stored[j], 16 * (TILES // 2))

            @block.tensor
            def _(pe):
                def score(n, h, j, c, free):
                    if free is not None:
                        pe.wait_ge(exped.sem, free)
                    for part in range(2):
                        ins = pe.matmul(sc[:, c, :], qT[:, j, h, :], kT[:, h // GROUP, part, c * 512:(c + 1) * 512], start=part == 0, stop=part == 1)
                    ins.then_inc(scored.sem, 1)

                def turn(n, h, c):
                    pe.wait_ge(*(copied(n, c - TB) if c >= TB else by_dve.last(n)))
                    pe.wait_ge(*exped.now(n, c + 1))
                    for q in range(4):
                        ins = pe.transpose(tr[:, c % TB, q, :], prob[:, h % 2, (4 * c + q) * P:(4 * c + q + 1) * P], ident[:, :])
                    ins.then_inc(turned.sem, 1)

                def weigh(i, j, n, h, c):
                    pe.wait_ge(*copied(n, c))
                    if c == 0:
                        pe.wait_ge(finished[h % 2], before(i, j, h) + h % 2)
                    for q in range(4):
                        t = 4 * c + q
                        ins = pe.matmul(po[:, h % 2, 0:VW], pT[:, c, q, :], v_in[:, t, h // GROUP, :], start=t == 0, stop=t == TILES - 1)
                    ins.then_inc(weighed.sem, 1)

                def tile(i, j, last=False):
                    for n, h, nxt in steps(i, j, last):
                        if nxt and nxt[0] == 0:
                            pe.wait_ge(*q_loaded.now(*following(i, j)))
                        for c in range(C):
                            if nxt:
                                score(n + 1, *nxt, c, n * C + c + 1)
                            if c < TB:
                                turn(n, h, c)
                        turn(n, h, 2)
                        weigh(i, j, n, h, 0)
                        turn(n, h, 3)
                        for c in range(1, C):
                            weigh(i, j, n, h, c)

                pe.wait_ge(q_loaded[0], 16)
                for c in range(C):
                    score(0, 0, 0, c, None)
                rounds(pe, None, tile)

            @block.vector
            def _(dve):
                own = Chain(dve, own_dve, 2 * H * (C + 2))

                def peaks(n, h):
                    p = h % 2
                    for c in range(C):
                        dve.wait_ge(*scored.now(n, c + 1))
                        own.mark(dve.tensor_reduce(peak[:, p, c:c + 1], sc[:, c, :], AX.X, ALU.max))
                    own.wait()
                    own.link(dve.tensor_reduce(bias[:, p, 0:1], peak[:, p, :], AX.X, ALU.max))
                    dve.tensor_scalar(bias[:, p, 1:2], bias[:, p, 0:1], -SCALE, None, ALU.mult).then_inc(peak_ready.sem, 1)

                def finish(n1, h, j, i):
                    dve.wait_ge(*weighed.last(n1))
                    own.link(dve.reciprocal(over[:, h % 2], po[:, h % 2, ATT_D:VW]))
                    if h == 0:
                        dve.wait_ge(*stored.before_last(i, j))
                    dve.tensor_scalar(o_out[:, j, h * ATT_D:(h + 1) * ATT_D], po[:, h % 2, 0:ATT_D], over[:, h % 2], None, ALU.mult).then_inc(finished[h % 2], 1)

                def tile(i, j, last=False):
                    for n, h, nxt in steps(i, j, last):
                        if nxt:
                            peaks(n + 1, nxt[0])
                        finish(n, (h - 1) % H, j if h else 1 - j, i)
                        for c in range(len(BY_ACT), C):
                            dve.wait_ge(*turned.now(n, c + 1))
                            dve.wait_ge(*weighed.last(n))
                            dve.tensor_copy(pT[:, c, :, :], tr[:, c % TB, :, :]).then_inc(by_dve.sem, 1)

                dve.memset(po[:, 1, 0:VW], 1.0).then_inc(blank_set, 1)
                dve.wait_ge(blank_set, 1)
                peaks(0, 0)
                rounds(dve, own, tile)
                finish(TILES * H, H - 1, 1, TILES // 2 - 1)

            @block.scalar
            def _(act):
                def exps(n, h, quarters, free):
                    act.wait_ge(*peak_ready.now(n))
                    if free is not None:
                        act.wait_ge(turned.sem, free)
                    for c in quarters:
                        act.activation(prob[:, h % 2, c * 512:(c + 1) * 512], sc[:, c, :], ACT.Exp, bias=bias[:, h % 2, 1:2],
                                       scale=SCALE).then_inc(exped.sem, 1)

                def tile(i, j, last=False):
                    for n, h, nxt in steps(i, j, last):
                        for c in BY_ACT:
                            act.wait_ge(*turned.now(n, c + 1))
                            act.wait_ge(*weighed.last(n))
                            act.activation(pT[:, c, :, :], tr[:, c % TB, :, :], ACT.Copy).then_inc(by_act.sem, 1)
                        if nxt:
                            exps(n + 1, nxt[0], range(C), n * C)

                exps(0, 0, range(C), None)
                rounds(act, None, tile)


def mix_out(nc, top, dr, logits, w_out, load_experts):
    H, W = GDN_HEADS, GDN_W
    NL = N_GROUPS + N_EXPERTS
    with ExitStack() as ctx:
        sb = lambda n, s, d=F32: ctx.enter_context(nc.sbuf_tensor(n, s, d))
        ps = lambda n, s, d=F32: ctx.enter_context(nc.psum_tensor(n, s, d))
        sem = lambda n: top.semaphore(n)
        ev = lambda n, per=1: Event(top, f"e_{n}", per)
        ident, eps = sb("ident_e", [P, P]), sb("eps_e", [P, 1])
        w_rt = sb("w_router", [P, KD, NL])
        nw = sb("norm_ffn_rows", [P, D_MODEL])
        gw = sb("gdn_norm_rows", [P, GDN_D])
        o_in = sb("o_both", [P, 2, 2, W])
        z_in = sb("z_in", [P, 2, W])
        a_in = sb("att_in", [P, 2, W])
        x_in = sb("x_in_e", [P, 2, D_MODEL])
        gn = sb("gdn_out", [P, 2, W])
        gsq = sb("gdn_squares", [P, W])
        gst = sb("gdn_stats", [P, 3, H])
        catT = sb("mixed_T", [P, 2, KD, P])
        x1 = sb("x1_tile", [P, 2, D_MODEL])
        sq = sb("squares_e", [P, D_MODEL])
        st = sb("stats_e", [P, 2, 3])
        h2 = sb("h2_tile", [P, 2, D_MODEL])
        hT = sb("h2_T", [P, KD, P])
        pc, po, ph, pl = ps("cat_turned", [P, KD, P]), ps("out_proj", [P, 2, 512]), ps("h2_turned", [P, KD, P]), ps("router", [P, NL])
        consts_in, late_in, eps_set, own_dve = sem("e_consts"), sem("e_late"), sem("e_eps"), sem("e_own_dve")
        o_loaded, x_loaded = ev("o_loaded", 64), ev("x_loaded", 16)
        g_sums, g_rms, g_ready, cat_turned, cat_ready = (ev(n) for n in ("g_sums", "g_rms", "g_ready", "cat_turned", "cat_ready"))
        mixed, x1_ready = ev("mixed", 2), ev("x1_ready", 2)
        x1_sum, x1_rms, h2_ready = (ev(n) for n in ("x1_sum", "x1_rms", "h2_ready"))
        h_turned, hT_ready, routed, kept = (ev(n) for n in ("h_turned", "hT_ready", "routed", "kept"))
        x1_stored, h2_stored = ev("x1_stored", 16), ev("h2_stored", 16)

        with nc.Block() as block:
            @block.sync
            def _(sp):
                def consts(dst, src):
                    sp.dma_start(dst, src).then_inc(consts_in, 16)

                def load(i, j):
                    t = i * 2 + j
                    sp.wait_ge(*g_ready.before_last(i, j))
                    sp.wait_ge(*cat_turned.before_last(i, j))
                    for d in range(2):
                        sp.dma_start(o_in[:, j, d, :], tile_rows(dr["o_gdn"][d], t)).then_inc(o_loaded[j], 16)
                    sp.dma_start(z_in[:, j, :], tile_rows(dr["z"], t)).then_inc(o_loaded[j], 16)
                    sp.dma_start(a_in[:, j, :], tile_rows(dr["o_att"], t)).then_inc(o_loaded[j], 16)
                    sp.wait_ge(*x1_ready.before_last(i, j))
                    sp.dma_start(x_in[:, j, :], tile_rows(dr["x"], t)).then_inc(x_loaded[j], 16)

                consts(ident[:, :], dr["c_ident"])
                consts(gw[:, :], dr["gdn_norm_w"].unsqueeze(0).broadcast_to([P, GDN_D]))
                load(0, 0)
                load(0, 1)
                for dst, src in ((nw[:, :], dr["norm_ffn_w"].unsqueeze(0).broadcast_to([P, D_MODEL])),
                                 (w_rt[:, :, 0:N_GROUPS], dr["w_router_group"].rearrange("(k p) n -> p k n", p=P)),
                                 (w_rt[:, :, N_GROUPS:], dr["w_router_expert"].rearrange("(k p) n -> p k n", p=P))):
                    sp.dma_start(dst, src, allow_slow_non_contiguous=True).then_inc(late_in, 16)
                load_experts(sp)

                def tile(i, j, last=False):
                    t = i * 2 + j
                    sp.wait_ge(*x1_ready.now(i, j))
                    sp.dma_start(tile_rows(dr["x1"], t), x1[:, j, :]).then_inc(x1_stored[j], 16)
                    if not isinstance(i, int):
                        load(i + 1, j)
                    sp.wait_ge(*h2_ready.now(i, j))
                    sp.dma_start(tile_rows(dr["h2"], t), h2[:, j, :]).then_inc(h2_stored[j], 16)

                rounds(sp, None, tile)
                for j in range(2):
                    sp.wait_ge(x1_stored[j], 16 * (TILES // 2))
                    sp.wait_ge(h2_stored[j], 16 * (TILES // 2))

            @block.scalar
            def _(act):
                act.wait_ge(eps_set, 1)

                def head_rms(i, j):
                    act.wait_ge(*g_sums.now(i, j))
                    act.activation(gst[:, 1, :], gst[:, 0, :], ACT.Sqrt, bias=eps[:, :], scale=1.0 / GDN_D).then_inc(g_rms[j], 1)

                def copy_cat(i, j):
                    act.wait_ge(*cat_turned.now(i, j))
                    act.wait_ge(*mixed.before_last(i, j))
                    act.activation(catT[:, j, :, :], pc[:, :, :], ACT.Copy).then_inc(cat_ready[j], 1)

                def tile(i, j, last=False):
                    t = i * 2 + j
                    act.wait_ge(*x1_ready.now(i, j))
                    act.wait_ge(*h2_ready.before_last(i, j))
                    act.activation(sq[:, :], x1[:, j, :], ACT.Square, accum_out=st[:, j, 0:1]).then_inc(x1_sum[j], 1)
                    act.wait_ge(*x1_sum.now(i, j))
                    act.activation(st[:, j, 1:2], st[:, j, 0:1], ACT.Sqrt, bias=eps[:, :], scale=1.0 / D_MODEL).then_inc(x1_rms[j], 1)
                    if not isinstance(i, int):
                        head_rms(i + 1, j)
                    act.wait_ge(*h_turned.now(i, j))
                    act.wait_ge(*routed.last(i, j))
                    act.activation(hT[:, :, :], ph[:, :, :], ACT.Copy).then_inc(hT_ready[j], 1)
                    if not isinstance(i, int):
                        copy_cat(i + 1, j)
                    act.wait_ge(*routed.now(i, j))
                    act.activation(at(logits, t), pl[:, :], ACT.Copy).then_inc(kept[j], 1)

                head_rms(0, 0)
                head_rms(0, 1)
                copy_cat(0, 0)
                copy_cat(0, 1)
                rounds(act, None, tile)

            @block.vector
            def _(dve):
                own = Chain(dve, own_dve, 2 * 6)
                dve.memset(eps[:, :], EPS).then_inc(eps_set, 1)

                def gdn_out(i, j):
                    heads = lambda x: x.rearrange("p (h d) -> p h d", h=H)
                    o = o_in[:, j, 0, :]
                    dve.wait_ge(*o_loaded.now(i, j))
                    own.link(dve.tensor_tensor(o, o, o_in[:, j, 1, :], ALU.add))
                    own.link(dve.tensor_tensor(gsq[:, :], o, o, ALU.mult))
                    dve.tensor_reduce(gst[:, 0, :], heads(gsq[:, :]), AX.X, ALU.add).then_inc(g_sums[j], 1)
                    own.mark(dve.tensor_tensor(heads(z_in[:, j, :]), heads(z_in[:, j, :]), gw[:, :].unsqueeze(1).broadcast_to([P, H, GDN_D]), ALU.mult))
                    dve.wait_ge(*g_rms.now(i, j))
                    own.link(dve.reciprocal(gst[:, 2, :], gst[:, 1, :]))
                    own.link(dve.tensor_tensor(heads(o), heads(o), gst[:, 2, :].unsqueeze(2).broadcast_to([P, H, GDN_D]), ALU.mult))
                    dve.wait_ge(*cat_turned.before_last(i, j))
                    dve.tensor_tensor(gn[:, j, :], o, z_in[:, j, :], ALU.mult).then_inc(g_ready[j], 1)

                def tile(i, j, last=False):
                    dve.wait_ge(*x_loaded.now(i, j))
                    dve.wait_ge(*x1_stored.before_last(i, j))
                    for half in range(2):
                        dve.wait_ge(*mixed.now(i, j, half + 1))
                        part = slice(half * 512, (half + 1) * 512)
                        dve.tensor_tensor(x1[:, j, part], x_in[:, j, part], po[:, half, :], ALU.add).then_inc(x1_ready[j], 1)
                    dve.wait_ge(*x1_rms.now(i, j))
                    own.link(dve.reciprocal(st[:, j, 2:3], st[:, j, 1:2]))
                    dve.wait_ge(*h2_stored.before_last(i, j))
                    dve.wait_ge(*h_turned.before_last(i, j))
                    dve.scalar_tensor_tensor(out=h2[:, j, :], in0=x1[:, j, :], scalar=st[:, j, 2:3], in1=nw[:, :], op0=ALU.mult, op1=ALU.mult).then_inc(h2_ready[j], 1)
                    if not isinstance(i, int):
                        gdn_out(i + 1, j)

                dve.wait_ge(consts_in, 32)
                gdn_out(0, 0)
                gdn_out(0, 1)
                dve.wait_ge(late_in, 48)
                rounds(dve, own, tile)

            @block.tensor
            def _(pe):
                pe.wait_ge(consts_in, 32)

                def turn_cat(i, j):
                    pe.wait_ge(*g_ready.now(i, j))
                    pe.wait_ge(*o_loaded.now(i, j))
                    pe.wait_ge(*cat_ready.last(i, j))
                    for k in range(KD):
                        src = gn[:, j, k * P:(k + 1) * P] if k < H else a_in[:, j, (k - H) * P:(k - H + 1) * P]
                        ins = pe.transpose(pc[:, k, :], src, ident[:, :])
                    ins.then_inc(cat_turned[j], 1)

                def mix(i, j, half, prev=None):
                    if half == 0:
                        pe.wait_ge(*cat_ready.now(i, j))
                    if prev:
                        pe.wait_ge(*x1_ready.now(*prev, half + 1))
                    for k in range(KD):
                        ins = pe.matmul(po[:, half, :], catT[:, j, k, :], w_out[:, k, half * 512:(half + 1) * 512], start=k == 0, stop=k == KD - 1)
                    ins.then_inc(mixed[j], 1)

                def tile(i, j, last=False):
                    nxt = following(i, j)
                    if not last:
                        mix(*nxt, 0, (i, j))
                    pe.wait_ge(*h2_ready.now(i, j))
                    pe.wait_ge(*hT_ready.last(i, j))
                    for k in range(KD):
                        ins = pe.transpose(ph[:, k, :], h2[:, j, k * P:(k + 1) * P], ident[:, :])
                    ins.then_inc(h_turned[j], 1)
                    if not last:
                        mix(*nxt, 1, (i, j))
                    if not isinstance(i, int):
                        turn_cat(i + 1, j)
                    pe.wait_ge(*hT_ready.now(i, j))
                    pe.wait_ge(*kept.last(i, j))
                    for k in range(KD):
                        ins = pe.matmul(pl[:, :], hT[:, k, :], w_rt[:, k, :], start=k == 0, stop=k == KD - 1)
                    ins.then_inc(routed[j], 1)

                turn_cat(0, 0)
                turn_cat(0, 1)
                mix(0, 0, 0)
                mix(0, 0, 1)
                pe.wait_ge(late_in, 48)
                rounds(pe, None, tile)


BT_SLOT, BT_EVEN, BT_ODD, BT_UPTO = range(4)
BT_ROWS = 4
W_DMAS = 3 * 16


def route(nc, top, dr, logits, dest, gate, table):
    G, E, N = N_GROUPS, PER_GROUP, N_EXPERTS
    BIG = 1e30
    with ExitStack() as ctx:
        sb = lambda n, s, d=F32: ctx.enter_context(nc.sbuf_tensor(n, s, d))
        ps = lambda n, s, d=F32: ctx.enter_context(nc.psum_tensor(n, s, d))
        sem = lambda n: top.semaphore(n)
        iota, before, ones = sb("iota", [P, 64]), sb("before", [P, P]), sb("ones_f", [P, P])
        tokens = sb("token_ids", [P, TILES], I32)
        wide = [P, TILES, E]
        group_d, group_e, group_1 = sb("group_diff", [P, TILES, G]), sb("group_exp", [P, TILES, G]), sb("group_onehot", [P, TILES, G])
        group_p = sb("group_prob", [P, TILES])
        picked = sb("picked_products", [P, TILES, G, E])
        fine, fine_d, fine_e = sb("fine", wide), sb("fine_diff", wide), sb("fine_exp", wide)
        hot = [sb(f"expert_onehot{k}", wide) for k in range(TOP_K)]
        top_v = sb("top_values", [P, 4, TILES])
        col = sb("columns_f", [P, 4, TILES])
        work = sb("index_work", wide)
        OH = [sb(f"assigned{k}", [P, TILES, N]) for k in range(TOP_K)]
        cnt, pos = sb("assigned_both", [P, TILES, N]), sb("positions", [P, TILES, N])
        base = sb("tile_base", [P, TILES + 1, N])
        nb, nbi, incl = sb("expert_blocks", [P, N]), sb("expert_blocks_int", [P, N], I32), sb("blocks_upto", [P, N])
        start = sb("first_slot", [P, N])
        cmp = sb("block_compare", [1, N_BLOCKS, N])
        eb, ebi = sb("block_expert", [1, N_BLOCKS]), sb("block_expert_int", [1, 2, N_BLOCKS], I32)
        rank, tot = ps("rank_in_tile", [P, TILES, N]), ps("tile_totals", [P, TILES, N])
        consts_in, cleared, chain, act_done, counted = sem("f_consts"), sem("f_cleared"), sem("f_dve"), sem("f_act"), sem("f_counted")
        marks = {n: sem(f"f_{n}") for n in ("group_diff", "fine_diff", "counts", "dest")}
        scattered = [sem(f"f_scattered{k}") for k in range(2)]

        with nc.Block() as block:
            @block.sync
            def _(sp):
                for dst, src in ((iota[:, :], "c_iota"), (before[:, :], "c_before"), (ones[:, :], "c_ones"), (tokens[:, :], "c_tokens")):
                    sp.dma_start(dst, dr[src]).then_inc(consts_in, 16)
                sp.dma_start(dr["slot_token"], dr["c_slot0"]).then_inc(cleared, 16)

            @block.vector
            def _(dve):
                own = Chain(dve, chain)
                link = own.link
                tt, ts = dve.tensor_tensor, dve.tensor_scalar
                along = lambda x, n: x.unsqueeze(2).broadcast_to([P, TILES, n])
                numbers = lambda n: iota[:, 0:n].unsqueeze(1).broadcast_to([P, TILES, n])

                def first_hot(out, hits, n, c):
                    w = work[:, :, 0:n]
                    link(ts(w, numbers(n), -64.0, None, ALU.add))
                    link(tt(w, w, hits, ALU.mult))
                    link(dve.tensor_reduce(col[:, c, :], w, AX.X, ALU.min))
                    link(ts(w, numbers(n), -64.0, None, ALU.add))
                    link(tt(out, w, along(col[:, c, :], n), ALU.is_equal))

                dve.wait_ge(consts_in, 64)
                gl = logits[:, :, 0:G]
                link(dve.tensor_reduce(top_v[:, 0, :], gl, AX.X, ALU.max))
                tt(group_d[:, :, :], gl, along(top_v[:, 0, :], G), ALU.subtract).then_inc(marks["group_diff"], 1)
                dve.wait_ge(marks["group_diff"], 1)
                link(ts(group_1[:, :, :], group_d[:, :, :], 0.0, None, ALU.is_ge))
                first_hot(group_1[:, :, :], group_1[:, :, :], G, 0)
                link(tt(picked[:, :, :, :], logits[:, :, G:].rearrange("p t (g e) -> p t g e", g=G),
                        group_1[:, :, :].unsqueeze(3).broadcast_to([P, TILES, G, E]), ALU.mult))
                link(dve.tensor_reduce(fine[:, :, :], picked[:, :, :, :].rearrange("p t g e -> p t e g"), AX.X, ALU.add))
                link(dve.tensor_reduce(top_v[:, 1, :], fine[:, :, :], AX.X, ALU.max))
                tt(fine_d[:, :, :], fine[:, :, :], along(top_v[:, 1, :], E), ALU.subtract).then_inc(marks["fine_diff"], 1)
                dve.wait_ge(marks["fine_diff"], 1)
                link(ts(hot[0][:, :, :], fine_d[:, :, :], 0.0, None, ALU.is_ge))
                first_hot(hot[0][:, :, :], hot[0][:, :, :], E, 1)
                link(dve.scalar_tensor_tensor(out=fine[:, :, :], in0=hot[0][:, :, :], scalar=-BIG, in1=fine_d[:, :, :], op0=ALU.mult, op1=ALU.add))
                dve.tensor_reduce(top_v[:, 2, :], fine[:, :, :], AX.X, ALU.max).then_inc(marks["fine_diff"], 1)
                dve.wait_ge(marks["fine_diff"], 2)
                link(tt(hot[1][:, :, :], fine[:, :, :], along(top_v[:, 2, :], E), ALU.is_equal))
                first_hot(hot[1][:, :, :], hot[1][:, :, :], E, 2)
                for k in range(TOP_K):
                    own.mark(tt(OH[k][:, :, :].rearrange("p t (g e) -> p t g e", g=G), group_1[:, :, :].unsqueeze(3).broadcast_to([P, TILES, G, E]),
                                hot[k][:, :, :].unsqueeze(2).broadcast_to([P, TILES, G, E]), ALU.mult))
                own.wait()
                tt(cnt[:, :, :], OH[0][:, :, :], OH[1][:, :, :], ALU.add).then_inc(marks["counts"], 1)
                dve.wait_ge(act_done, 3)
                own.mark(dve.tensor_reduce(col[:, 0, :], group_e[:, :, :], AX.X, ALU.add))
                link(dve.tensor_reduce(col[:, 1, :], fine_e[:, :, :], AX.X, ALU.add))
                link(dve.reciprocal(col[:, 0:2, :], col[:, 0:2, :]))
                link(tt(col[:, 2, :], top_v[:, 3, :], col[:, 1, :], ALU.mult))
                link(tt(col[:, 3, :], col[:, 1, :], col[:, 2, :], ALU.add))
                link(dve.reciprocal(col[:, 3, :], col[:, 3, :]))
                link(tt(col[:, 3, :], col[:, 3, :], col[:, 0, :], ALU.mult))
                own.mark(tt(gate[:, 0, :], col[:, 1, :], col[:, 3, :], ALU.mult))
                own.mark(tt(gate[:, 1, :], col[:, 2, :], col[:, 3, :], ALU.mult))
                dve.wait_ge(counted, 1)
                link(dve.memset(base[:, 0, :], 0.0))
                for t in range(TILES):
                    link(tt(base[:, t + 1, :], base[:, t, :], tot[:, t, :], ALU.add))
                link(ts(nb[:, :], base[:, TILES, :], float(P - 1), None, ALU.add))
                link(dve.tensor_copy(nbi[:, :], nb[:, :]))
                link(ts(nbi[:, :], nbi[:, :], 7, None, ALU.logical_shift_right))
                link(dve.tensor_copy(nb[:, :], nbi[:, :]))
                link(dve.tensor_tensor_scan(incl[:, :], ones[:, 0:N], nb[:, :], 0.0, ALU.mult, ALU.add))
                link(tt(start[:, :], incl[:, :], nb[:, :], ALU.subtract))
                link(ts(start[:, :], start[:, :], float(P), None, ALU.mult))
                link(tt(pos[:, :, :], rank[:, :, :], base[:, 0:TILES, :], ALU.add))
                link(tt(pos[:, :, :], pos[:, :, :], start[:, :].unsqueeze(1).broadcast_to([P, TILES, N]), ALU.add))
                for k in range(TOP_K):
                    link(tt(OH[k][:, :, :], OH[k][:, :, :], pos[:, :, :], ALU.mult))
                    link(dve.tensor_reduce(col[:, k, :], OH[k][:, :, :], AX.X, ALU.add))
                dve.tensor_copy(dest[:, :, :], col[:, 0:TOP_K, :]).then_inc(marks["dest"], 1)
                link(tt(cmp[:, :, :], incl[0:1, :].unsqueeze(1).broadcast_to([1, N_BLOCKS, N]),
                        iota[0:1, 0:N_BLOCKS].unsqueeze(2).broadcast_to([1, N_BLOCKS, N]), ALU.is_le))
                link(dve.tensor_reduce(eb[:, :], cmp[:, :, :], AX.X, ALU.add))
                link(ts(eb[:, :], eb[:, :], float(N - 1), None, ALU.min))
                link(dve.tensor_copy(ebi[:, 0, :], eb[:, :]))
                own.mark(ts(table[:, BT_SLOT, :], ebi[:, 0, :], 1, None, ALU.bitwise_and))
                link(ts(ebi[:, 1, :], ebi[:, 0, :], 1, None, ALU.logical_shift_right))
                link(dve.tensor_copy(eb[:, :], ebi[:, 1, :]))
                link(ts(eb[:, :], eb[:, :], float(W_DMAS), float(W_DMAS), ALU.mult, ALU.add))
                link(dve.tensor_copy(table[:, BT_EVEN, :], eb[:, :]))
                own.mark(dve.tensor_copy(cmp[:, 0, :], ebi[:, 0, 0:N]))
                link(dve.tensor_copy(cmp[:, 1, :], ebi[:, 0, N:2 * N]))
                odd = cmp[:, 0:2, :].rearrange("o a b -> o (a b)")
                link(ts(odd, odd, 1.0, None, ALU.add))
                link(dve.tensor_copy(ebi[:, 1, :], odd))
                link(ts(ebi[:, 1, :], ebi[:, 1, :], 1, None, ALU.logical_shift_right))
                link(dve.tensor_copy(odd, ebi[:, 1, :]))
                link(ts(odd, odd, float(W_DMAS), None, ALU.mult))
                link(dve.tensor_copy(table[:, BT_ODD, :], odd))
                link(dve.tensor_copy(table[:, BT_UPTO, 0:N], incl[0:1, :]))

            @block.scalar
            def _(act):
                act.wait_ge(marks["group_diff"], 1)
                act.activation(group_e[:, :, :], group_d[:, :, :], ACT.Exp).then_inc(act_done, 1)
                act.wait_ge(marks["fine_diff"], 1)
                act.activation(fine_e[:, :, :], fine_d[:, :, :], ACT.Exp).then_inc(act_done, 1)
                act.wait_ge(marks["fine_diff"], 2)
                act.activation(top_v[:, 3, :], top_v[:, 2, :], ACT.Exp).then_inc(act_done, 1)

            @block.tensor
            def _(pe):
                pe.wait_ge(marks["counts"], 1)
                rows = cnt[:, :, :].rearrange("p t e -> p (t e)")
                pe.matmul(rank[:, :, :].rearrange("p t e -> p (t e)"), before[:, :], rows, start=True, stop=True)
                pe.matmul(tot[:, :, :].rearrange("p t e -> p (t e)"), ones[:, :], rows, start=True, stop=True).then_inc(counted, 1)

            @block.gpsimd
            def _(pool):
                pool.wait_ge(cleared, 16)
                pool.wait_ge(marks["dest"], 1)
                n = 0
                for t in range(TILES):
                    for k in range(TOP_K):
                        if n >= 2:
                            pool.wait_ge(scattered[n % 2], 16 * (n // 2))
                        pool.indirect_dma_start(dr["slot_token"], bass.IndirectOffsetOnAxis(ap=dest[:, k, t:t + 1], axis=0),
                                                tokens[:, t:t + 1], None).then_inc(scattered[n % 2], 16)
                        n += 1
                for x in range(2):
                    pool.wait_ge(scattered[x], 16 * (n // 2))


class ExpertWeights:

    def __init__(self, nc, ctx, top, dr):
        sb = lambda n, s: ctx.enter_context(nc.sbuf_tensor(n, s, F32))
        self.dr = dr
        self.gate, self.up = sb("w_gate_slots", [P, 2, KD * FF]), sb("w_up_slots", [P, 2, KD * FF])
        self.down = sb("w_down_slots", [P, 2, KF * D_MODEL])
        self.loaded = Event(top, "g_weights", W_DMAS)

    def load(self, sp, e, j):
        for buf, name, k in ((self.gate, "w_gate", KD), (self.up, "w_up", KD), (self.down, "w_down", KF)):
            src = self.dr[name][bass.ds(e, 1) if not isinstance(e, int) else slice(e, e + 1), :, :].rearrange("a (k p) n -> p (a k) n", p=P)
            sp.dma_start(buf[:, j, :].rearrange("p (k n) -> p k n", k=k), src).then_inc(self.loaded[j], 16)

    def load_first(self, sp):
        for e in range(2):
            self.load(sp, e, e)


def experts(nc, top, dr, table, weights):
    HALF = FF // 2
    KH = KF // 2
    with ExitStack() as ctx:
        sb = lambda n, s, d=F32: ctx.enter_context(nc.sbuf_tensor(n, s, d))
        ps = lambda n, s, d=F32: ctx.enter_context(nc.psum_tensor(n, s, d))
        sem = lambda n: top.semaphore(n)
        ev = lambda n, per=1: Event(top, f"g_{n}", per)
        wg, wu, wd, loaded = weights.gate, weights.up, weights.down, weights.loaded
        ident = sb("ident_g", [P, P])
        ids = sb("row_tokens", [P, 2, 1], I32)
        rows = sb("rows", [P, 2, D_MODEL])
        rowsT = sb("rows_T", [P, 2, KD, P])
        sg, hid, hidT = sb("silu_gate", [P, FF]), sb("hidden", [P, FF]), sb("hidden_T", [P, KF, P])
        y = sb("y_block", [P, 2, D_MODEL])
        zeros = sb("zeros_g", [P, D_MODEL])
        pt = ps("rows_turned", [P, KD, P])
        pg, ph = ps("gate_psum", [P, FF]), ps("hidden_turned", [P, KF, P])
        pu = ps("up_psum", [P, 2, 512])
        py = ps("down", [P, 2, 512])
        consts_in, zeros_set, passed = sem("g_consts"), sem("g_zeros"), sem("g_passed")
        ids_in, gathered, turned, rowsT_ready = ev("ids", 16), ev("gathered", 16), ev("turned"), ev("rowsT")
        gated, silued, downed, stored = ev("gate"), ev("silu"), ev("down"), ev("stored", 16)
        upped, hid_ready, hid_turned, hidT_ready = (ev(n, 2) for n in ("up", "hid", "hid_turned", "hidT"))
        y_ready = Count(top, "g_y_ready")

        def block_loop(eng, body, without=None):
            count = eng.value_load(table[0:1, BT_UPTO, N_EXPERTS - 1:N_EXPERTS], min_val=1, max_val=N_BLOCKS)
            with eng.Fori(0, N_BLOCKS // 2) as i:
                for j in range(2):
                    with eng.If(i * 2 + j < count):
                        body(i, j)
                    if without:
                        with eng.Else():
                            without(i, j)

        with nc.Block() as block:
            @block.sync
            def _(sp):
                sp.dma_start(ident[:, :], dr["c_ident"]).then_inc(consts_in, 16)

                with sp.Fori(1, N_EXPERTS // 2) as i:
                    for j in range(2):
                        upto = sp.value_load(table[0:1, BT_UPTO, bass.ds(i * 2 + (j - 2), 1)], min_val=0, max_val=N_BLOCKS)
                        sp.wait_ge(y_ready.sem, upto)
                        weights.load(sp, i * 2 + j, j)
                for j in range(2):
                    sp.wait_ge(loaded[j], W_DMAS * (N_EXPERTS // 2))

            @block.gpsimd
            def _(pool):
                def gather(i, j):
                    b = i * 2 + j
                    pool.wait_ge(*turned.before_last(i, j))
                    pool.dma_start(ids[:, j, :], tile_rows(dr["slot_token"], b)).then_inc(ids_in[j], 16)
                    pool.wait_ge(*ids_in.now(i, j))
                    pool.sem_inc(passed, 1)
                    pool.indirect_dma_start(rows[:, j, :], None, dr["h2"], bass.IndirectOffsetOnAxis(ap=ids[:, j, :], axis=0)).then_inc(gathered[j], 16)

                gather(0, 0)
                block_loop(pool, lambda i, j: gather(*following(i, j)))

            @block.scalar
            def _(act):
                def body(i, j):
                    act.wait_ge(*gated.now(i, j))
                    act.wait_ge(*hid_ready.last(i, j))
                    act.activation(sg[:, :], pg[:, :], ACT.Silu).then_inc(silued[j], 1)
                    act.wait_ge(*downed.last(i, j))
                    for half in range(2):
                        act.wait_ge(*hid_turned.now(i, j, half + 1))
                        part = slice(half * KH, (half + 1) * KH)
                        act.activation(hidT[:, part, :], ph[:, part, :], ACT.Copy).then_inc(hidT_ready[j], 1)
                    act.wait_ge(*y_ready.now(i * 2 + j))
                    act.dma_start(tile_rows(dr["y"], i * 2 + j), y[:, j, :]).then_inc(stored[j], 16)

                def zero(i, j):
                    act.dma_start(tile_rows(dr["y"], i * 2 + j), zeros[:, :]).then_inc(stored[j], 16)

                act.wait_ge(zeros_set, 1)
                block_loop(act, body, zero)
                for j in range(2):
                    act.wait_ge(stored[j], 16 * (N_BLOCKS // 2))

            @block.vector
            def _(dve):
                def copy_rows(i, j):
                    dve.wait_ge(*turned.now(i, j))
                    dve.wait_ge(*upped.before_last(i, j))
                    dve.tensor_copy(rowsT[:, j, :, :], pt[:, :, :]).then_inc(rowsT_ready[j], 1)

                def body(i, j):
                    dve.wait_ge(*silued.now(i, j))
                    dve.wait_ge(*hid_turned.last(i, j))
                    for half in range(2):
                        dve.wait_ge(*upped.now(i, j, half + 1))
                        part = slice(half * HALF, (half + 1) * HALF)
                        dve.tensor_tensor(hid[:, part], sg[:, part], pu[:, half, 0:HALF], ALU.mult).then_inc(hid_ready[j], 1)
                    copy_rows(*following(i, j))
                    dve.wait_ge(*downed.now(i, j))
                    dve.wait_ge(*stored.before_last(i, j))
                    dve.tensor_copy(y[:, j, :], py[:, :, :].rearrange("p a n -> p (a n)")).then_inc(y_ready.sem, 1)

                dve.memset(zeros[:, :], 0.0).then_inc(zeros_set, 1)
                copy_rows(0, 0)
                block_loop(dve, body)

            @block.tensor
            def _(pe):
                pe.wait_ge(consts_in, 16)

                def turn_rows(i, j):
                    pe.wait_ge(*gathered.now(i, j))
                    pe.wait_ge(*rowsT_ready.last(i, j))
                    for k in range(KD):
                        ins = pe.transpose(pt[:, k, :], rows[:, j, k * P:(k + 1) * P], ident[:, :])
                    ins.then_inc(turned[j], 1)

                def body(i, j):
                    b = i * 2 + j
                    entry = lambda r, top: pe.value_load(table[0:1, r, bass.ds(b, 1)], min_val=0, max_val=top)
                    even, odd = entry(BT_EVEN, 65535), entry(BT_ODD, 65535)
                    slot = entry(BT_SLOT, 1)
                    pe.wait_ge(loaded[0], even)
                    pe.wait_ge(loaded[1], odd)
                    part = lambda w, c0, c1: w[:, bass.ds(slot, 1), c0:c1].rearrange("p a n -> p (a n)")
                    pe.wait_ge(*rowsT_ready.now(i, j))
                    pe.wait_ge(*silued.last(i, j))
                    for k in range(KD):
                        ins = pe.matmul(pg[:, :], rowsT[:, j, k, :], part(wg, k * FF, (k + 1) * FF), start=k == 0, stop=k == KD - 1)
                    ins.then_inc(gated[j], 1)
                    for half in range(2):
                        pe.wait_ge(*hid_ready.last(i, j))
                        for k in range(KD):
                            c = k * FF + half * HALF
                            ins = pe.matmul(pu[:, half, 0:HALF], rowsT[:, j, k, :], part(wu, c, c + HALF), start=k == 0, stop=k == KD - 1)
                        ins.then_inc(upped[j], 1)

                    def turn_hidden(half):
                        pe.wait_ge(*hid_ready.now(i, j, half + 1))
                        pe.wait_ge(*(hidT_ready.now(i, j, 1) if half else hidT_ready.last(i, j)))
                        for k in range(half * KH, (half + 1) * KH):
                            ins = pe.transpose(ph[:, k, :], hid[:, k * P:(k + 1) * P], ident[:, :])
                        ins.then_inc(hid_turned[j], 1)

                    def down(k, n):
                        c = k * D_MODEL + n * 512
                        return pe.matmul(py[:, n, :], hidT[:, k, :], part(wd, c, c + 512), start=k == 0, stop=k == KF - 1)

                    turn_hidden(0)
                    turn_rows(*following(i, j))
                    pe.wait_ge(*hidT_ready.now(i, j, 1))
                    pe.wait_ge(*y_ready.last(b))
                    down(0, 0)
                    turn_hidden(1)
                    down(0, 1)
                    for k in range(1, KF):
                        if k == KH:
                            pe.wait_ge(*hidT_ready.now(i, j, 2))
                        for n in range(2):
                            ins = down(k, n)
                    ins.then_inc(downed[j], 1)

                turn_rows(0, 0)
                block_loop(pe, body)


def combine(nc, top, dr, dest, gate):
    with ExitStack() as ctx:
        sb = lambda n, s, d=F32: ctx.enter_context(nc.sbuf_tensor(n, s, d))
        sem = lambda n: top.semaphore(n)
        ev = lambda n, per=1: Event(top, f"h_{n}", per)
        eps, nw = sb("eps_h", [P, 1]), sb("final_norm_rows", [P, D_MODEL])
        x1 = sb("x1_h", [P, 2, D_MODEL])
        idx = sb("slots_h", [P, 2, TOP_K], I32)
        g = sb("gates_h", [P, 2, TOP_K])
        ys = sb("y_rows", [P, 2, TOP_K, D_MODEL])
        acc, sq = sb("sum_h", [P, 2, D_MODEL]), sb("squares_h", [P, D_MODEL])
        st = sb("stats_h", [P, 2, 3])
        out = sb("out_tile", [P, 2, D_MODEL])
        consts_in, eps_set, own_dve = sem("h_consts"), sem("h_eps"), sem("h_own_dve")
        passed = sem("h_passed")
        x_loaded, indexed, gathered, summed = ev("x_loaded", 16), ev("indexed"), ev("gathered", 32), ev("summed")
        sum_sq, rms, ready, stored = ev("sum_sq"), ev("rms"), ev("ready"), ev("stored", 16)

        with nc.Block() as block:
            @block.sync
            def _(sp):
                sp.dma_start(nw[:, :], dr["final_norm_w"].unsqueeze(0).broadcast_to([P, D_MODEL])).then_inc(consts_in, 16)

                def load(i, j):
                    sp.wait_ge(*summed.before_last(i, j))
                    sp.dma_start(x1[:, j, :], tile_rows(dr["x1"], i * 2 + j)).then_inc(x_loaded[j], 16)

                def tile(i, j, last=False):
                    if not last:
                        load(*following(i, j))
                    sp.wait_ge(*ready.now(i, j))
                    sp.dma_start(tile_rows(dr["out"], i * 2 + j), out[:, j, :]).then_inc(stored[j], 16)

                load(0, 0)
                rounds(sp, None, tile)
                for j in range(2):
                    sp.wait_ge(stored[j], 16 * (TILES // 2))

            @block.gpsimd
            def _(pool):
                with pool.Fori(0, TILES // 2) as i:
                    for j in range(2):
                        pool.wait_ge(*indexed.now(i, j))
                        pool.wait_ge(*summed.before_last(i, j))
                        pool.sem_inc(passed, 1)
                        for k in range(TOP_K):
                            pool.indirect_dma_start(ys[:, j, k, :], None, dr["y"],
                                                    bass.IndirectOffsetOnAxis(ap=idx[:, j, k:k + 1], axis=0)).then_inc(gathered[j], 16)

            @block.scalar
            def _(act):
                act.wait_ge(eps_set, 1)
                with act.Fori(0, TILES // 2) as i:
                    for j in range(2):
                        act.wait_ge(*summed.now(i, j))
                        act.activation(sq[:, :], acc[:, j, :], ACT.Square, accum_out=st[:, j, 0:1]).then_inc(sum_sq[j], 1)
                        act.wait_ge(*sum_sq.now(i, j))
                        act.activation(st[:, j, 1:2], st[:, j, 0:1], ACT.Sqrt, bias=eps[:, :], scale=1.0 / D_MODEL).then_inc(rms[j], 1)

            @block.vector
            def _(dve):
                own = Chain(dve, own_dve, 2 * 4)

                def index(i, j):
                    t = i * 2 + j
                    dve.wait_ge(*gathered.before_last(i, j))
                    own.mark(dve.tensor_copy(g[:, j, :].unsqueeze(2), gate[:, :, bass.ds(t, 1)]))
                    dve.tensor_copy(idx[:, j, :].unsqueeze(2), dest[:, :, bass.ds(t, 1)]).then_inc(indexed[j], 1)

                def tile(i, j, last=False):
                    if not last:
                        index(*following(i, j))
                    own.wait()
                    dve.wait_ge(*gathered.now(i, j))
                    own.link(dve.tensor_scalar(acc[:, j, :], ys[:, j, 0, :], g[:, j, 0:1], None, ALU.mult))
                    own.link(dve.scalar_tensor_tensor(out=acc[:, j, :], in0=ys[:, j, 1, :], scalar=g[:, j, 1:2], in1=acc[:, j, :], op0=ALU.mult, op1=ALU.add))
                    dve.wait_ge(*x_loaded.now(i, j))
                    dve.tensor_tensor(acc[:, j, :], acc[:, j, :], x1[:, j, :], ALU.add).then_inc(summed[j], 1)
                    dve.wait_ge(*rms.now(i, j))
                    own.link(dve.reciprocal(st[:, j, 2:3], st[:, j, 1:2]))
                    dve.wait_ge(*stored.before_last(i, j))
                    dve.scalar_tensor_tensor(out=out[:, j, :], in0=acc[:, j, :], scalar=st[:, j, 2:3], in1=nw[:, :], op0=ALU.mult, op1=ALU.mult).then_inc(ready[j], 1)

                dve.memset(eps[:, :], EPS).then_inc(eps_set, 1)
                dve.wait_ge(consts_in, 16)
                index(0, 0)
                rounds(dve, own, tile)


def build(nc, dr, until=99):
    for name, shape in SCRATCH.items():
        dr[name] = nc.dram_tensor(f"scratch_{name}", shape, F32, kind="Internal").ap()
    dr["qT"] = nc.dram_tensor("scratch_qT", (TILES, P, ATT_HEADS, P), F32, kind="Internal").ap()
    dr["slot_token"] = nc.dram_tensor("scratch_slot_token", (SLOTS + P, 1), I32, kind="Internal").ap()
    with ExitStack() as top:
        sb = lambda n, s, d=F32: top.enter_context(nc.sbuf_tensor(n, s, d))
        gates = sb("gates", [P, TILES, 16])
        with nc.sbuf_tensor("xT_all", [P, KD, SEQ], F32) as xT_all:
            keep = {"xT_all": xT_all, "gates": gates}
            with Stage(nc) as stage:
                project_tokens(nc, stage, dr, keep)
            if until > 1:
                with Stage(nc) as stage:
                    project_features(nc, stage, dr, keep)
        if until > 2:
            with Stage(nc) as stage:
                gated_delta(nc, stage, dr, gates)
        w_scope = top.enter_context(ExitStack())
        w_out = w_scope.enter_context(nc.sbuf_tensor("w_out_sb", [P, KD, D_MODEL], F32))
        if until > 3:
            with Stage(nc) as stage:
                attention(nc, stage, dr, w_out)
        if until > 4:
            logits = sb("logits", [P, TILES, N_GROUPS + N_EXPERTS])
            dest = sb("dest", [P, TOP_K, TILES], I32)
            gate = sb("gate", [P, TOP_K, TILES])
            table = sb("block_table", [1, BT_ROWS, N_BLOCKS], I32)
            with Stage(nc) as lasting, ExitStack() as slots:
                weights = ExpertWeights(nc, slots, lasting, dr)
                with Stage(nc) as stage:
                    mix_out(nc, stage, dr, logits, w_out, weights.load_first)
                if until > 5:
                    with Stage(nc) as stage:
                        route(nc, stage, dr, logits, dest, gate, table)
                if until > 6:
                    with Stage(nc) as stage:
                        experts(nc, stage, dr, table, weights)
            if until > 7:
                with Stage(nc) as stage:
                    combine(nc, stage, dr, dest, gate)
def constants():
    f = np.float32
    p = np.arange(P)
    rows = SEQ // GRID_W
    row = np.repeat(np.arange(rows), GRID_W).astype(f)
    col = np.tile(np.arange(GRID_W), rows).astype(f)
    axis = ATT_D // 2
    inv = (f(10000.0) ** (-np.arange(0, axis, 2).astype(f) / f(axis))).astype(f)
    ang = np.concatenate([row[:, None] * inv, col[:, None] * inv], axis=-1).astype(f)
    out = {"c_ident": np.eye(P, dtype=f), "c_cos": np.cos(ang).astype(f), "c_sin": np.sin(ang).astype(f),
           "c_ones": np.ones((P, P), f)}
    upto = (p[:, None] <= p[None, :]).astype(f)
    out["c_upto"] = np.stack([upto, upto.T], 0).transpose(1, 0, 2).copy()
    out["c_before"] = (p[:, None] < p[None, :]).astype(f)
    level = []
    for n in range(7):
        b = 1 << n
        same = (p[:, None] // (2 * b)) == (p[None, :] // (2 * b))
        m = (same & (p[:, None] % (2 * b) < b) & (p[None, :] % (2 * b) >= b)).astype(f)
        level.append([m, m.T])
    out["c_level"] = np.array(level, f).transpose(2, 1, 0, 3).copy()
    n = np.zeros((2, CONV_BLOCKS), f)
    n[0, :GDN_HEADS], n[1, :GDN_HEADS] = GDN_D, GDN_D * EPS
    n[0, GDN_HEADS:2 * GDN_HEADS], n[1, GDN_HEADS:2 * GDN_HEADS] = 1, EPS
    n[1, 2 * GDN_HEADS:] = 1
    out["c_norm"] = np.broadcast_to(n.reshape(1, -1), (P, 2 * CONV_BLOCKS)).copy()
    out["c_iota"] = np.broadcast_to(np.arange(64, dtype=f), (P, 64)).copy()
    out["c_slot0"] = np.zeros((SLOTS + P, 1), np.int32)
    out["c_tokens"] = (np.arange(TILES)[None, :] * P + p[:, None]).astype(np.int32)
    return out


SHAPES = {"x": (SEQ, D_MODEL), "norm_mix_w": (D_MODEL,), "w_in": (D_MODEL, D_IN), "conv_w": (CONV_W, 3 * GDN_W),
          "a_log": (1, 8), "dt_bias": (1, 8), "gdn_norm_w": (GDN_D,), "q_norm_w": (ATT_D,),
          "k_norm_w": (ATT_D,), "w_out": (D_MODEL, D_MODEL), "norm_ffn_w": (D_MODEL,),
          "w_router_group": (D_MODEL, N_GROUPS), "w_router_expert": (D_MODEL, N_EXPERTS),
          "w_gate": (N_EXPERTS, D_MODEL, FF), "w_up": (N_EXPERTS, D_MODEL, FF), "w_down": (N_EXPERTS, FF, D_MODEL),
          "final_norm_w": (D_MODEL,)}
SCRATCH = {"z": (SEQ, GDN_W), "qk": (SEQ, ATT_QK), "v": (SEQ, ATT_KV),
           "feat": (CONV_BLOCKS, P, SEQ), "tok": (SEQ, 3 * GDN_W), "o_gdn": (2, SEQ, GDN_W), "o_att": (SEQ, GDN_W), 
           "x1": (SEQ, D_MODEL), "h2": (SEQ, D_MODEL), "y": (SLOTS, D_MODEL)}


def kernel(**inputs):
    import numpy as _np
    import concourse.bacc as _bacc
    from concourse import mybir as _mybir
    from concourse.bass_utils import run_bass_kernel_spmd as _run

    nc = _bacc.Bacc("TRN2", target_bir_lowering=False, num_devices=1)
    arrays, dr = {}, {}
    for name, shape in SHAPES.items():
        a = _np.ascontiguousarray(inputs[name]).reshape(shape)
        arrays[f"in_{name}"] = a
        dr[name] = nc.dram_tensor(f"in_{name}", a.shape, _mybir.dt.from_np(a.dtype), kind="ExternalInput").ap()
    for name, a in constants().items():
        arrays[name] = a
        dr[name] = nc.dram_tensor(name, a.shape, _mybir.dt.from_np(a.dtype), kind="ExternalInput").ap()
    dr["out"] = nc.dram_tensor("out", (SEQ, D_MODEL), F32, kind="ExternalOutput").ap()
    build(nc, dr)
    r = _run(nc, [arrays], core_ids=[0])
    return r.results[0]["out"].reshape(1, SEQ, D_MODEL)
```

```python
import numpy as np
from contextlib import ExitStack
import concourse.bass as bass
from concourse import mybir
from concourse.alu_op_type import AluOpType as ALU

F32 = mybir.dt.float32
F32R = mybir.dt.float32r
I32 = mybir.dt.int32
ACT = mybir.ActivationFunctionType
AX = mybir.AxisListType

P = 128
SEQ, D_MODEL = 2048, 1024
TILES = SEQ // P
KD = D_MODEL // P
GDN_HEADS, GDN_D = 4, 128
CONV_W = 5
CONV_BLOCKS = 3 * GDN_HEADS
ATT_HEADS, KV_HEADS, ATT_D = 8, 2, 64
GROUP = ATT_HEADS // KV_HEADS
GRID_W = 64
N_GROUPS, PER_GROUP, TOP_K = 4, 8, 2
N_EXPERTS = N_GROUPS * PER_GROUP
FF = 512
KF = FF // P
EPS = 1e-6
GDN_W = GDN_HEADS * GDN_D
C_Z = 3 * GDN_W
C_GATES = C_Z + GDN_W
C_ATT = C_GATES + 4 * GDN_HEADS
ATT_QK = (ATT_HEADS + KV_HEADS) * ATT_D
ATT_KV = KV_HEADS * ATT_D
D_IN = C_ATT + ATT_QK + ATT_KV
N_BLOCKS = -(-(SEQ * TOP_K + N_EXPERTS * (P - 1)) // P)
SLOTS = N_BLOCKS * P


class Stage:

    def __init__(self, nc):
        self.nc, self.sems = nc, []

    def semaphore(self, name):
        self.sems.append(self.nc.alloc_semaphore(name=name))
        return self.sems[-1]

    def __enter__(self):
        return self

    def __exit__(self, *_):
        self.nc.clear_and_free_semaphores(self.sems)
        self.nc.all_engine_barrier()


class Event:

    def __init__(self, stage, name, per=1):
        self.sems = [stage.semaphore(f"{name}_{x}") for x in ("even", "odd")]
        self.per = per

    def __getitem__(self, j):
        return self.sems[j]

    def now(self, i, j, n=None):
        return self.sems[j], i * self.per + (self.per if n is None else n)

    def last(self, i, j):
        return self.sems[1 - j], (i + j) * self.per

    def before_last(self, i, j):
        return self.sems[j], i * self.per


class Count:

    def __init__(self, stage, name, per=1):
        self.sem, self.per = stage.semaphore(name), per

    def now(self, t, n=None):
        return self.sem, t * self.per + (self.per if n is None else n)

    def last(self, t):
        return self.sem, t * self.per


class Chain:

    def __init__(self, eng, sem, per_round=0):
        self.eng, self.sem, self.per, self.base, self.n, self.start = eng, sem, per_round, 0, 0, 0

    def round(self, i):
        self.base, self.n = i * self.per + self.start, 0

    def mark(self, ins):
        ins.then_inc(self.sem, 1)
        self.n += 1

    def wait(self):
        self.eng.wait_ge(self.sem, self.base + self.n)

    def link(self, ins):
        self.mark(ins)
        self.wait()

    def close(self):
        assert self.n == self.per, f"a round has {self.n} links"


def following(i, j):
    return (i, 1) if j == 0 else (i + 1, 0)


def rounds(eng, own, tile, n=TILES):
    def pair(i, end):
        if own:
            own.round(i)
        for j in range(2):
            tile(i, j, end and j == 1)

    if own:
        own.start = own.n
    with eng.Fori(0, n // 2 - 1) as i:
        pair(i, False)
        if own:
            own.close()
    pair(n // 2 - 1, True)


def tile_rows(dram, t, n=1):
    return dram.rearrange("(t p) w -> t p w", p=P)[bass.ds(t, 1), :, :].rearrange("a p w -> (a p) w")


def at(tensor, t):
    return tensor[:, bass.ds(t, 1), :].rearrange("p a w -> p (a w)")


def project_tokens(nc, top, dr, gates):
    NT = GDN_W + ATT_QK + ATT_KV + 16
    Z0, Q0, K0 = 0, GDN_W, 2 * GDN_W
    NK = NT - K0
    NH = ATT_HEADS + KV_HEADS
    half = ATT_D // 2
    with ExitStack() as ctx:
        sb = lambda n, s, d=F32: ctx.enter_context(nc.sbuf_tensor(n, s, d))
        ps = lambda n, s, d=F32: ctx.enter_context(nc.psum_tensor(n, s, d))
        sem = lambda n: top.semaphore(n)
        ev = lambda n, per=1: Event(top, n, per)
        w_zq = sb("w_zq", [P, KD, K0])
        w_first, w_rest = sb("w_zq_first", [P, KD, K0], F32R), sb("w_zq_rest", [P, KD, K0], F32R)
        w_kv = sb("w_kv", [P, KD, NK])
        ident = sb("ident_a", [P, P])
        nw = sb("norm_mix_cols", [P, KD])
        qkw = sb("qk_norm_rows", [P, NH, ATT_D])
        cos = sb("rope_cos", [P, TILES, half])
        sin = sb("rope_sin", [P, TILES, half])
        x_in = sb("x_in", [P, 2, D_MODEL])
        stat = sb("stat_a", [P, 2, 4])
        eps = sb("eps_a", [P, 1])
        xn = sb("xn", [P, 2, D_MODEL])
        xT = sb("xT_tile", [P, 2, KD, P])
        xT_first, xT_rest = sb("xT_first", [P, 2, KD, P], F32R), sb("xT_rest", [P, 2, KD, P], F32R)
        zs = sb("z_silu", [P, GDN_W])
        qk = sb("qk_raw", [P, 2, ATT_QK + ATT_KV])
        qs = sb("qk_stats", [P, 2, 3, NH])
        qn = sb("qk_normed", [P, NH, ATT_D])
        rot = sb("rope_products", [P, 4, NH, half])
        qsq = rot[:, 0:2].rearrange("p a h f -> p (a h f)").rearrange("p (h d) -> p h d", d=ATT_D)
        qr = sb("qk_roped", [P, 2, ATT_QK])
        tp = ps("transposed", [P, KD, P])
        pz = ps("proj_z", [P, GDN_W])
        pq = ps("proj_q", [P, GDN_W])
        pk = ps("proj_kv", [P, NK])
        z_weights_in, q_weights_in, weights_in = sem("a_z_weights_in"), sem("a_q_weights_in"), sem("a_weights_in")
        w_rounded, w_ready = sem("a_w_rounded"), sem("a_w_ready")
        xT_rounded, parts_ready = ev("xT_rounded"), ev("xT_parts")
        consts_in, rope_in = sem("a_consts_in"), sem("a_rope_in")
        eps_set = sem("a_eps_set")
        x_loaded, row_sum, row_rms, normed = ev("x_loaded", 16), ev("row_sum"), ev("row_rms"), ev("x_normed")
        transposed, xT_ready, stored_xT = ev("x_transposed"), ev("xT_ready"), ev("xT_stored", 16)
        projected, taken, z_ready = ev("projected", 3), ev("proj_taken"), ev("z_ready")
        qk_sums, qk_rms, roped = ev("qk_sums"), ev("qk_rms"), ev("qk_roped")
        stored_z, stored_qk, stored_v = ev("z_stored", 16), ev("qk_stored", 16), ev("v_stored", 16)
        dve_chain = sem("a_dve")

        with nc.Block() as block:
            @block.sync
            def _(sp):
                def load(i, j):
                    sp.wait_ge(*row_sum.before_last(i, j))
                    sp.wait_ge(*normed.before_last(i, j))
                    sp.dma_start(x_in[:, j, :], tile_rows(dr["x"], i * 2 + j)).then_inc(x_loaded[j], 16)

                w = dr["w_in"].rearrange("(k p) n -> p k n", p=P)
                load(0, 0)
                sp.dma_start(ident[:, :], dr["c_ident"]).then_inc(consts_in, 16)
                sp.dma_start(nw[:, :], dr["norm_mix_w"].rearrange("(k p) -> p k", p=P),
                             allow_slow_non_contiguous=True).then_inc(consts_in, 16)
                sp.dma_start(w_zq[:, :, Z0:Q0], w[:, :, C_Z:C_GATES]).then_inc(z_weights_in, 16)
                load(0, 1)
                sp.dma_start(w_zq[:, :, Q0:K0], w[:, :, C_ATT:C_ATT + GDN_W]).then_inc(q_weights_in, 16)
                sp.dma_start(w_kv[:, :, 0:NK - 16], w[:, :, C_ATT + GDN_W:D_IN]).then_inc(weights_in, 16)
                sp.dma_start(w_kv[:, :, NK - 16:NK], w[:, :, C_GATES:C_ATT],
                             allow_slow_non_contiguous=True).then_inc(weights_in, 16)
                for h in range(NH):
                    src = dr["q_norm_w"] if h < ATT_HEADS else dr["k_norm_w"]
                    sp.dma_start(qkw[:, h, :], src.unsqueeze(0).broadcast_to([P, ATT_D])).then_inc(rope_in, 16)
                sp.dma_start(cos[:, :, :], dr["c_cos"].rearrange("(t p) f -> p t f", p=P)).then_inc(rope_in, 16)
                sp.dma_start(sin[:, :, :], dr["c_sin"].rearrange("(t p) f -> p t f", p=P)).then_inc(rope_in, 16)
                with sp.Fori(1, TILES // 2) as i:
                    for j in range(2):
                        load(i, j)

            @block.gpsimd
            def _(pool):
                with pool.Fori(0, TILES // 2) as i:
                    for j in range(2):
                        t = i * 2 + j
                        pool.wait_ge(*xT_ready.now(i, j))
                        pool.dma_start(dr["xT"][:, :, bass.ds(t * P, P)], xT[:, j, :, :]).then_inc(stored_xT[j], 16)
                        pool.wait_ge(*z_ready.now(i, j))
                        pool.dma_start(tile_rows(dr["z"], t), zs[:, :]).then_inc(stored_z[j], 16)
                        pool.wait_ge(*roped.now(i, j))
                        pool.dma_start(tile_rows(dr["qk"], t), qr[:, j, :]).then_inc(stored_qk[j], 16)
                        pool.dma_start(tile_rows(dr["v"], t), qk[:, j, ATT_QK:]).then_inc(stored_v[j], 16)
                for j in range(2):
                    for s in (stored_xT, stored_z, stored_qk, stored_v):
                        pool.wait_ge(s[j], 16 * (TILES // 2))

            @block.scalar
            def _(act):
                act.wait_ge(eps_set, 1)

                def row_stats(i, j):
                    act.wait_ge(*x_loaded.now(i, j))
                    act.wait_ge(*normed.before_last(i, j))
                    act.wait_ge(*transposed.before_last(i, j))
                    act.activation(xn[:, j, :], x_in[:, j, :], ACT.Square, accum_out=stat[:, j, 0:1]).then_inc(row_sum[j], 1)
                    act.wait_ge(*row_sum.now(i, j))
                    act.activation(stat[:, j, 1:2], stat[:, j, 0:1], ACT.Sqrt, bias=eps[:, 0:1], scale=1.0 / D_MODEL).then_inc(row_rms[j], 1)

                def round_weights(n):
                    act.wait_ge((z_weights_in, q_weights_in)[n], 16)
                    part = slice(n * GDN_W, (n + 1) * GDN_W)
                    act.activation(w_first[:, :, part], w_zq[:, :, part], ACT.Copy).then_inc(w_rounded, 1)

                def round_xT(i, j):
                    act.wait_ge(*xT_ready.now(i, j))
                    act.wait_ge(*projected.before_last(i, j))
                    act.activation(xT_first[:, j, :, :], xT[:, j, :, :], ACT.Copy).then_inc(xT_rounded[j], 1)

                def tile(i, j, last=False):
                    t = i * 2 + j
                    if not last:
                        row_stats(*following(i, j))
                    act.wait_ge(*projected.now(i, j, 1))
                    act.wait_ge(*stored_z.last(i, j))
                    act.activation(zs[:, :], pz[:, :], ACT.Silu).then_inc(z_ready[j], 1)
                    if not last:
                        round_xT(*following(i, j))
                    act.wait_ge(*projected.now(i, j, 3))
                    act.wait_ge(*stored_v.before_last(i, j))
                    act.wait_ge(*roped.before_last(i, j))
                    act.activation(qk[:, j, 0:GDN_W], pq[:, :], ACT.Copy)
                    act.activation(qk[:, j, GDN_W:], pk[:, 0:NK - 16], ACT.Copy)
                    act.activation(at(gates, t), pk[:, NK - 16:NK], ACT.Copy).then_inc(taken[j], 1)
                    act.wait_ge(*qk_sums.now(i, j))
                    act.activation(qs[:, j, 1, :], qs[:, j, 0, :], ACT.Sqrt, bias=eps[:, 0:1], scale=1.0 / ATT_D).then_inc(qk_rms[j], 1)

                row_stats(0, 0)
                round_weights(0)
                round_xT(0, 0)
                round_weights(1)
                rounds(act, None, tile)

            @block.vector
            def _(dve):
                own = Chain(dve, dve_chain, 2 * 10)
                dve.memset(eps[:, :], EPS).then_inc(eps_set, 1)
                dve.wait_ge(consts_in, 32)

                def normalize(i, j):
                    dve.wait_ge(*row_rms.now(i, j))
                    own.link(dve.reciprocal(stat[:, j, 2:3], stat[:, j, 1:2]))
                    dve.wait_ge(*transposed.before_last(i, j))
                    dve.tensor_scalar(xn[:, j, :], x_in[:, j, :], stat[:, j, 2:3], None, ALU.mult).then_inc(normed[j], 1)
                    dve.wait_ge(*transposed.now(i, j))
                    dve.wait_ge(*projected.before_last(i, j))
                    dve.wait_ge(*stored_xT.before_last(i, j))
                    dve.tensor_tensor(xT[:, j, :, :], tp[:, :, :], nw[:, :].unsqueeze(2).broadcast_to([P, KD, P]),
                                      ALU.mult).then_inc(xT_ready[j], 1)
                    dve.wait_ge(*xT_rounded.now(i, j))
                    dve.tensor_tensor(xT_rest[:, j, :, :], xT[:, j, :, :], xT_first[:, j, :, :].bitcast(F32), ALU.subtract).then_inc(parts_ready[j], 1)

                def rest_of_weights(n):
                    dve.wait_ge(w_rounded, n + 1)
                    part = slice(n * GDN_W, (n + 1) * GDN_W)
                    dve.tensor_tensor(w_rest[:, :, part], w_zq[:, :, part], w_first[:, :, part].bitcast(F32), ALU.subtract).then_inc(w_ready, 1)

                def tile(i, j, last=False):
                    t = i * 2 + j
                    if not last:
                        normalize(*following(i, j))
                    dve.wait_ge(*taken.now(i, j))
                    raw = qk[:, j, 0:ATT_QK].rearrange("p (h d) -> p h d", d=ATT_D)
                    dve.wait_ge(*roped.last(i, j))
                    own.link(dve.tensor_tensor(qsq, raw, raw, ALU.mult))
                    dve.tensor_reduce(qs[:, j, 0, :], qsq, AX.X, ALU.add).then_inc(qk_sums[j], 1)
                    dve.wait_ge(*qk_rms.now(i, j))
                    own.link(dve.reciprocal(qs[:, j, 2, :], qs[:, j, 1, :]))
                    own.link(dve.tensor_tensor(qn[:, :, :], raw, qs[:, j, 2, :].unsqueeze(2).broadcast_to([P, NH, ATT_D]), ALU.mult))
                    own.link(dve.tensor_tensor(qn[:, :, :], qn[:, :, :], qkw[:, :, :], ALU.mult))
                    pair = qn[:, :, :].rearrange("p h (f two) -> p h f two", two=2)
                    c = at(cos, t).unsqueeze(1).broadcast_to([P, NH, half])
                    s = at(sin, t).unsqueeze(1).broadcast_to([P, NH, half])
                    own.mark(dve.tensor_tensor(rot[:, 0], pair[:, :, :, 0], c, ALU.mult))
                    own.mark(dve.tensor_tensor(rot[:, 1], pair[:, :, :, 1], s, ALU.mult))
                    own.mark(dve.tensor_tensor(rot[:, 2], pair[:, :, :, 0], s, ALU.mult))
                    own.link(dve.tensor_tensor(rot[:, 3], pair[:, :, :, 1], c, ALU.mult))
                    out = qr[:, j, :].rearrange("p (h f two) -> p h f two", h=NH, two=2)
                    dve.wait_ge(*stored_qk.before_last(i, j))
                    own.mark(dve.tensor_tensor(out[:, :, :, 0], rot[:, 0], rot[:, 1], ALU.subtract))
                    dve.tensor_tensor(out[:, :, :, 1], rot[:, 2], rot[:, 3], ALU.add).then_inc(roped[j], 1)

                normalize(0, 0)
                for n in range(2):
                    rest_of_weights(n)
                dve.wait_ge(rope_in, 16 * (2 + NH))
                rounds(dve, own, tile)

            @block.tensor
            def _(pe):
                pe.wait_ge(consts_in, 32)

                def transposes(i, j):
                    pe.wait_ge(*normed.now(i, j))
                    pe.wait_ge(*xT_ready.last(i, j))
                    for k in range(KD):
                        ins = pe.transpose(tp[:, k, :], xn[:, j, k * P:(k + 1) * P], ident[:, :])
                    ins.then_inc(transposed[j], 1)

                def tile(i, j, last=False):
                    pe.wait_ge(*parts_ready.now(i, j))
                    for n, out in enumerate((pz, pq)):
                        pe.wait_ge(w_ready, n + 1)
                        pe.wait_ge(*(taken if n else z_ready).last(i, j))
                        for k in range(KD):
                            for x, w in ((xT_first, w_first), (xT_first, w_rest), (xT_rest, w_first)):
                                ins = pe.matmul(out[:, :], x[:, j, k, :], w[:, k, n * GDN_W:(n + 1) * GDN_W],
                                                start=k == 0 and x is xT_first and w is w_first, stop=k == KD - 1 and x is xT_rest)
                        ins.then_inc(projected[j], 1)
                    if not last:
                        transposes(*following(i, j))
                    pe.wait_ge(weights_in, 32)
                    for k in range(KD):
                        ins = pe.matmul(pk[:, :], xT[:, j, k, :], w_kv[:, k, :], start=k == 0, stop=k == KD - 1)
                    ins.then_inc(projected[j], 1)

                transposes(0, 0)
                rounds(pe, None, tile)


def project_features(nc, top, dr):
    N = CONV_BLOCKS
    C = SEQ // 512
    PAD = CONV_W // 2
    TB = 3
    with ExitStack() as ctx:
        sb = lambda n, s, d=F32: ctx.enter_context(nc.sbuf_tensor(n, s, d))
        ps = lambda n, s, d=F32: ctx.enter_context(nc.psum_tensor(n, s, d))
        sem = lambda n: top.semaphore(n)
        ev = lambda n, per=1: Event(top, n, per)
        x_first, x_rest = sb("x_first", [P, KD, SEQ], F32R), sb("x_rest", [P, KD, SEQ], F32R)
        w_blk = sb("w_blk", [P, KD, P])
        w_first, w_rest = sb("w_first", [P, 2, KD, P], F32R), sb("w_rest", [P, 2, KD, P], F32R)
        ident = sb("ident_b", [P, P])
        norm = sb("norm_scale_bias", [P, 2, N, 1])
        cw = sb("conv_w_cols", [P, N, CONV_W])
        raw = sb("conv_in", [P, 2, SEQ + 2 * PAD])
        acc = sb("conv_acc", [P, SEQ])
        act_out = sb("silu_out", [P, SEQ])
        inv = sb("norms_b", [P, 3, TILES])
        feat = sb("features", [P, SEQ])
        tok = sb("features_by_token", [P, 2, TILES, P])
        pp = ps("proj_b", [P, C, 512])
        pt = ps("to_tokens", [P, TB, 4, P])
        pb = ps("to_channels", [P, 4, P])
        consts_in, cw_done, cw_ready, pads = sem("b_consts"), sem("b_conv_w_T"), sem("b_conv_w_ready"), sem("b_pads")
        w_loaded, w_rounded, w_ready = ev("w_blk_loaded", 16), ev("w_rounded"), ev("w_ready")
        HALF = KD // 2
        x_in = (tok[:, 0].rearrange("p t c -> p (t c)"), tok[:, 1].rearrange("p t c -> p (t c)"), acc[:, :])
        x_in = [b.rearrange("p (k s) -> p k s", k=HALF) for b in x_in]
        piece = lambda x, n: x[:, n % 2 * HALF:(n % 2 + 1) * HALF, n // 2 * 512:(n // 2 + 1) * 512]
        x_loaded = [sem(f"b_x_loaded{n}") for n in range(3)]
        x_rounded, x_ready = sem("b_x_rounded"), sem("b_x_ready")
        cw_rows = act_out[0:CONV_W, 0:N * P]
        projected, raw_ready, conv_done = ev("b_projected", C), ev("b_raw", C), ev("b_conv")
        silu_done = ev("b_silu")
        summed, norm2_ready, rms_ready = ev("b_summed", C), ev("b_norm2", C), ev("b_rms", C)
        turned, tok_ready, returned, feat_ready = ev("b_turned", C), ev("b_tok", C), ev("b_returned", C), ev("b_feat", C)
        stored_f, stored_t = ev("b_feat_stored", 16), ev("b_tok_stored", 16)
        dve_chain = sem("b_dve")

        with nc.Block() as block:
            @block.sync
            def _(sp):
                sp.dma_start(ident[:, :], dr["c_ident"]).then_inc(consts_in, 16)
                sp.dma_start(cw_rows, dr["conv_w"]).then_inc(consts_in, 16)
                sp.dma_start(norm[:, :, :, :], dr["c_norm"].rearrange("p (a n) -> p a n", a=2).unsqueeze(3)).then_inc(consts_in, 16)
                for n in range(2 * C):
                    if n >= 3:
                        sp.wait_ge(x_ready, n - 2)
                    sp.dma_start(x_in[n % 3], piece(dr["xT"], n)).then_inc(x_loaded[n % 3], 16)
                    if n == 0:
                        sp.dma_start(w_blk[:, :, :], dr["w_in"].rearrange("(k p) n -> p k n", p=P)[:, :, 0:P]).then_inc(w_loaded[0], 16)

                def load(i, j):
                    w = dr["w_in"].rearrange("(k p) n -> p k n", p=P)
                    sp.wait_ge(*w_ready.last(i, j))
                    sp.dma_start(w_blk[:, :, :], w[:, :, bass.ds((i * 2 + j) * P, P)]).then_inc(w_loaded[j], 16)

                def tile(i, j, ahead):
                    m = i * 2 + j
                    if ahead:
                        load(i + 1, j)
                    sp.wait_ge(*tok_ready.now(i, j))
                    sp.dma_start(dr["tok"].rearrange("(t p) c -> p t c", p=P)[:, :, bass.ds(m * P, P)], tok[:, j, :, :]).then_inc(stored_t[j], 16)
                    sp.wait_ge(*feat_ready.now(i, j))
                    sp.dma_start(dr["feat"][bass.ds(m, 1), :, :].rearrange("a p s -> (a p) s"), feat[:, :]).then_inc(stored_f[j], 16)

                load(0, 1)
                with sp.Fori(0, N // 2 - 1) as i:
                    for j in range(2):
                        tile(i, j, True)
                for j in range(2):
                    tile(N // 2 - 1, j, False)
                for j in range(2):
                    sp.wait_ge(stored_f[j], 16 * (N // 2))
                    sp.wait_ge(stored_t[j], 16 * (N // 2))

            @block.tensor
            def _(pe):
                pe.wait_ge(consts_in, 48)
                for m in range(N):
                    ins = pe.transpose(pt[:, 0, 0, m * CONV_W:(m + 1) * CONV_W], cw_rows[:, m * P:(m + 1) * P], ident[0:CONV_W, 0:CONV_W])
                ins.then_inc(cw_done, 1)
                pe.wait_ge(cw_ready, 1)

                def project(i, j, c, ks=range(KD)):
                    if c == 0:
                        pe.wait_ge(*w_ready.now(i, j))
                    if ks[0] == 0:
                        pe.wait_ge(*raw_ready.last(i, j))
                    for k in ks:
                        for w, x in ((w_first, x_first), (w_first, x_rest), (w_rest, x_first)):
                            ins = pe.matmul(pp[:, c, :], w[:, j, k, :], x[:, k, c * 512:(c + 1) * 512],
                                            start=k == 0 and x is x_first and w is w_first, stop=k == KD - 1 and w is w_rest)
                    if ks[-1] == KD - 1:
                        ins.then_inc(projected[j], 1)

                def turn(i, j, c):
                    pe.wait_ge(*(tok_ready.now(i, j, c - TB + 1) if c >= TB else tok_ready.last(i, j)))
                    if c == 0:
                        pe.wait_ge(*silu_done.now(i, j))
                    for q in range(4):
                        ins = pe.transpose(pt[:, c % TB, q, :], act_out[:, (4 * c + q) * P:(4 * c + q + 1) * P], ident[:, :])
                    ins.then_inc(turned[j], 1)

                def turn_back(i, j, c):
                    pe.wait_ge(*tok_ready.now(i, j, c + 1))
                    pe.wait_ge(*(feat_ready.now(i, j, c) if c else feat_ready.last(i, j)))
                    for q in range(4):
                        ins = pe.transpose(pb[:, q, :], tok[:, j, 4 * c + q, :], ident[:, :])
                    ins.then_inc(returned[j], 1)

                def tile(i, j, last=False):
                    nxt = following(i, j)
                    if not last:
                        for c in range(3):
                            project(*nxt, c)
                    for c in range(TB):
                        turn(i, j, c)
                    if not last:
                        project(*nxt, 3)
                    turn(i, j, 3)
                    for c in range(C):
                        turn_back(i, j, c)

                for c in range(C):
                    pe.wait_ge(x_ready, 2 * (c + 1))
                    project(0, 0, c)
                rounds(pe, None, tile, N)

            @block.scalar
            def _(act):
                act.wait_ge(pads, 1)

                def round_weights(i, j):
                    act.wait_ge(*w_loaded.now(i, j))
                    act.wait_ge(*projected.before_last(i, j))
                    act.activation(w_first[:, j, :, :], w_blk[:, :, :], ACT.Copy).then_inc(w_rounded[j], 1)

                def round_x(n):
                    act.wait_ge(x_loaded[n % 3], 16 * (n // 3 + 1))
                    act.activation(piece(x_first, n), x_in[n % 3], ACT.Copy).then_inc(x_rounded, 1)

                def copy_raw(i, j, c):
                    act.wait_ge(*projected.now(i, j, c + 1))
                    act.wait_ge(*conv_done.before_last(i, j))
                    act.activation(raw[:, j, PAD + c * 512:PAD + (c + 1) * 512], pp[:, c, :], ACT.Copy).then_inc(raw_ready[j], 1)

                def tile(i, j, last=False):
                    m = i * 2 + j
                    if not last:
                        copy_raw(*following(i, j), 0)
                        copy_raw(*following(i, j), 1)
                    if not isinstance(i, int):
                        round_weights(i + 1, j)
                    act.wait_ge(*conv_done.now(i, j))
                    act.wait_ge(*turned.last(i, j))
                    act.activation(act_out[:, :], acc[:, :], ACT.Silu).then_inc(silu_done[j], 1)
                    act.wait_ge(*tok_ready.last(i, j))

                    def norms(c):
                        act.wait_ge(*turned.now(i, j, c + 1))
                        for q in range(4):
                            n = 4 * c + q
                            ins = act.activation(act_out[:, n * P:(n + 1) * P], pt[:, c % TB, q, :], ACT.Square, accum_out=inv[:, 0, n:n + 1])
                        ins.then_inc(summed[j], 1)
                        act.wait_ge(*norm2_ready.now(i, j, c + 1))
                        act.activation(inv[:, 1, 4 * c:4 * c + 4], inv[:, 0, 4 * c:4 * c + 4], ACT.Sqrt).then_inc(rms_ready[j], 1)

                    for c in range(TB):
                        norms(c)
                        if c == 0 and not last:
                            copy_raw(*following(i, j), 2)

                    def copy_feat(c):
                        act.wait_ge(*returned.now(i, j, c + 1))
                        act.wait_ge(*stored_f.last(i, j))
                        act.activation(feat[:, c * 512:(c + 1) * 512], pb[:, :, :].rearrange("p q c -> p (q c)"), ACT.Copy).then_inc(feat_ready[j], 1)

                    if not last:
                        copy_raw(*following(i, j), 3)
                    norms(3)
                    for c in range(C):
                        copy_feat(c)

                round_weights(0, 0)
                for n in range(2 * C):
                    round_x(n)
                round_weights(0, 1)
                for c in range(C):
                    copy_raw(0, 0, c)
                rounds(act, None, tile, N)

            @block.vector
            def _(dve):
                own = Chain(dve, dve_chain, 2 * (CONV_W - 1 + C))
                dve.memset(raw[:, :, 0:PAD], 0.0)
                dve.memset(raw[:, :, SEQ + PAD:], 0.0).then_inc(pads, 1)
                dve.wait_ge(cw_done, 1)
                dve.tensor_copy(cw[:, :, :], pt[:, 0, 0, 0:N * CONV_W].rearrange("p (m w) -> p m w", w=CONV_W)).then_inc(cw_ready, 1)
                dve.wait_ge(cw_ready, 1)
                dve.wait_ge(consts_in, 48)

                def rest_of_weights(i, j):
                    dve.wait_ge(*w_rounded.now(i, j))
                    dve.tensor_tensor(w_rest[:, j, :, :], w_blk[:, :, :], w_first[:, j, :, :].bitcast(F32), ALU.subtract).then_inc(w_ready[j], 1)

                def rest_of_x(n):
                    dve.wait_ge(x_rounded, n + 1)
                    dve.tensor_tensor(piece(x_rest, n), x_in[n % 3], piece(x_first, n).bitcast(F32), ALU.subtract).then_inc(x_ready, 1)

                def convolve(i, j):
                    m = i * 2 + j
                    dve.wait_ge(*raw_ready.now(i, j))
                    dve.wait_ge(*silu_done.last(i, j))
                    for w in range(CONV_W):
                        c = cw[:, bass.ds(m, 1), w:w + 1].rearrange("p a b -> p (a b)")
                        x = raw[:, j, w:w + SEQ]
                        if w == 0:
                            own.link(dve.tensor_scalar(acc[:, :], x, c, None, ALU.mult))
                        elif w < CONV_W - 1:
                            own.link(dve.scalar_tensor_tensor(out=acc[:, :], in0=x, scalar=c, in1=acc[:, :], op0=ALU.mult, op1=ALU.add))
                        else:
                            dve.scalar_tensor_tensor(out=acc[:, :], in0=x, scalar=c, in1=acc[:, :], op0=ALU.mult, op1=ALU.add).then_inc(conv_done[j], 1)

                def tile(i, j, last=False):
                    m = i * 2 + j
                    dve.wait_ge(*stored_t.before_last(i, j))
                    dve.wait_ge(*returned.before_last(i, j))
                    for c in range(C):
                        part = slice(4 * c, 4 * c + 4)
                        col = lambda r: norm[:, r, bass.ds(m, 1), :].rearrange("p a b -> p (a b)")
                        dve.wait_ge(*summed.now(i, j, c + 1))
                        dve.tensor_scalar(inv[:, 0, part], inv[:, 0, part], col(0), col(1), ALU.mult, ALU.add).then_inc(norm2_ready[j], 1)
                        dve.wait_ge(*rms_ready.now(i, j, c + 1))
                        own.link(dve.reciprocal(inv[:, 2, part], inv[:, 1, part]))
                        dve.tensor_tensor(tok[:, j, part, :], pt[:, c % TB, :, :],
                                          inv[:, 2, part].unsqueeze(2).broadcast_to([P, 4, P]), ALU.mult).then_inc(tok_ready[j], 1)
                    if not isinstance(i, int):
                        rest_of_weights(i + 1, j)
                    if not last:
                        convolve(*following(i, j))

                rest_of_weights(0, 0)
                for n in range(2 * C):
                    rest_of_x(n)
                rest_of_weights(0, 1)
                convolve(0, 0)
                rounds(dve, own, tile, N)


def gated_delta(nc, top, dr, gates):
    H, W = GDN_HEADS, GDN_W
    LEVELS = 7
    CUM, BETA, GROW, TAIL, END, LOG = range(6)
    with ExitStack() as ctx:
        sb = lambda n, s, d=F32: ctx.enter_context(nc.sbuf_tensor(n, s, d))
        ps = lambda n, s, d=F32: ctx.enter_context(nc.psum_tensor(n, s, d))
        sem = lambda n: top.semaphore(n)
        both = lambda make: [make(d) for d in ("fwd", "bwd")]
        ct = lambda n, per=1: both(lambda d: Count(top, f"c_{n}_{d}", per))
        ident, ones = sb("ident_c", [P, P]), sb("ones_c", [P, P])
        upto = sb("upto", [P, 2, P])
        level = sb("level_masks", [P, 2, LEVELS, P])
        dt_rows, a_rows = sb("dt_rows", [P, 8]), sb("a_log_rows", [P, 8])
        pre = sb("gate_work", [P, 4, TILES, 8])
        logs = sb("log_decays", [P, 2, TILES, H])
        cums = sb("cum_decays", [P, 2, 2, TILES, H])
        tab = sb("gate_table", [P, TILES, 2, 6 * H])
        banks = [[ps(f"bank_{d}{n}", [P, H, P]) for n in "abcd"] for d in ("f", "b")]
        consts_in, prep = sem("c_consts"), sem("c_prep")
        prep_act, prep_pe = sem("c_prep_act"), sem("c_prep_pe")

        def turned(eng, i, j):
            return i * (-2) + (TILES - 1 - j)

        with nc.Block() as block:
            @block.sync
            def _(sp):
                sp.dma_start(ident[:, :], dr["c_ident"]).then_inc(consts_in, 16)
                sp.dma_start(ones[:, :], dr["c_ones"]).then_inc(consts_in, 16)
                sp.dma_start(upto[:, :, :], dr["c_upto"]).then_inc(consts_in, 16)
                sp.dma_start(level[:, :, :, :], dr["c_level"]).then_inc(consts_in, 16)
                sp.dma_start(dt_rows[:, :], dr["dt_bias"].broadcast_to([P, 8])).then_inc(consts_in, 16)
                sp.dma_start(a_rows[:, :], dr["a_log"].broadcast_to([P, 8])).then_inc(consts_in, 16)

            @block.vector
            def _(dve):
                own = Chain(dve, prep)
                dve.wait_ge(consts_in, 96)
                rows = lambda x: x[:, :].unsqueeze(1).broadcast_to([P, TILES, 8])
                own.link(dve.tensor_tensor(pre[:, 0], gates[:, :, 8:16], rows(dt_rows), ALU.add))
                dve.wait_ge(prep_act, 4)
                own.link(dve.scalar_tensor_tensor(out=pre[:, 2], in0=pre[:, 0], scalar=0.0, in1=pre[:, 1], op0=ALU.max, op1=ALU.add))
                own.link(dve.tensor_scalar(a_rows[:, :], a_rows[:, :], -1.0, None, ALU.mult))
                for d in range(2):
                    own.link(dve.tensor_tensor(logs[:, d], pre[:, 2, :, 4 * d:4 * d + 4],
                                               a_rows[:, 4 * d:4 * d + 4].unsqueeze(1).broadcast_to([P, TILES, H]), ALU.mult))
                dve.wait_ge(prep_pe, 1)
                for d in range(2):
                    g = banks[d][0][:, 0, 0:TILES * H].rearrange("p (t h) -> p t h", h=H)
                    end = banks[d][1][:, 0, 0:TILES * H].rearrange("p (t h) -> p t h", h=H)
                    col = lambda n: tab[:, :, d, n * H:(n + 1) * H]
                    own.mark(dve.tensor_copy(col(CUM), g))
                    own.mark(dve.tensor_copy(col(LOG), logs[:, d]))
                    own.mark(dve.tensor_copy(cums[:, d, 0], end))
                    own.wait()
                    own.mark(dve.tensor_tensor(cums[:, d, 1], cums[:, d, 0], col(CUM), ALU.subtract))
                own.wait()

            @block.scalar
            def _(act):
                act.wait_ge(prep, 1)
                act.activation(pre[:, 1], pre[:, 0], ACT.Abs).then_inc(prep_act, 1)
                act.wait_ge(prep_act, 1)
                act.activation(pre[:, 1], pre[:, 1], ACT.Exp, scale=-1.0).then_inc(prep_act, 1)
                act.wait_ge(prep_act, 2)
                act.activation(pre[:, 1], pre[:, 1], ACT.Ln, bias=1.0).then_inc(prep_act, 1)
                act.activation(a_rows[:, :], a_rows[:, :], ACT.Exp).then_inc(prep_act, 1)
                for d in range(2):
                    act.activation(tab[:, :, d, BETA * H:(BETA + 1) * H], gates[:, :, 4 * d:4 * d + 4], ACT.Sigmoid)
                act.wait_ge(prep, 13)
                for d in range(2):
                    col = lambda n: tab[:, :, d, n * H:(n + 1) * H]
                    act.activation(col(GROW), col(CUM), ACT.Exp)
                    act.activation(col(TAIL), cums[:, d, 1], ACT.Exp)
                    act.activation(col(END), cums[:, d, 0], ACT.Exp)

            @block.tensor
            def _(pe):
                pe.wait_ge(prep, 5)
                for d in range(2):
                    x = logs[:, d].rearrange("p t h -> p (t h)")
                    pe.matmul(banks[d][0][:, 0, 0:TILES * H], upto[:, d, :], x, start=True, stop=True)
                    ins = pe.matmul(banks[d][1][:, 0, 0:TILES * H], ones[:, :], x, start=True, stop=True)
                ins.then_inc(prep_pe, 1)

        k_ch, q_ch = sb("k_channels", [P, 2, 2, H, P]), sb("q_channels", [P, 2, 2, H, P])
        k_tok, v_tok = sb("k_tokens", [P, 2, 2, H, P]), sb("v_tokens", [P, 2, 2, H, P])
        big = lambda n: [sb(f"{n}_{d}", [P, H, P]) for d in ("f", "b")]
        pair = lambda n: [[sb(f"{n}_{d}{j}", [P, H, P]) for j in range(2)] for d in ("f", "b")]
        sc = sb("scalars", [P, 2, 2, 6, H])
        g_wide, decay, grow, lt = big("g_wide"), big("decay"), big("grow"), big("L_T")
        qd, kg, kt, at_ = pair("q_grown"), pair("k_grown"), pair("k_tail"), pair("attn_T")
        T, U, rest, vn, S = big("T"), big("U"), big("v_less_known"), big("v_new"), big("state")
        M = [sb(f"M_T_{d}", [P, LEVELS, H, P]) for d in ("f", "b")]
        Y, Y_last = big("Y"), big("Y_last")
        o_sb = sb("o_chunk", [P, 2, 2, H, P])
        loaded = both(lambda d: Event(top, f"c_loaded_{d}", 64))
        stored = both(lambda d: Event(top, f"c_stored_{d}", 16))
        state_ready = both(lambda d: Event(top, f"c_state_{d}"))
        scalars, gram, diff, exps = ct("scalars"), ct("gram", 3), ct("diff"), ct("exps", 2)
        k_tail, grown = ct("k_tail"), ct("grown", 2)
        masks = ct("masks", LEVELS + 1)
        products = ct("products", 2)
        y_pe, y_copied = ct("y_pe", LEVELS - 1), ct("y_copied", LEVELS - 1)
        tmt_pe, t_ready = ct("tmt_pe", LEVELS - 1), ct("t_ready", LEVELS - 1)
        u_first, u_last, umu_pe = ct("u_first"), ct("u_last"), ct("umu_pe")
        u_pe, u_copied = ct("u_pe", LEVELS - 2), ct("u_copied", LEVELS - 2)
        known_pe, rest_ready, vnew_pe, vnew, o_pe, o_copied, s_pe = (ct(x) for x in
            ("known_pe", "rest", "vnew_pe", "vnew", "o_pe", "o_copied", "s_pe"))
        cleared = sem("c_cleared")
        own_dve = sem("c_own_dve")
        wide = lambda x: x.unsqueeze(2).broadcast_to([P, H, P])
        heads = lambda m: m.unsqueeze(1).broadcast_to([P, H, P])

        def blocks(x, n, parity):
            return x.rearrange("p h (m two b) -> p (h m) two b", two=2, b=1 << n)[:, :, parity, :]

        WIDE = 2
        some_blocks = lambda x, n, parity: x if n <= WIDE else blocks(x, n, parity)

        def head_blocks(x, n, parity):
            return x if n <= WIDE else mask_blocks(x, n, parity)

        def mask_blocks(x, n, parity):
            return x.rearrange("p (m two b) -> p m two b", two=2, b=1 << n)[:, :, parity, :]

        with nc.Block() as block:
            @block.sync
            def _(sp):
                def load(i, j):
                    cs = (i * 2 + j, turned(sp, i, j))
                    for d in range(2):
                        c = cs[d]
                        sp.wait_ge(*state_ready[d].before_last(i, j))
                        for buf, h0 in ((q_ch, 0), (k_ch, H)):
                            sp.dma_start(buf[:, j, d], dr["feat"][h0:h0 + H, :, bass.ds(c * P, P)].rearrange("h p s -> p h s")).then_inc(loaded[d][j], 16)
                        for buf, c0 in ((k_tok, W), (v_tok, 2 * W)):
                            sp.dma_start(buf[:, j, d].rearrange("p h c -> p (h c)"), tile_rows(dr["tok"][:, c0:c0 + W], c)).then_inc(loaded[d][j], 16)

                def chunk(i, j, last=False):
                    if not last:
                        load(*following(i, j))
                    cs = (i * 2 + j, turned(sp, i, j))
                    for d in range(2):
                        c = cs[d]
                        sp.wait_ge(*o_copied[d].now(i * 2 + j))
                        sp.dma_start(tile_rows(dr["o_gdn"][d], c), o_sb[:, j, d].rearrange("p h c -> p (h c)")).then_inc(stored[d][j], 16)

                load(0, 0)
                rounds(sp, None, chunk)
                for d in range(2):
                    for j in range(2):
                        sp.wait_ge(stored[d][j], 16 * (TILES // 2))

            @block.gpsimd
            def _(pool):
                def prepare(i, j, last_t):
                    t = i * 2 + j
                    for d in range(2):
                        pool.wait_ge(*loaded[d].now(i, j))
                        pool.wait_ge(*scalars[d].now(t))
                        pool.wait_ge(*state_ready[d].before_last(i, j))
                        pool.tensor_tensor(kt[d][j][:, :, :], k_tok[:, j, d], wide(sc[:, d, j, TAIL, :]), ALU.mult).then_inc(k_tail[d].sem, 1)
                    for d in range(2):
                        pool.wait_ge(*exps[d].now(t, 1))
                        pool.tensor_tensor(decay[d][:, :, :], decay[d][:, :, :], heads(upto[:, d, :]), ALU.mult).then_inc(masks[d].sem, 1)
                        pool.wait_ge(*exps[d].now(t, 2))
                        pool.tensor_tensor(kg[d][j][:, :, :], k_ch[:, j, d], grow[d][:, :, :], ALU.mult).then_inc(grown[d].sem, 1)
                        pool.tensor_tensor(qd[d][j][:, :, :], q_ch[:, j, d], grow[d][:, :, :], ALU.mult).then_inc(grown[d].sem, 1)
                    for n in range(LEVELS):
                        for d in range(2):
                            pool.wait_ge(*products[d].now(t, 1))
                            if last_t is not None:
                                if n == 0:
                                    pool.wait_ge(*u_first[d].now(last_t))
                                    pool.wait_ge(*tmt_pe[d].now(last_t, 1))
                                else:
                                    pool.wait_ge(*y_pe[d].now(last_t, n))
                            b = 1 << n
                            cols = lambda x: x.rearrange("p h (m two b) -> p h m two b", two=2, b=b)[:, :, :, 1 - d, :]
                            mask = mask_blocks(level[:, d, n, :], n, 1 - d).unsqueeze(1).broadcast_to([P, H, P // (2 * b), b])
                            pool.tensor_tensor(cols(M[d][:, n]), cols(lt[d][:, :, :]), mask, ALU.mult).then_inc(masks[d].sem, 1)

                pool.wait_ge(cleared, 1)
                prepare(0, 0, None)
                rounds(pool, None, lambda i, j, last=False: None if last else prepare(*following(i, j), i * 2 + j))

            @block.scalar
            def _(act):
                def exponents(i, j, d):
                    t = i * 2 + j
                    act.wait_ge(*diff[d].now(t))
                    act.activation(decay[d][:, :, :], decay[d][:, :, :], ACT.Exp).then_inc(exps[d].sem, 1)
                    act.wait_ge(*grown[d].last(t))
                    act.activation(grow[d][:, :, :], banks[d][3][:, :, :], ACT.Exp).then_inc(exps[d].sem, 1)

                def chunk(i, j, last=False):
                    t = i * 2 + j
                    for n in range(1, LEVELS):
                        for d in range(2):
                            act.wait_ge(*y_pe[d].now(t, n))
                            if n == LEVELS - 1:
                                act.wait_ge(*umu_pe[d].last(t))
                            out = Y if n < LEVELS - 1 else Y_last
                            act.activation(some_blocks(out[d][:, :, :], n, d), some_blocks(banks[d][0][:, :, :], n, d), ACT.Copy).then_inc(y_copied[d].sem, 1)
                            if n > 1:
                                act.wait_ge(*u_pe[d].now(t, n - 1))
                                act.activation(U[d][:, :, :], banks[d][2][:, :, :], ACT.Copy).then_inc(u_copied[d].sem, 1)
                        if n in (2, 3) and not last:
                            exponents(*following(i, j), n - 2)
                    for d in range(2):
                        act.wait_ge(*o_pe[d].now(t))
                        act.wait_ge(*stored[d].before_last(i, j))
                        act.activation(o_sb[:, j, d], banks[d][3][:, :, :], ACT.Copy).then_inc(o_copied[d].sem, 1)

                act.wait_ge(cleared, 1)
                for d in range(2):
                    exponents(0, 0, d)
                rounds(act, None, chunk)

            @block.vector
            def _(dve):
                own = Chain(dve, own_dve, 2 * 2 * (1 + 3 * (H - 1)))
                for d in range(2):
                    dve.memset(S[d][:, :, :], 0.0)
                    dve.memset(Y_last[d][:, :, :], 0.0)
                    ins = dve.memset(M[d][:, :, :, :], 0.0)
                ins.then_inc(cleared, 1)

                def take_scalars(i, j):
                    cs = (i * 2 + j, turned(dve, i, j))
                    for d in range(2):
                        row = tab[:, bass.ds(cs[d], 1), d, :].rearrange("p a w -> p (a w)")
                        dve.wait_ge(*state_ready[d].before_last(i, j))
                        own.link(dve.tensor_copy(sc[:, d, j, :, :].rearrange("p n h -> p (n h)"), row))
                        dve.tensor_copy(g_wide[d][:, :, :], wide(sc[:, d, j, LOG, :])).then_inc(scalars[d].sem, 1)

                def differences(i, j, d):
                    dve.wait_ge(*gram[d].now(i * 2 + j, 1))
                    for h in range(H):
                        ins = dve.tensor_scalar(decay[d][:, h, :], banks[d][3][:, h, :], sc[:, d, j, CUM, h:h + 1], 0.0, ALU.subtract, ALU.min)
                        if h < H - 1:
                            own.mark(ins)
                    ins.then_inc(diff[d].sem, 1)

                def lower(i, j, d):
                    t = i * 2 + j
                    dve.wait_ge(*masks[d].last(t))
                    dve.wait_ge(*masks[d].now(t, 1))
                    dve.wait_ge(*gram[d].now(t, 2))
                    for h in range(H):
                        ins = dve.scalar_tensor_tensor(out=lt[d][:, h, :], in0=banks[d][3][:, h, :], scalar=sc[:, d, j, BETA, h:h + 1],
                                                       in1=decay[d][:, h, :], op0=ALU.mult, op1=ALU.mult)
                        if h < H - 1:
                            own.mark(ins)
                    ins.then_inc(products[d].sem, 1)

                def attend(i, j, d):
                    dve.wait_ge(*gram[d].now(i * 2 + j, 3))
                    dve.tensor_tensor(at_[d][j][:, :, :], banks[d][3][:, :, :], decay[d][:, :, :], ALU.mult).then_inc(products[d].sem, 1)

                def first_level(t, d):
                    dve.wait_ge(*masks[d].now(t, 2))
                    dve.tensor_tensor(U[d][:, :, :], heads(ident[:, :]), M[d][:, 0], ALU.subtract).then_inc(u_first[d].sem, 1)
                    dve.wait_ge(*tmt_pe[d].now(t, 1))
                    dve.tensor_tensor(T[d][:, :, :], heads(ident[:, :]), banks[d][1][:, :, :], ALU.subtract).then_inc(t_ready[d].sem, 1)

                def chunk(i, j, last=False):
                    t = i * 2 + j
                    nxt = following(i, j)
                    if not last:
                        take_scalars(*nxt)
                    for n in range(1, LEVELS):
                        for d in range(2):
                            if n < LEVELS - 1:
                                dve.wait_ge(*t_ready[d].now(t, n))
                                dve.wait_ge(*tmt_pe[d].now(t, n + 1))
                                x = blocks(T[d][:, :, :], n, d)
                                dve.tensor_tensor(x, x, blocks(banks[d][1][:, :, :], n, d), ALU.subtract).then_inc(t_ready[d].sem, 1)
                            else:
                                dve.wait_ge(*umu_pe[d].now(t))
                                x = blocks(U[d][:, :, :], n, 1 - d)
                                dve.tensor_tensor(x, x, blocks(banks[d][2][:, :, :], n, 1 - d), ALU.subtract).then_inc(u_last[d].sem, 1)
                        if not last:
                            if n in (1, 2):
                                differences(*nxt, n - 1)
                            if n in (4, 5):
                                lower(*nxt, n - 4)
                            if n == 5:
                                attend(*nxt, 0)
                    for d in range(2):
                        dve.wait_ge(*known_pe[d].now(t))
                        dve.tensor_tensor(rest[d][:, :, :], v_tok[:, j, d], banks[d][0][:, :, :], ALU.subtract).then_inc(rest_ready[d].sem, 1)
                    if not last:
                        attend(*nxt, 1)
                    for d in range(2):
                        dve.wait_ge(*vnew_pe[d].now(t))
                        dve.tensor_tensor(vn[d][:, :, :], banks[d][1][:, :, :], wide(sc[:, d, j, BETA, :]), ALU.mult).then_inc(vnew[d].sem, 1)
                    if not last:
                        for d in range(2):
                            first_level(nxt[0] * 2 + nxt[1], d)
                    for d in range(2):
                        dve.wait_ge(*s_pe[d].now(t))
                        for h in range(H):
                            ins = dve.scalar_tensor_tensor(out=S[d][:, h, :], in0=S[d][:, h, :], scalar=sc[:, d, j, END, h:h + 1],
                                                           in1=banks[d][2][:, h, :], op0=ALU.mult, op1=ALU.add)
                            if h < H - 1:
                                own.mark(ins)
                        ins.then_inc(state_ready[d][j], 1)

                take_scalars(0, 0)
                for step in (differences, lower, attend):
                    for d in range(2):
                        step(0, 0, d)
                for d in range(2):
                    first_level(0, d)
                rounds(dve, own, chunk)

            @block.tensor
            def _(pe):
                mm = pe.matmul
                A, B, C, D = zip(*banks)

                def each_head(f):
                    for h in range(H):
                        ins = f(h)
                    return ins

                def sums(i, j, d, last_t):
                    pe.wait_ge(*scalars[d].now(i * 2 + j))
                    if last_t is not None:
                        pe.wait_ge(*o_copied[d].last(last_t))
                    each_head(lambda h: mm(D[d][:, h, :], g_wide[d][:, h, :], upto[:, d, :], start=True, stop=True)).then_inc(gram[d].sem, 1)

                def keys_keys(i, j, d):
                    pe.wait_ge(*loaded[d].now(i, j))
                    pe.wait_ge(*exps[d].now(i * 2 + j, 2))
                    each_head(lambda h: mm(D[d][:, h, :], k_ch[:, j, d, h, :], k_ch[:, j, d, h, :], start=True, stop=True)).then_inc(gram[d].sem, 1)

                def keys_queries(i, j, d):
                    pe.wait_ge(*products[d].now(i * 2 + j, 1))
                    each_head(lambda h: mm(D[d][:, h, :], k_ch[:, j, d, h, :], q_ch[:, j, d, h, :], start=True, stop=True)).then_inc(gram[d].sem, 1)

                def first_level(t, d):
                    pe.wait_ge(*masks[d].now(t, 2))
                    each_head(lambda h: pe.transpose(B[d][:, h, :], M[d][:, 0, h, :], ident[:, :])).then_inc(tmt_pe[d].sem, 1)

                def m_t(t, n, d):
                    pe.wait_ge(*masks[d].now(t, n + 2))
                    pe.wait_ge(*t_ready[d].now(t, n))
                    each_head(lambda h: mm(head_blocks(A[d][:, h, :], n, d), M[d][:, n, h, :], head_blocks(T[d][:, h, :], n, d),
                                           start=True, stop=True)).then_inc(y_pe[d].sem, 1)

                def t_turned(t, n, d):
                    pe.wait_ge(*t_ready[d].now(t, n))
                    if n > 2:
                        pe.wait_ge(*u_copied[d].now(t, n - 2))
                    each_head(lambda h: pe.transpose(C[d][:, h, :], T[d][:, h, :], ident[:, :])).then_inc(u_pe[d].sem, 1)

                def t_m_t(t, n, d):
                    pe.wait_ge(*y_copied[d].now(t, n))
                    pe.wait_ge(*(u_first[d].now(t) if n == 1 else u_copied[d].now(t, n - 1)))
                    each_head(lambda h: mm(head_blocks(B[d][:, h, :], n, d), U[d][:, h, :], head_blocks(Y[d][:, h, :], n, d),
                                           start=True, stop=True)).then_inc(tmt_pe[d].sem, 1)

                def t_m_t_turned(t, d):
                    pe.wait_ge(*y_copied[d].now(t))
                    pe.wait_ge(*u_copied[d].now(t))
                    each_head(lambda h: mm(head_blocks(C[d][:, h, :], LEVELS - 1, 1 - d), Y_last[d][:, h, :],
                                           head_blocks(U[d][:, h, :], LEVELS - 1, 1 - d), start=True, stop=True)).then_inc(umu_pe[d].sem, 1)

                def chunk(i, j, last=False):
                    t = i * 2 + j
                    nxt = following(i, j)
                    for n in range(1, LEVELS):
                        for d in range(2):
                            m_t(t, n, d)
                            if n == 2:
                                pe.wait_ge(*state_ready[d].last(i, j))
                            if n > 1:
                                t_turned(t, n, d)
                        if n < LEVELS - 1:
                            for d in range(2):
                                t_m_t(t, n, d)
                        if not last:
                            if n in (1, 2):
                                sums(*nxt, n - 1, t)
                            if n in (3, 4):
                                keys_keys(*nxt, n - 3)
                            if n in (5, 6):
                                keys_queries(*nxt, n - 5)
                    for d in range(2):
                        t_m_t_turned(t, d)
                        pe.wait_ge(*grown[d].now(t))
                        each_head(lambda h: mm(A[d][:, h, :], kg[d][j][:, h, :], S[d][:, h, :], start=True, stop=True)).then_inc(known_pe[d].sem, 1)
                    for d in range(2):
                        pe.wait_ge(*u_last[d].now(t))
                        pe.wait_ge(*rest_ready[d].now(t))
                        each_head(lambda h: mm(B[d][:, h, :], U[d][:, h, :], rest[d][:, h, :], start=True, stop=True)).then_inc(vnew_pe[d].sem, 1)
                    for d in range(2):
                        pe.wait_ge(*vnew[d].now(t))
                        if not last:
                            first_level(nxt[0] * 2 + nxt[1], d)
                        pe.wait_ge(*k_tail[d].now(t))
                        pe.wait_ge(*(products[d].now(t) if last else products[d].now(nxt[0] * 2 + nxt[1])))
                        for h in range(H):
                            mm(D[d][:, h, :], qd[d][j][:, h, :], S[d][:, h, :], start=True, stop=False)
                            ins = mm(D[d][:, h, :], at_[d][j][:, h, :], vn[d][:, h, :], start=False, stop=True)
                        ins.then_inc(o_pe[d].sem, 1)
                        each_head(lambda h: mm(C[d][:, h, :], kt[d][j][:, h, :], vn[d][:, h, :], start=True, stop=True)).then_inc(s_pe[d].sem, 1)

                pe.wait_ge(cleared, 1)
                for d in range(2):
                    sums(0, 0, d, None)
                for d in range(2):
                    keys_keys(0, 0, d)
                for d in range(2):
                    keys_queries(0, 0, d)
                for d in range(2):
                    first_level(0, d)
                rounds(pe, None, chunk)


def attention(nc, top, dr, w_out):
    H, K = ATT_HEADS, KV_HEADS
    C = SEQ // 512
    SCALE = ATT_D ** -0.5
    PAIRS = H // 2
    HALF = ATT_D
    with ExitStack() as ctx:
        sb = lambda n, s, d=F32: ctx.enter_context(nc.sbuf_tensor(n, s, d))
        ps = lambda n, s, d=F32: ctx.enter_context(nc.psum_tensor(n, s, d))
        sem = lambda n: top.semaphore(n)
        ident = sb("ident_d", [P, P])
        v_parts = sb("v_parts", [P, TILES, K, P], F32R)
        fold = sb("two_identities", [P, ATT_D])
        kT = sb("kT", [P, K, 2, SEQ], F32R)
        sc = ps("scores", [P, C, 512])
        consts_in = sem("d_consts")
        q_tok = sb("q_tokens", [P, 2, H, 2, ATT_D])
        qT = sb("qT_tile", [P, 2, H, P], F32R)
        pT = sb("probs_T", [P, 2, 2, TILES, 2, P], F32R)
        q_loaded = Event(top, "d_q_loaded", 32)

        def load_queries(eng, i, j):
            for half in range(2):
                eng.dma_start(q_tok[:, j, :, half, :], tile_rows(dr["qk"], i * 2 + j)[:, 0:H * ATT_D].rearrange("p (h d) -> p h d", h=H)).then_inc(q_loaded[j], 16)

        with ExitStack() as pre:
            k_in = pre.enter_context(nc.sbuf_tensor("k_in", [P, TILES, K, 2, ATT_D], F32))
            v_in = pre.enter_context(nc.sbuf_tensor("v_in", [P, TILES, K, ATT_D], F32))
            v_first = sem("d_v_first")
            sc2 = pre.enter_context(nc.psum_tensor("turned_k", [P, C, 512], F32))
            turned_k = (sc, sc2)
            k_turned, k_first = sem("d_k_turned"), sem("d_k_first")
            banks = lambda x: x.rearrange("p (c n) -> p c n", c=C)

            with nc.Block() as block:
                @block.sync
                def _(sp):
                    sp.dma_start(ident[:, :], dr["c_ident"]).then_inc(consts_in, 16)
                    k = dr["qk"][:, H * ATT_D:].rearrange("(t p) (g d) -> p t g d", p=P, g=K)
                    for half in range(2):
                        for g in range(K):
                            sp.dma_start(k_in[:, :, g, half, :], k[:, :, g, :]).then_inc(consts_in, 16)
                    sp.dma_start(v_in[:, :, :, :], dr["v"].rearrange("(t p) (g d) -> p t g d", p=P, g=K)).then_inc(consts_in, 16)
                    load_queries(sp, 0, 0)

                @block.gpsimd
                def _(pool):
                    pool.memset(pT[:, 1].bitcast(F32), 0.0)

                @block.tensor
                def _(pe):
                    pe.wait_ge(consts_in, 16 * 6)
                    for g in range(K):
                        for t in range(TILES):
                            ins = pe.transpose(turned_k[g][:, t // 4, (t % 4) * P:(t % 4 + 1) * P], k_in[:, t, g].rearrange("p a d -> p (a d)"), ident[:, :])
                        ins.then_inc(k_turned, 1)

                @block.scalar
                def _(act):
                    act.wait_ge(consts_in, 16 * 6)
                    by_head = lambda x: x.rearrange("p t g d -> p (t g) d")
                    act.activation(by_head(v_parts[:, :, :, :])[:, :, 0:ATT_D], by_head(v_in[:, :, :, :]), ACT.Copy).then_inc(v_first, 1)
                    for g in range(K):
                        act.wait_ge(k_turned, g + 1)
                        act.activation(banks(kT[:, g, 0, :]), turned_k[g][:, :, :], ACT.Copy).then_inc(k_first, 1)

                @block.vector
                def _(dve):
                    dve.wait_ge(consts_in, 16 * 6)
                    dve.tensor_tensor(fold[:, :], ident[:, 0:ATT_D], ident[:, ATT_D:], ALU.add)
                    dve.wait_ge(v_first, 1)
                    by_head = lambda x: x.rearrange("p t g d -> p (t g) d")
                    v_both = by_head(v_parts[:, :, :, :])
                    dve.tensor_tensor(v_both[:, :, ATT_D:], by_head(v_in[:, :, :, :]), v_both[:, :, 0:ATT_D].bitcast(F32), ALU.subtract)
                    for g in range(K):
                        dve.wait_ge(k_first, g + 1)
                        dve.tensor_tensor(banks(kT[:, g, 1, :]), turned_k[g][:, :, :], banks(kT[:, g, 0, :].bitcast(F32)), ALU.subtract)

        TB = 2
        peak = sb("row_max", [P, 2, C])
        bias = sb("minus_max", [P, 2, 2])
        prob = sb("probs", [P, 2, SEQ])
        row_sum = sb("row_sums", [P, 2, H, C])
        over = sb("over_sum", [P, 2, 2])
        o_turned = sb("o_by_channel", [P, 2 * P])
        o_out = sb("o_tile", [P, 2, H * ATT_D])
        tr = ps("probs_turned", [P, TB, 4, P])
        po, pf = ps("pv", [P, 512]), ps("pv_folded", [P, 512])
        stored = Event(top, "d_stored", 16)
        ct = lambda n, per=1: Count(top, f"d_{n}", per)
        scored, peak_ready, exped, turned = ct("scored", C), ct("peak_ready"), ct("exped", C), ct("turned", C)
        first_ready, parts_ready = ct("first_ready", C), ct("parts_ready", C)
        q_turned, q_first, q_ready = ct("q_turned", 2), ct("q_first", 2), ct("q_ready", 2)
        weighed, o_copied, folded, finished = (sem(f"d_{n}") for n in ("weighed", "o_copied", "folded", "finished"))
        w_out_in, passed = sem("d_w_out_in"), sem("d_passed")
        own_dve, blank_set = sem("d_own_dve"), sem("d_blank_set")

        pair = lambda i, j, h: (i * 2 + j) * PAIRS + h // 2
        part_of = lambda h, part, c: pT[:, h // 2 % 2, part, 4 * c:4 * c + 4, h % 2, :]

        batch = lambda b: slice(b * H // 2, (b + 1) * H // 2)
        tile_no = lambda i, j: i * 2 + j

        def steps(i, j, last):
            for h in range(H):
                nxt = (h + 1, j) if h < H - 1 else (0, 1 - j)
                yield (i * 2 + j) * H + h, h, None if last and h == H - 1 else nxt

        with nc.Block() as block:
            @block.sync
            def _(sp):
                def tile(i, j, last=False):
                    if not last:
                        sp.wait_ge(*q_turned.last(tile_no(i, j)))
                        load_queries(sp, *following(i, j))

                sp.dma_start(w_out[:, :, :], dr["w_out"].rearrange("(k p) n -> p k n", p=P)).then_inc(w_out_in, 16)
                rounds(sp, None, tile)
                sp.wait_ge(w_out_in, 16)

            @block.gpsimd
            def _(pool):
                with pool.Fori(0, TILES // 2) as i:
                    for j in range(2):
                        pool.wait_ge(finished, pair(i, j, H - 1) + 3)
                        pool.sem_inc(passed, 1)
                        pool.dma_start(tile_rows(dr["o_att"], i * 2 + j), o_out[:, j, :]).then_inc(stored[j], 16)
                for j in range(2):
                    pool.wait_ge(stored[j], 16 * (TILES // 2))

            @block.tensor
            def _(pe):
                def score(n, h, j, c, free):
                    if free is not None:
                        pe.wait_ge(exped.sem, free)
                    for part in range(2):
                        ins = pe.matmul(sc[:, c, :], qT[:, j, h, :], kT[:, h // GROUP, part, c * 512:(c + 1) * 512], start=part == 0, stop=part == 1)
                    ins.then_inc(scored.sem, 1)

                def turn_queries(i, j, b):
                    pe.wait_ge(*q_loaded.now(i, j))
                    for x in range(H // 2):
                        ins = pe.transpose(pf[:, x * P:(x + 1) * P], q_tok[:, j, b * H // 2 + x].rearrange("p a d -> p (a d)"), ident[:, :])
                    ins.then_inc(q_turned.sem, 1)

                def turn(n, h, c):
                    pe.wait_ge(*(parts_ready.now(n, c - TB + 1) if c >= TB else parts_ready.last(n)))
                    pe.wait_ge(*exped.now(n, c + 1))
                    for q in range(4):
                        ins = pe.transpose(tr[:, c % TB, q, :], prob[:, h % 2, (4 * c + q) * P:(4 * c + q + 1) * P], ident[:, :])
                    ins.then_inc(turned.sem, 1)

                HALF_KEYS = TILES // 2

                def weigh(m, p, half, some=range(HALF_KEYS)):
                    if half == 0 and some[0] == 0:
                        pe.wait_ge(o_copied, p + 2)
                    for t in (half * HALF_KEYS + x for x in some):
                        for part in range(2):
                            ins = pe.matmul(po[:, 0:2 * P], v_parts[:, t, 2 * m // GROUP, :], pT[:, m % 2, part, t, :, :].rearrange("p a b -> p (a b)"),
                                            start=t == 0 and part == 0, stop=t == TILES - 1 and part == 1)
                    if some[-1] == HALF_KEYS - 1:
                        ins.then_inc(weighed, 1)

                def add_parts(p):
                    pe.wait_ge(o_copied, p + 3)
                    pe.wait_ge(finished, p + 2)
                    for x in range(2):
                        ins = pe.matmul(pf[:, x * ATT_D:(x + 1) * ATT_D], o_turned[:, x * P:(x + 1) * P], fold[:, :], start=True, stop=True)
                    ins.then_inc(folded, 1)

                def tile(i, j, last=False):
                    for n, h, nxt in steps(i, j, last):
                        if nxt and nxt[0] == 0:
                            pe.wait_ge(*q_ready.now(tile_no(*following(i, j))))
                        p = pair(i, j, h)
                        some = lambda a, b: weigh((h // 2 - 1) % PAIRS, p - 1, h % 2, range(a, b))
                        ahead = lambda c: score(n + 1, *nxt, c, n * C + c + 1) if nxt else None
                        ahead(0)
                        turn(n, h, 0)
                        ahead(1)
                        turn(n, h, 1)
                        ahead(2)
                        if h % 2 == 0:
                            pe.wait_ge(*parts_ready.last(n))
                        some(0, 1)
                        ahead(3)
                        some(1, 2)
                        if h in (3, 5) and not last:
                            pe.wait_ge(finished, p + 1)
                            turn_queries(*following(i, j), (h - 3) // 2)
                        turn(n, h, 2)
                        some(2, 4)
                        turn(n, h, 3)
                        if h % 2 == 0:
                            if h in (4, 6) and not last:
                                pe.wait_ge(*q_ready.now(tile_no(*following(i, j)), h // 2 - 1))
                            add_parts(p - 2)
                        some(4, 8)

                for b in range(2):
                    if b:
                        pe.wait_ge(*q_ready.now(0, b))
                    turn_queries(0, 0, b)
                pe.wait_ge(*q_ready.now(0))
                for c in range(C):
                    score(0, 0, 0, c, None)
                pe.wait_ge(blank_set, 1)
                rounds(pe, None, tile)
                end = TILES * PAIRS
                add_parts(end - 2)
                pe.wait_ge(*parts_ready.last(TILES * H))
                for half in range(2):
                    weigh(PAIRS - 1, end - 1, half)
                add_parts(end - 1)

            @block.vector
            def _(dve):
                own = Chain(dve, own_dve, 2 * (H * (C + 1) + PAIRS * 2))

                def peak_of(n, h, c):
                    dve.wait_ge(*scored.now(n, c + 1))
                    own.mark(dve.tensor_reduce(peak[:, h % 2, c:c + 1], sc[:, c, :], AX.X, ALU.max))

                def minus_max(n, h):
                    b = h % 2
                    own.wait()
                    own.link(dve.tensor_reduce(bias[:, b, 0:1], peak[:, b, :], AX.X, ALU.max))
                    dve.tensor_scalar(bias[:, b, 1:2], bias[:, b, 0:1], -SCALE, None, ALU.mult).then_inc(peak_ready.sem, 1)

                def rest_of(n, h, c):
                    dve.wait_ge(*first_ready.now(n, c + 1))
                    dve.tensor_tensor(part_of(h, 1, c), tr[:, c % TB, :, :], part_of(h, 0, c).bitcast(F32), ALU.subtract).then_inc(parts_ready.sem, 1)

                def rest_of_queries(i, j, b):
                    dve.wait_ge(*q_first.now(tile_no(i, j), b + 1))
                    low = qT[HALF:P, j, batch(b), :]
                    dve.tensor_tensor(low, pf[HALF:P, :].rearrange("p (h c) -> p h c", h=H // 2), low.bitcast(F32), ALU.subtract).then_inc(q_ready.sem, 1)

                def finish(p, m, j, i):
                    h = 2 * m
                    own.link(dve.tensor_reduce(over[:, 0, :], row_sum[:, j, h:h + 2, :], AX.X, ALU.add))
                    own.link(dve.reciprocal(over[:, 1, :], over[:, 0, :]))
                    dve.wait_ge(folded, p + 3)
                    if m == 0:
                        dve.wait_ge(*stored.before_last(i, j))
                    dve.tensor_tensor(o_out[:, j, h * ATT_D:(h + 2) * ATT_D].rearrange("p (h d) -> p h d", h=2),
                                      pf[:, 0:2 * ATT_D].rearrange("p (h d) -> p h d", h=2),
                                      over[:, 1, :].unsqueeze(2).broadcast_to([P, 2, ATT_D]), ALU.mult).then_inc(finished, 1)

                def tile(i, j, last=False):
                    for n, h, nxt in steps(i, j, last):
                        if h in (4, 6) and not last:
                            rest_of_queries(*following(i, j), h // 2 - 2)
                        if nxt:
                            peak_of(n + 1, nxt[0], 0)
                            peak_of(n + 1, nxt[0], 1)
                        rest_of(n, h, 0)
                        if nxt:
                            peak_of(n + 1, nxt[0], 2)
                        rest_of(n, h, 1)
                        if nxt:
                            peak_of(n + 1, nxt[0], 3)
                            minus_max(n + 1, nxt[0])
                        rest_of(n, h, 2)
                        rest_of(n, h, 3)
                        if h % 2 == 0:
                            m = (h // 2 - 2) % PAIRS
                            finish(pair(i, j, h) - 2, m, j if h >= 4 else 1 - j, i)

                dve.memset(po[:, :], 0.0)
                dve.memset(row_sum[:, :, :, :], 1.0).then_inc(blank_set, 1)
                dve.wait_ge(blank_set, 1)
                for b in range(2):
                    rest_of_queries(0, 0, b)
                for c in range(C):
                    peak_of(0, 0, c)
                minus_max(0, 0)
                rounds(dve, own, tile)
                for m in (PAIRS - 2, PAIRS - 1):
                    finish((TILES - 1) * PAIRS + m, m, 1, TILES // 2 - 1)

            @block.scalar
            def _(act):
                def exp_of(n, h, j, c, free=None):
                    act.wait_ge(*peak_ready.now(n))
                    if free is not None:
                        act.wait_ge(turned.sem, free)
                    act.activation(prob[:, h % 2, c * 512:(c + 1) * 512], sc[:, c, :], ACT.Exp, bias=bias[:, h % 2, 1:2],
                                   scale=SCALE, accum_out=row_sum[:, j, h, c:c + 1]).then_inc(exped.sem, 1)

                def first_of(n, h, c, p):
                    act.wait_ge(*turned.now(n, c + 1))
                    if c == 0:
                        act.wait_ge(weighed, 2 * p)
                    act.activation(part_of(h, 0, c), tr[:, c % TB, :, :], ACT.Copy).then_inc(first_ready.sem, 1)

                def first_of_queries(i, j, b):
                    act.wait_ge(*q_turned.now(tile_no(i, j), b + 1))
                    act.activation(qT[:, j, batch(b), :], pf[:, :].rearrange("p (h c) -> p h c", h=H // 2), ACT.Copy).then_inc(q_first.sem, 1)

                def copy_output(p):
                    act.wait_ge(weighed, 2 * (p + 2))
                    act.wait_ge(folded, p + 2)
                    act.activation(o_turned[:, :], po[:, 0:2 * P], ACT.Copy).then_inc(o_copied, 1)

                def tile(i, j, last=False):
                    for n, h, nxt in steps(i, j, last):
                        p = pair(i, j, h)
                        if h % 2 == 0:
                            copy_output(p - 2)
                        for c in range(C):
                            if c == TB and h in (3, 5) and not last:
                                first_of_queries(*following(i, j), (h - 3) // 2)
                            first_of(n, h, c, p)
                        for c in range(C):
                            if nxt:
                                exp_of(n + 1, *nxt, c, n * C)

                for b in range(2):
                    first_of_queries(0, 0, b)
                act.wait_ge(blank_set, 1)
                for c in range(C):
                    exp_of(0, 0, 0, c)
                rounds(act, None, tile)
                for p in (TILES * PAIRS - 2, TILES * PAIRS - 1):
                    copy_output(p)


def mix_out(nc, top, dr, logits, w_out, load_experts):
    H, W = GDN_HEADS, GDN_W
    NL = N_GROUPS + N_EXPERTS
    with ExitStack() as ctx:
        sb = lambda n, s, d=F32: ctx.enter_context(nc.sbuf_tensor(n, s, d))
        ps = lambda n, s, d=F32: ctx.enter_context(nc.psum_tensor(n, s, d))
        sem = lambda n: top.semaphore(n)
        ev = lambda n, per=1: Event(top, f"e_{n}", per)
        ident, eps = sb("ident_e", [P, P]), sb("eps_e", [P, 1])
        w_rt = sb("w_router", [P, KD, NL])
        nw = sb("norm_ffn_rows", [P, D_MODEL])
        gw = sb("gdn_norm_rows", [P, GDN_D])
        o_in = sb("o_both", [P, 2, 2, W])
        z_in = sb("z_in", [P, 2, W])
        a_in = sb("att_in", [P, 2, W])
        x_in = sb("x_in_e", [P, 2, D_MODEL])
        gn = sb("gdn_out", [P, 2, W])
        gsq = sb("gdn_squares", [P, W])
        gst = sb("gdn_stats", [P, 3, H])
        catT = sb("mixed_T", [P, 2, KD, P])
        x1 = sb("x1_tile", [P, 2, D_MODEL])
        sq = sb("squares_e", [P, D_MODEL])
        st = sb("stats_e", [P, 2, 3])
        h2 = sb("h2_tile", [P, 2, D_MODEL])
        hT = sb("h2_T", [P, KD, P])
        pc, po, ph, pl = ps("cat_turned", [P, KD, P]), ps("out_proj", [P, 2, 512]), ps("h2_turned", [P, KD, P]), ps("router", [P, NL])
        consts_in, late_in, eps_set, own_dve = sem("e_consts"), sem("e_late"), sem("e_eps"), sem("e_own_dve")
        o_loaded, x_loaded = ev("o_loaded", 64), ev("x_loaded", 16)
        g_sums, g_rms, g_ready, cat_turned, cat_ready = (ev(n) for n in ("g_sums", "g_rms", "g_ready", "cat_turned", "cat_ready"))
        mixed, x1_ready = ev("mixed", 2), ev("x1_ready", 2)
        x1_sum, x1_rms, h2_ready = (ev(n) for n in ("x1_sum", "x1_rms", "h2_ready"))
        h_turned, hT_ready, routed, kept = (ev(n) for n in ("h_turned", "hT_ready", "routed", "kept"))
        x1_stored, h2_stored = ev("x1_stored", 16), ev("h2_stored", 16)

        with nc.Block() as block:
            @block.sync
            def _(sp):
                def consts(dst, src):
                    sp.dma_start(dst, src).then_inc(consts_in, 16)

                def load(i, j):
                    t = i * 2 + j
                    sp.wait_ge(*g_ready.before_last(i, j))
                    sp.wait_ge(*cat_turned.before_last(i, j))
                    for d in range(2):
                        sp.dma_start(o_in[:, j, d, :], tile_rows(dr["o_gdn"][d], t)).then_inc(o_loaded[j], 16)
                    sp.dma_start(z_in[:, j, :], tile_rows(dr["z"], t)).then_inc(o_loaded[j], 16)
                    sp.dma_start(a_in[:, j, :], tile_rows(dr["o_att"], t)).then_inc(o_loaded[j], 16)
                    sp.wait_ge(*x1_ready.before_last(i, j))
                    sp.dma_start(x_in[:, j, :], tile_rows(dr["x"], t)).then_inc(x_loaded[j], 16)

                consts(ident[:, :], dr["c_ident"])
                consts(gw[:, :], dr["gdn_norm_w"].unsqueeze(0).broadcast_to([P, GDN_D]))
                load(0, 0)
                load(0, 1)
                for dst, src in ((nw[:, :], dr["norm_ffn_w"].unsqueeze(0).broadcast_to([P, D_MODEL])),
                                 (w_rt[:, :, 0:N_GROUPS], dr["w_router_group"].rearrange("(k p) n -> p k n", p=P)),
                                 (w_rt[:, :, N_GROUPS:], dr["w_router_expert"].rearrange("(k p) n -> p k n", p=P))):
                    sp.dma_start(dst, src, allow_slow_non_contiguous=True).then_inc(late_in, 16)
                load_experts(sp)

                def tile(i, j, last=False):
                    t = i * 2 + j
                    sp.wait_ge(*x1_ready.now(i, j))
                    sp.dma_start(tile_rows(dr["x1"], t), x1[:, j, :]).then_inc(x1_stored[j], 16)
                    if not isinstance(i, int):
                        load(i + 1, j)
                    sp.wait_ge(*h2_ready.now(i, j))
                    sp.dma_start(tile_rows(dr["h2"], t), h2[:, j, :]).then_inc(h2_stored[j], 16)

                rounds(sp, None, tile)
                for j in range(2):
                    sp.wait_ge(x1_stored[j], 16 * (TILES // 2))
                    sp.wait_ge(h2_stored[j], 16 * (TILES // 2))

            @block.scalar
            def _(act):
                act.wait_ge(eps_set, 1)

                def head_rms(i, j):
                    act.wait_ge(*g_sums.now(i, j))
                    act.activation(gst[:, 1, :], gst[:, 0, :], ACT.Sqrt, bias=eps[:, :], scale=1.0 / GDN_D).then_inc(g_rms[j], 1)

                def copy_cat(i, j):
                    act.wait_ge(*cat_turned.now(i, j))
                    act.wait_ge(*mixed.before_last(i, j))
                    act.activation(catT[:, j, :, :], pc[:, :, :], ACT.Copy).then_inc(cat_ready[j], 1)

                def tile(i, j, last=False):
                    t = i * 2 + j
                    act.wait_ge(*x1_ready.now(i, j))
                    act.wait_ge(*h2_ready.before_last(i, j))
                    act.activation(sq[:, :], x1[:, j, :], ACT.Square, accum_out=st[:, j, 0:1]).then_inc(x1_sum[j], 1)
                    act.wait_ge(*x1_sum.now(i, j))
                    act.activation(st[:, j, 1:2], st[:, j, 0:1], ACT.Sqrt, bias=eps[:, :], scale=1.0 / D_MODEL).then_inc(x1_rms[j], 1)
                    if not isinstance(i, int):
                        head_rms(i + 1, j)
                    act.wait_ge(*h_turned.now(i, j))
                    act.wait_ge(*routed.last(i, j))
                    act.activation(hT[:, :, :], ph[:, :, :], ACT.Copy).then_inc(hT_ready[j], 1)
                    if not isinstance(i, int):
                        copy_cat(i + 1, j)
                    act.wait_ge(*routed.now(i, j))
                    act.activation(at(logits, t), pl[:, :], ACT.Copy).then_inc(kept[j], 1)

                head_rms(0, 0)
                head_rms(0, 1)
                copy_cat(0, 0)
                copy_cat(0, 1)
                rounds(act, None, tile)

            @block.vector
            def _(dve):
                own = Chain(dve, own_dve, 2 * 6)
                dve.memset(eps[:, :], EPS).then_inc(eps_set, 1)

                def gdn_out(i, j):
                    heads = lambda x: x.rearrange("p (h d) -> p h d", h=H)
                    o = o_in[:, j, 0, :]
                    dve.wait_ge(*o_loaded.now(i, j))
                    own.link(dve.tensor_tensor(o, o, o_in[:, j, 1, :], ALU.add))
                    own.link(dve.tensor_tensor(gsq[:, :], o, o, ALU.mult))
                    dve.tensor_reduce(gst[:, 0, :], heads(gsq[:, :]), AX.X, ALU.add).then_inc(g_sums[j], 1)
                    own.mark(dve.tensor_tensor(heads(z_in[:, j, :]), heads(z_in[:, j, :]), gw[:, :].unsqueeze(1).broadcast_to([P, H, GDN_D]), ALU.mult))
                    dve.wait_ge(*g_rms.now(i, j))
                    own.link(dve.reciprocal(gst[:, 2, :], gst[:, 1, :]))
                    own.link(dve.tensor_tensor(heads(o), heads(o), gst[:, 2, :].unsqueeze(2).broadcast_to([P, H, GDN_D]), ALU.mult))
                    dve.wait_ge(*cat_turned.before_last(i, j))
                    dve.tensor_tensor(gn[:, j, :], o, z_in[:, j, :], ALU.mult).then_inc(g_ready[j], 1)

                def tile(i, j, last=False):
                    dve.wait_ge(*x_loaded.now(i, j))
                    dve.wait_ge(*x1_stored.before_last(i, j))
                    for half in range(2):
                        dve.wait_ge(*mixed.now(i, j, half + 1))
                        part = slice(half * 512, (half + 1) * 512)
                        dve.tensor_tensor(x1[:, j, part], x_in[:, j, part], po[:, half, :], ALU.add).then_inc(x1_ready[j], 1)
                    dve.wait_ge(*x1_rms.now(i, j))
                    own.link(dve.reciprocal(st[:, j, 2:3], st[:, j, 1:2]))
                    dve.wait_ge(*h2_stored.before_last(i, j))
                    dve.wait_ge(*h_turned.before_last(i, j))
                    dve.scalar_tensor_tensor(out=h2[:, j, :], in0=x1[:, j, :], scalar=st[:, j, 2:3], in1=nw[:, :], op0=ALU.mult, op1=ALU.mult).then_inc(h2_ready[j], 1)
                    if not isinstance(i, int):
                        gdn_out(i + 1, j)

                dve.wait_ge(consts_in, 32)
                gdn_out(0, 0)
                gdn_out(0, 1)
                dve.wait_ge(late_in, 48)
                rounds(dve, own, tile)

            @block.tensor
            def _(pe):
                pe.wait_ge(consts_in, 32)

                def turn_cat(i, j):
                    pe.wait_ge(*g_ready.now(i, j))
                    pe.wait_ge(*o_loaded.now(i, j))
                    pe.wait_ge(*cat_ready.last(i, j))
                    for k in range(KD):
                        src = gn[:, j, k * P:(k + 1) * P] if k < H else a_in[:, j, (k - H) * P:(k - H + 1) * P]
                        ins = pe.transpose(pc[:, k, :], src, ident[:, :])
                    ins.then_inc(cat_turned[j], 1)

                def mix(i, j, half, prev=None):
                    if half == 0:
                        pe.wait_ge(*cat_ready.now(i, j))
                    if prev:
                        pe.wait_ge(*x1_ready.now(*prev, half + 1))
                    for k in range(KD):
                        ins = pe.matmul(po[:, half, :], catT[:, j, k, :], w_out[:, k, half * 512:(half + 1) * 512], start=k == 0, stop=k == KD - 1)
                    ins.then_inc(mixed[j], 1)

                def tile(i, j, last=False):
                    nxt = following(i, j)
                    if not last:
                        mix(*nxt, 0, (i, j))
                    pe.wait_ge(*h2_ready.now(i, j))
                    pe.wait_ge(*hT_ready.last(i, j))
                    for k in range(KD):
                        ins = pe.transpose(ph[:, k, :], h2[:, j, k * P:(k + 1) * P], ident[:, :])
                    ins.then_inc(h_turned[j], 1)
                    if not last:
                        mix(*nxt, 1, (i, j))
                    if not isinstance(i, int):
                        turn_cat(i + 1, j)
                    pe.wait_ge(*hT_ready.now(i, j))
                    pe.wait_ge(*kept.last(i, j))
                    for k in range(KD):
                        ins = pe.matmul(pl[:, :], hT[:, k, :], w_rt[:, k, :], start=k == 0, stop=k == KD - 1)
                    ins.then_inc(routed[j], 1)

                turn_cat(0, 0)
                turn_cat(0, 1)
                mix(0, 0, 0)
                mix(0, 0, 1)
                pe.wait_ge(late_in, 48)
                rounds(pe, None, tile)


BT_SLOT, BT_EVEN, BT_ODD, BT_UPTO, BT_STORES = range(5)
BT_ROWS = 5
W_DMAS = 3 * 16


def route(nc, top, dr, logits, dest, gate, table):
    G, E, N = N_GROUPS, PER_GROUP, N_EXPERTS
    BIG = 1e30
    with ExitStack() as ctx:
        sb = lambda n, s, d=F32: ctx.enter_context(nc.sbuf_tensor(n, s, d))
        ps = lambda n, s, d=F32: ctx.enter_context(nc.psum_tensor(n, s, d))
        sem = lambda n: top.semaphore(n)
        iota, before, ones = sb("iota", [P, 64]), sb("before", [P, P]), sb("ones_f", [P, P])
        tokens = sb("token_ids", [P, TILES], I32)
        wide = [P, TILES, E]
        group_d, group_e, group_1 = sb("group_diff", [P, TILES, G]), sb("group_exp", [P, TILES, G]), sb("group_onehot", [P, TILES, G])
        group_p = sb("group_prob", [P, TILES])
        picked = sb("picked_products", [P, TILES, G, E])
        fine, fine_d, fine_e = sb("fine", wide), sb("fine_diff", wide), sb("fine_exp", wide)
        hot = [sb(f"expert_onehot{k}", wide) for k in range(TOP_K)]
        top_v = sb("top_values", [P, 4, TILES])
        col = sb("columns_f", [P, 4, TILES])
        work = sb("index_work", wide)
        OH = [sb(f"assigned{k}", [P, TILES, N]) for k in range(TOP_K)]
        cnt, pos = sb("assigned_both", [P, TILES, N]), sb("positions", [P, TILES, N])
        base = sb("tile_base", [P, TILES + 1, N])
        nb, nbi, incl = sb("expert_blocks", [P, N]), sb("expert_blocks_int", [P, N], I32), sb("blocks_upto", [P, N])
        start = sb("first_slot", [P, N])
        cmp = sb("block_compare", [1, N_BLOCKS, N])
        eb, ebi = sb("block_expert", [1, N_BLOCKS]), sb("block_expert_int", [1, 2, N_BLOCKS], I32)
        rank, tot = ps("rank_in_tile", [P, TILES, N]), ps("tile_totals", [P, TILES, N])
        consts_in, cleared, chain, act_done, counted = sem("f_consts"), sem("f_cleared"), sem("f_dve"), sem("f_act"), sem("f_counted")
        marks = {n: sem(f"f_{n}") for n in ("group_diff", "fine_diff", "counts", "dest")}
        scattered = [sem(f"f_scattered{k}") for k in range(2)]

        with nc.Block() as block:
            @block.sync
            def _(sp):
                for dst, src in ((iota[:, :], "c_iota"), (before[:, :], "c_before"), (ones[:, :], "c_ones"), (tokens[:, :], "c_tokens")):
                    sp.dma_start(dst, dr[src]).then_inc(consts_in, 16)
                sp.dma_start(dr["slot_token"], dr["c_slot0"]).then_inc(cleared, 16)

            @block.vector
            def _(dve):
                own = Chain(dve, chain)
                link = own.link
                tt, ts = dve.tensor_tensor, dve.tensor_scalar
                along = lambda x, n: x.unsqueeze(2).broadcast_to([P, TILES, n])
                numbers = lambda n: iota[:, 0:n].unsqueeze(1).broadcast_to([P, TILES, n])

                def first_hot(out, hits, n, c):
                    w = work[:, :, 0:n]
                    link(ts(w, numbers(n), -64.0, None, ALU.add))
                    link(tt(w, w, hits, ALU.mult))
                    link(dve.tensor_reduce(col[:, c, :], w, AX.X, ALU.min))
                    link(ts(w, numbers(n), -64.0, None, ALU.add))
                    link(tt(out, w, along(col[:, c, :], n), ALU.is_equal))

                dve.wait_ge(consts_in, 64)
                gl = logits[:, :, 0:G]
                link(dve.tensor_reduce(top_v[:, 0, :], gl, AX.X, ALU.max))
                tt(group_d[:, :, :], gl, along(top_v[:, 0, :], G), ALU.subtract).then_inc(marks["group_diff"], 1)
                dve.wait_ge(marks["group_diff"], 1)
                link(ts(group_1[:, :, :], group_d[:, :, :], 0.0, None, ALU.is_ge))
                first_hot(group_1[:, :, :], group_1[:, :, :], G, 0)
                link(tt(picked[:, :, :, :], logits[:, :, G:].rearrange("p t (g e) -> p t g e", g=G),
                        group_1[:, :, :].unsqueeze(3).broadcast_to([P, TILES, G, E]), ALU.mult))
                link(dve.tensor_reduce(fine[:, :, :], picked[:, :, :, :].rearrange("p t g e -> p t e g"), AX.X, ALU.add))
                link(dve.tensor_reduce(top_v[:, 1, :], fine[:, :, :], AX.X, ALU.max))
                tt(fine_d[:, :, :], fine[:, :, :], along(top_v[:, 1, :], E), ALU.subtract).then_inc(marks["fine_diff"], 1)
                dve.wait_ge(marks["fine_diff"], 1)
                link(ts(hot[0][:, :, :], fine_d[:, :, :], 0.0, None, ALU.is_ge))
                first_hot(hot[0][:, :, :], hot[0][:, :, :], E, 1)
                link(dve.scalar_tensor_tensor(out=fine[:, :, :], in0=hot[0][:, :, :], scalar=-BIG, in1=fine_d[:, :, :], op0=ALU.mult, op1=ALU.add))
                dve.tensor_reduce(top_v[:, 2, :], fine[:, :, :], AX.X, ALU.max).then_inc(marks["fine_diff"], 1)
                dve.wait_ge(marks["fine_diff"], 2)
                link(tt(hot[1][:, :, :], fine[:, :, :], along(top_v[:, 2, :], E), ALU.is_equal))
                first_hot(hot[1][:, :, :], hot[1][:, :, :], E, 2)
                for k in range(TOP_K):
                    own.mark(tt(OH[k][:, :, :].rearrange("p t (g e) -> p t g e", g=G), group_1[:, :, :].unsqueeze(3).broadcast_to([P, TILES, G, E]),
                                hot[k][:, :, :].unsqueeze(2).broadcast_to([P, TILES, G, E]), ALU.mult))
                own.wait()
                tt(cnt[:, :, :], OH[0][:, :, :], OH[1][:, :, :], ALU.add).then_inc(marks["counts"], 1)
                dve.wait_ge(act_done, 3)
                own.mark(dve.tensor_reduce(col[:, 0, :], group_e[:, :, :], AX.X, ALU.add))
                link(dve.tensor_reduce(col[:, 1, :], fine_e[:, :, :], AX.X, ALU.add))
                link(dve.reciprocal(col[:, 0:2, :], col[:, 0:2, :]))
                link(tt(col[:, 2, :], top_v[:, 3, :], col[:, 1, :], ALU.mult))
                link(tt(col[:, 3, :], col[:, 1, :], col[:, 2, :], ALU.add))
                link(dve.reciprocal(col[:, 3, :], col[:, 3, :]))
                link(tt(col[:, 3, :], col[:, 3, :], col[:, 0, :], ALU.mult))
                own.mark(tt(gate[:, 0, :], col[:, 1, :], col[:, 3, :], ALU.mult))
                own.mark(tt(gate[:, 1, :], col[:, 2, :], col[:, 3, :], ALU.mult))
                dve.wait_ge(counted, 1)
                link(dve.memset(base[:, 0, :], 0.0))
                for t in range(TILES):
                    link(tt(base[:, t + 1, :], base[:, t, :], tot[:, t, :], ALU.add))
                link(ts(nb[:, :], base[:, TILES, :], float(P - 1), None, ALU.add))
                link(dve.tensor_copy(nbi[:, :], nb[:, :]))
                link(ts(nbi[:, :], nbi[:, :], 7, None, ALU.logical_shift_right))
                link(dve.tensor_copy(nb[:, :], nbi[:, :]))
                link(dve.tensor_tensor_scan(incl[:, :], ones[:, 0:N], nb[:, :], 0.0, ALU.mult, ALU.add))
                link(tt(start[:, :], incl[:, :], nb[:, :], ALU.subtract))
                link(ts(start[:, :], start[:, :], float(P), None, ALU.mult))
                link(tt(pos[:, :, :], rank[:, :, :], base[:, 0:TILES, :], ALU.add))
                link(tt(pos[:, :, :], pos[:, :, :], start[:, :].unsqueeze(1).broadcast_to([P, TILES, N]), ALU.add))
                for k in range(TOP_K):
                    link(tt(OH[k][:, :, :], OH[k][:, :, :], pos[:, :, :], ALU.mult))
                    link(dve.tensor_reduce(col[:, k, :], OH[k][:, :, :], AX.X, ALU.add))
                dve.tensor_copy(dest[:, :, :], col[:, 0:TOP_K, :]).then_inc(marks["dest"], 1)
                link(tt(cmp[:, :, :], incl[0:1, :].unsqueeze(1).broadcast_to([1, N_BLOCKS, N]),
                        iota[0:1, 0:N_BLOCKS].unsqueeze(2).broadcast_to([1, N_BLOCKS, N]), ALU.is_le))
                link(dve.tensor_reduce(eb[:, :], cmp[:, :, :], AX.X, ALU.add))
                link(ts(eb[:, :], eb[:, :], float(N - 1), None, ALU.min))
                link(dve.tensor_copy(ebi[:, 0, :], eb[:, :]))
                own.mark(ts(table[:, BT_SLOT, :], ebi[:, 0, :], 1, None, ALU.bitwise_and))
                link(ts(ebi[:, 1, :], ebi[:, 0, :], 1, None, ALU.logical_shift_right))
                link(dve.tensor_copy(eb[:, :], ebi[:, 1, :]))
                link(ts(eb[:, :], eb[:, :], float(W_DMAS), float(W_DMAS), ALU.mult, ALU.add))
                link(dve.tensor_copy(table[:, BT_EVEN, :], eb[:, :]))
                own.mark(dve.tensor_copy(cmp[:, 0, :], ebi[:, 0, 0:N]))
                link(dve.tensor_copy(cmp[:, 1, :], ebi[:, 0, N:2 * N]))
                odd = cmp[:, 0:2, :].rearrange("o a b -> o (a b)")
                link(ts(odd, odd, 1.0, None, ALU.add))
                link(dve.tensor_copy(ebi[:, 1, :], odd))
                link(ts(ebi[:, 1, :], ebi[:, 1, :], 1, None, ALU.logical_shift_right))
                link(dve.tensor_copy(odd, ebi[:, 1, :]))
                link(ts(odd, odd, float(W_DMAS), None, ALU.mult))
                link(dve.tensor_copy(table[:, BT_ODD, :], odd))
                link(dve.tensor_copy(table[:, BT_UPTO, 0:N], incl[0:1, :]))
                for j in range(2):
                    link(ts(eb[:, j:j + 1], incl[0:1, N - 1:N], float(1 - j), None, ALU.add))
                link(dve.tensor_copy(ebi[:, 0, 0:2], eb[:, 0:2]))
                link(ts(ebi[:, 0, 0:2], ebi[:, 0, 0:2], 1, None, ALU.logical_shift_right))
                link(dve.tensor_copy(eb[:, 0:2], ebi[:, 0, 0:2]))
                link(ts(eb[:, 0:2], eb[:, 0:2], 16.0, None, ALU.mult))
                link(ts(eb[:, 2:3], incl[0:1, N - 1:N], -16.0, 16.0 * N_BLOCKS, ALU.mult, ALU.add))
                link(dve.tensor_copy(table[:, BT_STORES, 0:3], eb[:, 0:3]))

            @block.scalar
            def _(act):
                act.wait_ge(marks["group_diff"], 1)
                act.activation(group_e[:, :, :], group_d[:, :, :], ACT.Exp).then_inc(act_done, 1)
                act.wait_ge(marks["fine_diff"], 1)
                act.activation(fine_e[:, :, :], fine_d[:, :, :], ACT.Exp).then_inc(act_done, 1)
                act.wait_ge(marks["fine_diff"], 2)
                act.activation(top_v[:, 3, :], top_v[:, 2, :], ACT.Exp).then_inc(act_done, 1)

            @block.tensor
            def _(pe):
                pe.wait_ge(marks["counts"], 1)
                rows = cnt[:, :, :].rearrange("p t e -> p (t e)")
                pe.matmul(rank[:, :, :].rearrange("p t e -> p (t e)"), before[:, :], rows, start=True, stop=True)
                pe.matmul(tot[:, :, :].rearrange("p t e -> p (t e)"), ones[:, :], rows, start=True, stop=True).then_inc(counted, 1)

            @block.gpsimd
            def _(pool):
                pool.wait_ge(cleared, 16)
                pool.wait_ge(marks["dest"], 1)
                n = 0
                for t in range(TILES):
                    for k in range(TOP_K):
                        if n >= 2:
                            pool.wait_ge(scattered[n % 2], 16 * (n // 2))
                        pool.indirect_dma_start(dr["slot_token"], bass.IndirectOffsetOnAxis(ap=dest[:, k, t:t + 1], axis=0),
                                                tokens[:, t:t + 1], None).then_inc(scattered[n % 2], 16)
                        n += 1
                for x in range(2):
                    pool.wait_ge(scattered[x], 16 * (n // 2))


class ExpertWeights:

    def __init__(self, nc, ctx, top, dr):
        sb = lambda n, s: ctx.enter_context(nc.sbuf_tensor(n, s, F32))
        self.dr = dr
        self.gate, self.up = sb("w_gate_slots", [P, 2, KD * FF]), sb("w_up_slots", [P, 2, KD * FF])
        self.down = sb("w_down_slots", [P, 2, KF * D_MODEL])
        self.loaded = Event(top, "g_weights", W_DMAS)

    def load(self, sp, e, j):
        for buf, name, k in ((self.gate, "w_gate", KD), (self.up, "w_up", KD), (self.down, "w_down", KF)):
            src = self.dr[name][bass.ds(e, 1) if not isinstance(e, int) else slice(e, e + 1), :, :].rearrange("a (k p) n -> p (a k) n", p=P)
            sp.dma_start(buf[:, j, :].rearrange("p (k n) -> p k n", k=k), src).then_inc(self.loaded[j], 16)

    def load_first(self, sp):
        for e in range(2):
            self.load(sp, e, e)


def experts(nc, top, dr, table, weights):
    HALF = FF // 2
    KH = KF // 2
    with ExitStack() as ctx:
        sb = lambda n, s, d=F32: ctx.enter_context(nc.sbuf_tensor(n, s, d))
        ps = lambda n, s, d=F32: ctx.enter_context(nc.psum_tensor(n, s, d))
        sem = lambda n: top.semaphore(n)
        ev = lambda n, per=1: Event(top, f"g_{n}", per)
        wg, wu, wd, loaded = weights.gate, weights.up, weights.down, weights.loaded
        ident = sb("ident_g", [P, P])
        ids = sb("row_tokens", [P, 2, 1], I32)
        rows = sb("rows", [P, 2, D_MODEL])
        rowsT = sb("rows_T", [P, 2, KD, P])
        sg, hid, hidT = sb("silu_gate", [P, FF]), sb("hidden", [P, FF]), sb("hidden_T", [P, KF, P])
        y = sb("y_block", [P, 2, D_MODEL])
        zeros = sb("zeros_g", [P, D_MODEL])
        pt = ps("rows_turned", [P, KD, P])
        pg, ph = ps("gate_psum", [P, FF]), ps("hidden_turned", [P, KF, P])
        pu = ps("up_psum", [P, 2, 512])
        py = ps("down", [P, 2, 512])
        consts_in, zeros_set, zeroed, passed = sem("g_consts"), sem("g_zeros"), sem("g_zeroed"), sem("g_passed")
        sp_settled, act_settled = sem("g_sp_settled"), sem("g_act_settled")
        ids_in, gathered, turned, rowsT_ready = ev("ids", 16), ev("gathered", 16), ev("turned"), ev("rowsT")
        gated, silued, downed, stored = ev("gate"), ev("silu"), ev("down"), ev("stored", 16)
        upped, hid_ready, hid_turned, hidT_ready = (ev(n, 2) for n in ("up", "hid", "hid_turned", "hidT"))
        y_ready = Count(top, "g_y_ready")

        def block_loop(eng, body):
            count = eng.value_load(table[0:1, BT_UPTO, N_EXPERTS - 1:N_EXPERTS], min_val=1, max_val=N_BLOCKS)
            with eng.Fori(0, N_BLOCKS // 2) as i:
                for j in range(2):
                    with eng.If(i * 2 + j < count):
                        body(i, j)

        with nc.Block() as block:
            @block.sync
            def _(sp):
                sp.dma_start(ident[:, :], dr["c_ident"]).then_inc(consts_in, 16)

                count = sp.value_load(table[0:1, BT_UPTO, N_EXPERTS - 1:N_EXPERTS], min_val=1, max_val=N_BLOCKS)
                sp.wait_ge(zeros_set, 1)
                with sp.Fori(0, N_BLOCKS) as b:
                    with sp.If(b >= count):
                        sp.dma_start(tile_rows(dr["y"], b), zeros[:, :]).then_inc(zeroed, 16)
                with sp.Fori(1, N_EXPERTS // 2) as i:
                    for j in range(2):
                        upto = sp.value_load(table[0:1, BT_UPTO, bass.ds(i * 2 + (j - 2), 1)], min_val=0, max_val=N_BLOCKS)
                        sp.wait_ge(y_ready.sem, upto)
                        weights.load(sp, i * 2 + j, j)
                for j in range(2):
                    sp.wait_ge(loaded[j], W_DMAS * (N_EXPERTS // 2))
                all_zeroed = sp.value_load(table[0:1, BT_STORES, 2:3], min_val=0, max_val=16 * N_BLOCKS)
                sp.wait_ge(zeroed, all_zeroed)
                sp.sem_inc(sp_settled, 1)

            @block.gpsimd
            def _(pool):
                def gather(i, j):
                    b = i * 2 + j
                    pool.wait_ge(*turned.before_last(i, j))
                    pool.dma_start(ids[:, j, :], tile_rows(dr["slot_token"], b)).then_inc(ids_in[j], 16)
                    pool.wait_ge(*ids_in.now(i, j))
                    pool.sem_inc(passed, 1)
                    pool.indirect_dma_start(rows[:, j, :], None, dr["h2"], bass.IndirectOffsetOnAxis(ap=ids[:, j, :], axis=0)).then_inc(gathered[j], 16)

                gather(0, 0)
                block_loop(pool, lambda i, j: gather(*following(i, j)))

            @block.scalar
            def _(act):
                def body(i, j):
                    act.wait_ge(*gated.now(i, j))
                    act.wait_ge(*hid_ready.last(i, j))
                    act.activation(sg[:, :], pg[:, :], ACT.Silu).then_inc(silued[j], 1)
                    act.wait_ge(*downed.last(i, j))
                    for half in range(2):
                        act.wait_ge(*hid_turned.now(i, j, half + 1))
                        part = slice(half * KH, (half + 1) * KH)
                        act.activation(hidT[:, part, :], ph[:, part, :], ACT.Copy).then_inc(hidT_ready[j], 1)
                    act.wait_ge(*y_ready.now(i * 2 + j))
                    act.dma_start(tile_rows(dr["y"], i * 2 + j), y[:, j, :]).then_inc(stored[j], 16)

                block_loop(act, body)
                all_stored = [act.value_load(table[0:1, BT_STORES, j:j + 1], min_val=16, max_val=16 * N_BLOCKS) for j in range(2)]
                for j in range(2):
                    act.wait_ge(stored[j], all_stored[j])
                    act.sem_inc(act_settled, 1)

            @block.vector
            def _(dve):
                def copy_rows(i, j):
                    dve.wait_ge(*turned.now(i, j))
                    dve.wait_ge(*upped.before_last(i, j))
                    dve.tensor_copy(rowsT[:, j, :, :], pt[:, :, :]).then_inc(rowsT_ready[j], 1)

                def body(i, j):
                    dve.wait_ge(*silued.now(i, j))
                    dve.wait_ge(*hid_turned.last(i, j))
                    for half in range(2):
                        dve.wait_ge(*upped.now(i, j, half + 1))
                        part = slice(half * HALF, (half + 1) * HALF)
                        dve.tensor_tensor(hid[:, part], sg[:, part], pu[:, half, 0:HALF], ALU.mult).then_inc(hid_ready[j], 1)
                    copy_rows(*following(i, j))
                    dve.wait_ge(*downed.now(i, j))
                    dve.wait_ge(*stored.before_last(i, j))
                    dve.tensor_copy(y[:, j, :], py[:, :, :].rearrange("p a n -> p (a n)")).then_inc(y_ready.sem, 1)

                dve.memset(zeros[:, :], 0.0).then_inc(zeros_set, 1)
                copy_rows(0, 0)
                block_loop(dve, body)

            @block.tensor
            def _(pe):
                pe.wait_ge(consts_in, 16)

                def turn_rows(i, j):
                    pe.wait_ge(*gathered.now(i, j))
                    pe.wait_ge(*rowsT_ready.last(i, j))
                    for k in range(KD):
                        ins = pe.transpose(pt[:, k, :], rows[:, j, k * P:(k + 1) * P], ident[:, :])
                    ins.then_inc(turned[j], 1)

                def body(i, j):
                    b = i * 2 + j
                    entry = lambda r, top: pe.value_load(table[0:1, r, bass.ds(b, 1)], min_val=0, max_val=top)
                    even, odd = entry(BT_EVEN, 65535), entry(BT_ODD, 65535)
                    slot = entry(BT_SLOT, 1)
                    pe.wait_ge(loaded[0], even)
                    pe.wait_ge(loaded[1], odd)
                    part = lambda w, c0, c1: w[:, bass.ds(slot, 1), c0:c1].rearrange("p a n -> p (a n)")
                    pe.wait_ge(*rowsT_ready.now(i, j))
                    pe.wait_ge(*silued.last(i, j))
                    for k in range(KD):
                        ins = pe.matmul(pg[:, :], rowsT[:, j, k, :], part(wg, k * FF, (k + 1) * FF), start=k == 0, stop=k == KD - 1)
                    ins.then_inc(gated[j], 1)
                    for half in range(2):
                        pe.wait_ge(*hid_ready.last(i, j))
                        for k in range(KD):
                            c = k * FF + half * HALF
                            ins = pe.matmul(pu[:, half, 0:HALF], rowsT[:, j, k, :], part(wu, c, c + HALF), start=k == 0, stop=k == KD - 1)
                        ins.then_inc(upped[j], 1)

                    def turn_hidden(half):
                        pe.wait_ge(*hid_ready.now(i, j, half + 1))
                        pe.wait_ge(*(hidT_ready.now(i, j, 1) if half else hidT_ready.last(i, j)))
                        for k in range(half * KH, (half + 1) * KH):
                            ins = pe.transpose(ph[:, k, :], hid[:, k * P:(k + 1) * P], ident[:, :])
                        ins.then_inc(hid_turned[j], 1)

                    def down(k, n):
                        c = k * D_MODEL + n * 512
                        return pe.matmul(py[:, n, :], hidT[:, k, :], part(wd, c, c + 512), start=k == 0, stop=k == KF - 1)

                    turn_hidden(0)
                    turn_rows(*following(i, j))
                    pe.wait_ge(*hidT_ready.now(i, j, 1))
                    pe.wait_ge(*y_ready.last(b))
                    down(0, 0)
                    turn_hidden(1)
                    down(0, 1)
                    for k in range(1, KF):
                        if k == KH:
                            pe.wait_ge(*hidT_ready.now(i, j, 2))
                        for n in range(2):
                            ins = down(k, n)
                    ins.then_inc(downed[j], 1)

                turn_rows(0, 0)
                block_loop(pe, body)


def combine(nc, top, dr, dest, gate):
    N = TILES // 2
    with ExitStack() as ctx:
        sb = lambda n, s, d=F32: ctx.enter_context(nc.sbuf_tensor(n, s, d))
        sem = lambda n: top.semaphore(n)
        ev = lambda n, per=1: Event(top, f"h_{n}", per)
        eps, nw = sb("eps_h", [P, 1]), sb("final_norm_rows", [P, D_MODEL])
        x1 = sb("x1_h", [P, 2, 2, D_MODEL])
        idx = sb("slots_h", [P, 2, TOP_K, 2], I32)
        g = sb("gates_h", [P, 2, TOP_K, 2])
        ys = sb("y_rows", [P, 2, 2, TOP_K, D_MODEL])
        acc, sq = sb("sum_h", [P, 2, 2, D_MODEL]), sb("squares_h", [P, 2, D_MODEL])
        st = sb("stats_h", [P, 2, 3, 2])
        out = sb("out_tile", [P, 2, 2, D_MODEL])
        consts_in, eps_set, own_dve = sem("h_consts"), sem("h_eps"), sem("h_own_dve")
        passed = sem("h_passed")
        x_loaded, indexed, summed = ev("x_loaded", 16), ev("indexed"), ev("summed", 2)
        gathered = [ev(f"gathered{x}", 32) for x in range(2)]
        sum_sq, rms, ready, stored = ev("sum_sq"), ev("rms"), ev("ready"), ev("stored", 16)
        pair_rows = lambda dram, t: dram.rearrange("(t a p) w -> t p a w", p=P, a=2)[bass.ds(t, 1)].rearrange("o p a w -> (o p) a w")

        with nc.Block() as block:
            @block.sync
            def _(sp):
                sp.dma_start(nw[:, :], dr["final_norm_w"].unsqueeze(0).broadcast_to([P, D_MODEL])).then_inc(consts_in, 16)

                def load(i, j):
                    sp.wait_ge(*summed.before_last(i, j))
                    sp.dma_start(x1[:, j, :, :], pair_rows(dr["x1"], i * 2 + j)).then_inc(x_loaded[j], 16)

                def tile(i, j, last=False):
                    if not last:
                        load(*following(i, j))
                    sp.wait_ge(*ready.now(i, j))
                    sp.dma_start(pair_rows(dr["out"], i * 2 + j), out[:, j, :, :]).then_inc(stored[j], 16)

                load(0, 0)
                rounds(sp, None, tile, N)
                for j in range(2):
                    sp.wait_ge(stored[j], 16 * (N // 2))

            @block.gpsimd
            def _(pool):
                with pool.Fori(0, N // 2) as i:
                    for j in range(2):
                        pool.wait_ge(*indexed.now(i, j))
                        pool.wait_ge(*summed.before_last(i, j))
                        pool.sem_inc(passed, 1)
                        for x in range(2):
                            for k in range(TOP_K):
                                pool.indirect_dma_start(ys[:, j, x, k, :], None, dr["y"],
                                                        bass.IndirectOffsetOnAxis(ap=idx[:, j, k, x:x + 1], axis=0)).then_inc(gathered[x][j], 16)

            @block.scalar
            def _(act):
                act.wait_ge(eps_set, 1)
                with act.Fori(0, N // 2) as i:
                    for j in range(2):
                        act.wait_ge(*summed.now(i, j))
                        for x in range(2):
                            ins = act.activation(sq[:, x, :], acc[:, j, x, :], ACT.Square, accum_out=st[:, j, 0, x:x + 1])
                        ins.then_inc(sum_sq[j], 1)
                        act.wait_ge(*sum_sq.now(i, j))
                        act.activation(st[:, j, 1, :], st[:, j, 0, :], ACT.Sqrt, bias=eps[:, :], scale=1.0 / D_MODEL).then_inc(rms[j], 1)

            @block.vector
            def _(dve):
                own = Chain(dve, own_dve, 2 * 5)

                def index(i, j):
                    t = i * 2 + j
                    for x in range(2):
                        dve.wait_ge(*gathered[x].before_last(i, j))
                    own.mark(dve.tensor_copy(g[:, j, :, :], gate[:, :, bass.ds(t * 2, 2)]))
                    dve.tensor_copy(idx[:, j, :, :], dest[:, :, bass.ds(t * 2, 2)]).then_inc(indexed[j], 1)

                def combined(i, j):
                    dve.wait_ge(*x_loaded.now(i, j))
                    for x in range(2):
                        dve.wait_ge(*gathered[x].now(i, j))
                        a = acc[:, j, x, :]
                        own.link(dve.scalar_tensor_tensor(out=a, in0=ys[:, j, x, 0, :], scalar=g[:, j, 0, x:x + 1], in1=x1[:, j, x, :], op0=ALU.mult, op1=ALU.add))
                        dve.scalar_tensor_tensor(out=a, in0=ys[:, j, x, 1, :], scalar=g[:, j, 1, x:x + 1], in1=a, op0=ALU.mult, op1=ALU.add).then_inc(summed[j], 1)

                def normed(i, j):
                    dve.wait_ge(*rms.now(i, j))
                    own.link(dve.reciprocal(st[:, j, 2, :], st[:, j, 1, :]))
                    dve.wait_ge(*stored.before_last(i, j))
                    for x in range(2):
                        ins = dve.scalar_tensor_tensor(out=out[:, j, x, :], in0=acc[:, j, x, :], scalar=st[:, j, 2, x:x + 1], in1=nw[:, :], op0=ALU.mult, op1=ALU.mult)
                        if x == 0:
                            own.mark(ins)
                    ins.then_inc(ready[j], 1)

                def tile(i, j, last=False):
                    if not last:
                        index(*following(i, j))
                    own.wait()
                    combined(i, j)
                    normed(i, j)

                dve.memset(eps[:, :], EPS).then_inc(eps_set, 1)
                dve.wait_ge(consts_in, 16)
                index(0, 0)
                rounds(dve, own, tile, N)


def build(nc, dr, until=99):
    for name, shape in SCRATCH.items():
        dr[name] = nc.dram_tensor(f"scratch_{name}", shape, F32, kind="Internal").ap()
    dr["slot_token"] = nc.dram_tensor("scratch_slot_token", (SLOTS + P, 1), I32, kind="Internal").ap()
    with ExitStack() as top:
        sb = lambda n, s, d=F32: top.enter_context(nc.sbuf_tensor(n, s, d))
        gates = sb("gates", [P, TILES, 16])
        with Stage(nc) as stage:
            project_tokens(nc, stage, dr, gates)
        if until > 1:
            with Stage(nc) as stage:
                project_features(nc, stage, dr)
        if until > 2:
            with Stage(nc) as stage:
                gated_delta(nc, stage, dr, gates)
        w_scope = top.enter_context(ExitStack())
        w_out = w_scope.enter_context(nc.sbuf_tensor("w_out_sb", [P, KD, D_MODEL], F32))
        if until > 3:
            with Stage(nc) as stage:
                attention(nc, stage, dr, w_out)
        if until > 4:
            logits = sb("logits", [P, TILES, N_GROUPS + N_EXPERTS])
            dest = sb("dest", [P, TOP_K, TILES], I32)
            gate = sb("gate", [P, TOP_K, TILES])
            table = sb("block_table", [1, BT_ROWS, N_BLOCKS], I32)
            with Stage(nc) as lasting, ExitStack() as slots:
                weights = ExpertWeights(nc, slots, lasting, dr)
                with Stage(nc) as stage:
                    mix_out(nc, stage, dr, logits, w_out, weights.load_first)
                if until > 5:
                    with Stage(nc) as stage:
                        route(nc, stage, dr, logits, dest, gate, table)
                if until > 6:
                    with Stage(nc) as stage:
                        experts(nc, stage, dr, table, weights)
            if until > 7:
                with Stage(nc) as stage:
                    combine(nc, stage, dr, dest, gate)
def constants():
    f = np.float32
    p = np.arange(P)
    rows = SEQ // GRID_W
    row = np.repeat(np.arange(rows), GRID_W).astype(f)
    col = np.tile(np.arange(GRID_W), rows).astype(f)
    axis = ATT_D // 2
    inv = (f(10000.0) ** (-np.arange(0, axis, 2).astype(f) / f(axis))).astype(f)
    ang = np.concatenate([row[:, None] * inv, col[:, None] * inv], axis=-1).astype(f)
    out = {"c_ident": np.eye(P, dtype=f), "c_cos": np.cos(ang).astype(f), "c_sin": np.sin(ang).astype(f),
           "c_ones": np.ones((P, P), f)}
    upto = (p[:, None] <= p[None, :]).astype(f)
    out["c_upto"] = np.stack([upto, upto.T], 0).transpose(1, 0, 2).copy()
    out["c_before"] = (p[:, None] < p[None, :]).astype(f)
    level = []
    for n in range(7):
        b = 1 << n
        same = (p[:, None] // (2 * b)) == (p[None, :] // (2 * b))
        m = (same & (p[:, None] % (2 * b) < b) & (p[None, :] % (2 * b) >= b)).astype(f)
        level.append([m, m.T])
    out["c_level"] = np.array(level, f).transpose(2, 1, 0, 3).copy()
    n = np.zeros((2, CONV_BLOCKS), f)
    n[0, :GDN_HEADS], n[1, :GDN_HEADS] = GDN_D, GDN_D * EPS
    n[0, GDN_HEADS:2 * GDN_HEADS], n[1, GDN_HEADS:2 * GDN_HEADS] = 1, EPS
    n[1, 2 * GDN_HEADS:] = 1
    out["c_norm"] = np.broadcast_to(n.reshape(1, -1), (P, 2 * CONV_BLOCKS)).copy()
    out["c_iota"] = np.broadcast_to(np.arange(64, dtype=f), (P, 64)).copy()
    out["c_slot0"] = np.zeros((SLOTS + P, 1), np.int32)
    out["c_tokens"] = (np.arange(TILES)[None, :] * P + p[:, None]).astype(np.int32)
    return out


SHAPES = {"x": (SEQ, D_MODEL), "norm_mix_w": (D_MODEL,), "w_in": (D_MODEL, D_IN), "conv_w": (CONV_W, 3 * GDN_W),
          "a_log": (1, 8), "dt_bias": (1, 8), "gdn_norm_w": (GDN_D,), "q_norm_w": (ATT_D,),
          "k_norm_w": (ATT_D,), "w_out": (D_MODEL, D_MODEL), "norm_ffn_w": (D_MODEL,),
          "w_router_group": (D_MODEL, N_GROUPS), "w_router_expert": (D_MODEL, N_EXPERTS),
          "w_gate": (N_EXPERTS, D_MODEL, FF), "w_up": (N_EXPERTS, D_MODEL, FF), "w_down": (N_EXPERTS, FF, D_MODEL),
          "final_norm_w": (D_MODEL,)}
SCRATCH = {"xT": (P, KD, SEQ), "z": (SEQ, GDN_W), "qk": (SEQ, ATT_QK), "v": (SEQ, ATT_KV),
           "feat": (CONV_BLOCKS, P, SEQ), "tok": (SEQ, 3 * GDN_W), "o_gdn": (2, SEQ, GDN_W), "o_att": (SEQ, GDN_W), 
           "x1": (SEQ, D_MODEL), "h2": (SEQ, D_MODEL), "y": (SLOTS, D_MODEL)}


def kernel(**inputs):
    import numpy as _np
    import concourse.bacc as _bacc
    from concourse import mybir as _mybir
    from concourse.bass_utils import run_bass_kernel_spmd as _run

    nc = _bacc.Bacc("TRN2", target_bir_lowering=False, num_devices=1)
    arrays, dr = {}, {}
    for name, shape in SHAPES.items():
        a = _np.ascontiguousarray(inputs[name]).reshape(shape)
        arrays[f"in_{name}"] = a
        dr[name] = nc.dram_tensor(f"in_{name}", a.shape, _mybir.dt.from_np(a.dtype), kind="ExternalInput").ap()
    for name, a in constants().items():
        arrays[name] = a
        dr[name] = nc.dram_tensor(name, a.shape, _mybir.dt.from_np(a.dtype), kind="ExternalInput").ap()
    dr["out"] = nc.dram_tensor("out", (SEQ, D_MODEL), F32, kind="ExternalOutput").ap()
    build(nc, dr)
    r = _run(nc, [arrays], core_ids=[0])
    return r.results[0]["out"].reshape(1, SEQ, D_MODEL)
```
